# Optimizing a Trainium2 kernel written in Bass

```python
import math
import jax, jax.numpy as jnp
from jax import lax
import numpy as np

D_MODEL = 1024
BATCH = 1
SEQ = 1024
DEPTH = 1
DEC_BATCH = 8
DEC_SEQ = 4
PAST_LEN = 8192
PAGE_SIZE = 128

D_MIX = 2 * D_MODEL
D_SSM = D_MIX // 2
SSM_HEAD_DIM = 64
SSM_HEADS = D_SSM // SSM_HEAD_DIM
SSM_GROUPS = 2
HEADS_PER_GROUP = SSM_HEADS // SSM_GROUPS
SSM_STATE = 128
CONV_K = 4
C_CONV = D_SSM + 2 * SSM_GROUPS * SSM_STATE
SSD_CHUNK = 128
D_SG = D_MIX - D_SSM
SG_CHUNK = 128
SG_HEADS = 8
SG_HEAD_DIM = D_SG // SG_HEADS
IN_COLS = D_SSM + C_CONV + SSM_HEADS + 2 * D_SG
N_EXPERT_GROUPS = 4
EXPERTS_PER_GROUP = 8
N_EXPERTS = N_EXPERT_GROUPS * EXPERTS_PER_GROUP
TOP_K = 2
D_FF_EXPERT = D_MODEL // 2
MOE_BLOCK = 128
EPS = 1e-6

kernel_name = 'hymba_ssd_gmlp_hiermoe_step'

def rms_norm(x, w):
    xf = x.astype(jnp.float32)
    y = xf * lax.rsqrt(jnp.mean(xf * xf, axis=-1, keepdims=True) + EPS)
    return (y * w.astype(jnp.float32)).astype(x.dtype)

def gated_group_rms_norm(y, z, w):
    g = y.astype(jnp.float32) * jax.nn.silu(z.astype(jnp.float32))
    shp = g.shape
    g = g.reshape(shp[:-1] + (SSM_GROUPS, shp[-1] // SSM_GROUPS))
    g = g * lax.rsqrt(jnp.mean(g * g, axis=-1, keepdims=True) + EPS)
    return (g.reshape(shp) * w.astype(jnp.float32)).astype(z.dtype)

def ssd_scan(x, dt, a, b_in, c_in, s0, chunk):
    f32 = jnp.float32
    bsz, seq = x.shape[:2]
    nc = seq // chunk
    x = x.astype(f32).reshape((bsz, nc, chunk) + x.shape[2:])
    dt = dt.astype(f32).reshape((bsz, nc, chunk) + dt.shape[2:])
    b_in = b_in.astype(f32).reshape((bsz, nc, chunk) + b_in.shape[2:])
    c_in = c_in.astype(f32).reshape((bsz, nc, chunk) + c_in.shape[2:])
    acum = jnp.cumsum(dt * a, axis=2)
    xdt = x * dt[..., None]
    causal = jnp.tril(jnp.ones((chunk, chunk), bool))[:, :, None, None]
    seg = acum[:, :, :, None] - acum[:, :, None, :]
    decay = jnp.exp(jnp.where(causal, seg, -jnp.inf))
    cb = jnp.einsum('bclgn,bcsgn->bclsg', c_in, b_in)
    y_diag = jnp.einsum('bclsg,bclsgh,bcsghp->bclghp', cb, decay, xdt)
    decay_end = jnp.exp(acum[:, :, -1:] - acum)
    chunk_states = jnp.einsum('bclgn,bclgh,bclghp->bcghpn', b_in, decay_end, xdt)
    chunk_decay = jnp.exp(acum[:, :, -1])

    def step(s, inp):
        st, dec = inp
        return dec[..., None, None] * s + st, s

    s_fin, s_in = lax.scan(step, s0.astype(f32),
                           (jnp.moveaxis(chunk_states, 1, 0), jnp.moveaxis(chunk_decay, 1, 0)))
    s_in = jnp.moveaxis(s_in, 0, 1)
    y_off = jnp.einsum('bclgn,bcghpn,bclgh->bclghp', c_in, s_in, jnp.exp(acum))
    y = (y_diag + y_off).reshape((bsz, seq) + y_diag.shape[3:])
    return y, s_fin

def spatial_gating(u, v, sg_w, sg_b):
    bsz, seq, _ = v.shape
    n = min(seq, SG_CHUNK)
    nc = seq // n
    causal = jnp.tril(jnp.ones((n, n), bool))
    w_m = jnp.where(causal, sg_w[:, :n, :n], 0.0)
    vh = v.reshape(bsz, nc, n, SG_HEADS, SG_HEAD_DIM)
    sv = jnp.einsum('hts,bcshd->bcthd', w_m.astype(v.dtype), vh) + sg_b[:, :n].T[None, None, :, :, None].astype(v.dtype)
    return u * sv.reshape(bsz, seq, D_SG)

def mixer(hn, conv_prev, ssm_prev, w_in, conv_w, conv_b, dt_bias, a_log, d_skip,
          ssm_norm_w, sg_norm_w, sg_w, sg_b, w_out):
    bsz, seq, _ = hn.shape
    proj = hn @ w_in
    z, xbc, dt_raw, uv = jnp.split(proj, [D_SSM, D_SSM + C_CONV, D_SSM + C_CONV + SSM_HEADS], axis=-1)
    xbc_full = jnp.concatenate([conv_prev.astype(xbc.dtype), xbc], axis=1)
    conv_out = lax.conv_general_dilated(
        xbc_full, conv_w[:, None, :].astype(xbc.dtype), (1,), 'VALID',
        dimension_numbers=('NWC', 'WIO', 'NWC'), feature_group_count=C_CONV) + conv_b.astype(xbc.dtype)
    xbc_act = jax.nn.silu(conv_out)
    xs, b_in, c_in = jnp.split(xbc_act, [D_SSM, D_SSM + SSM_GROUPS * SSM_STATE], axis=-1)
    dt = jax.nn.softplus(dt_raw.astype(jnp.float32) + dt_bias.astype(jnp.float32))
    a = -jnp.exp(a_log.astype(jnp.float32))
    xs_h = xs.reshape(bsz, seq, SSM_GROUPS, HEADS_PER_GROUP, SSM_HEAD_DIM)
    y, s_fin = ssd_scan(xs_h, dt.reshape(bsz, seq, SSM_GROUPS, HEADS_PER_GROUP),
                        a.reshape(SSM_GROUPS, HEADS_PER_GROUP),
                        b_in.reshape(bsz, seq, SSM_GROUPS, SSM_STATE),
                        c_in.reshape(bsz, seq, SSM_GROUPS, SSM_STATE),
                        ssm_prev, min(SSD_CHUNK, seq))
    y = y + d_skip.astype(jnp.float32).reshape(SSM_GROUPS, HEADS_PER_GROUP)[..., None] * xs_h.astype(jnp.float32)
    y_ssm = gated_group_rms_norm(y.reshape(bsz, seq, D_SSM), z, ssm_norm_w)
    u, v = jnp.split(jax.nn.gelu(uv, approximate=False), 2, axis=-1)
    v = rms_norm(v, sg_norm_w)
    y_sg = spatial_gating(u, v, sg_w, sg_b)
    mix = jnp.concatenate([y_ssm, y_sg.astype(y_ssm.dtype)], axis=-1) @ w_out
    return mix, xbc_full[:, -(CONV_K - 1):], s_fin.astype(ssm_prev.dtype), v

def hier_moe(h, w_router_group, b_router_group, w_router_expert, b_router_expert, w_gate, w_up, w_down):
    shp = h.shape
    x = h.reshape(-1, D_MODEL)
    n_tok = x.shape[0]
    p_grp = jax.nn.softmax((x @ w_router_group).astype(jnp.float32) + b_router_group.astype(jnp.float32), axis=-1)
    g_idx = jnp.argmax(p_grp, axis=-1)
    g_p = jnp.max(p_grp, axis=-1)
    le = ((x @ w_router_expert).astype(jnp.float32) + b_router_expert.astype(jnp.float32))
    le = le.reshape(n_tok, N_EXPERT_GROUPS, EXPERTS_PER_GROUP)
    le = jnp.take_along_axis(le, g_idx[:, None, None], axis=1)[:, 0]
    top_v, top_i = lax.top_k(jax.nn.softmax(le, axis=-1), TOP_K)
    gate = g_p[:, None] * top_v / jnp.sum(top_v, axis=-1, keepdims=True)
    expert_idx = g_idx[:, None] * EXPERTS_PER_GROUP + top_i
    n_asg = n_tok * TOP_K
    e_flat = expert_idx.reshape(-1).astype(jnp.int32)
    t_flat = jnp.repeat(jnp.arange(n_tok, dtype=jnp.int32), TOP_K)
    w_flat = gate.reshape(-1)
    order = jnp.argsort(e_flat)
    e_s, t_s, w_s = e_flat[order], t_flat[order], w_flat[order]
    counts = jnp.bincount(e_flat, length=N_EXPERTS)
    padded = (counts + MOE_BLOCK - 1) // MOE_BLOCK * MOE_BLOCK
    start = jnp.cumsum(counts) - counts
    pend = jnp.cumsum(padded)
    pstart = pend - padded
    dest = pstart[e_s] + (jnp.arange(n_asg, dtype=jnp.int32) - start[e_s])
    n_blocks = -(-n_asg // MOE_BLOCK) + N_EXPERTS
    n_rows = n_blocks * MOE_BLOCK
    buf_tok = jnp.full((n_rows,), n_tok, jnp.int32).at[dest].set(t_s)
    buf_w = jnp.zeros((n_rows,), x.dtype).at[dest].set(w_s.astype(x.dtype))
    blk_expert = jnp.minimum(jnp.searchsorted(pend, jnp.arange(n_blocks) * MOE_BLOCK, side='right'),
                             N_EXPERTS - 1)
    x_pad = jnp.concatenate([x, jnp.zeros((1, D_MODEL), x.dtype)], axis=0)

    def expert_block(args):
        e, tok = args
        xb = x_pad[tok]
        hmid = jax.nn.silu(xb @ w_gate[e]) * (xb @ w_up[e])
        return hmid @ w_down[e]

    out = lax.map(expert_block, (blk_expert, buf_tok.reshape(n_blocks, MOE_BLOCK)))
    out = out.reshape(n_rows, D_MODEL) * buf_w[:, None]
    y = jax.ops.segment_sum(out, buf_tok, num_segments=n_tok + 1)[:n_tok]
    return y.reshape(shp).astype(h.dtype)

def decoder_layer(x, conv_prev, ssm_prev, norm_mix_w, w_in, conv_w, conv_b, dt_bias, a_log, d_skip,
                  ssm_norm_w, sg_norm_w, sg_w, sg_b, w_out, norm_ffn_w, w_router_group, b_router_group,
                  w_router_expert, b_router_expert, w_gate, w_up, w_down):
    mix, conv_new, ssm_new, v_rows = mixer(rms_norm(x, norm_mix_w), conv_prev, ssm_prev, w_in, conv_w, conv_b,
                                           dt_bias, a_log, d_skip, ssm_norm_w, sg_norm_w, sg_w, sg_b, w_out)
    h = x + mix
    h = h + hier_moe(rms_norm(h, norm_ffn_w), w_router_group, b_router_group, w_router_expert,
                     b_router_expert, w_gate, w_up, w_down)
    return h, conv_new, ssm_new, v_rows

def setup_inputs(seed: int = 0) -> dict:
    key = jax.random.key(seed)
    ks = jax.random.split(key, 24)
    f32 = jnp.float32

    def nrm(k, shape, scale):
        return jax.random.normal(k, shape, f32) * scale

    u_dt = jax.random.uniform(ks[6], (DEPTH, SSM_HEADS), f32)
    dt0 = jnp.exp(u_dt * (math.log(0.1) - math.log(0.001)) + math.log(0.001))
    return {
        'x_prompt': nrm(ks[0], (BATCH, SEQ, D_MODEL), 1.0),
        'x_sample': nrm(ks[1], (DEC_BATCH, DEC_SEQ, D_MODEL), 1.0),
        'state_conv': nrm(ks[2], (DEPTH, DEC_BATCH, CONV_K - 1, C_CONV), 1.0),
        'state_ssm': nrm(ks[3], (DEPTH, DEC_BATCH, SSM_GROUPS, HEADS_PER_GROUP, SSM_HEAD_DIM, SSM_STATE), 0.3),
        'norm_mix_w': 1.0 + nrm(ks[4], (DEPTH, D_MODEL), 0.02),
        'w_in': nrm(ks[5], (DEPTH, D_MODEL, IN_COLS), D_MODEL ** -0.5),
        'conv_w': nrm(ks[7], (DEPTH, CONV_K, C_CONV), CONV_K ** -0.5),
        'conv_b': nrm(ks[8], (DEPTH, C_CONV), 0.02),
        'dt_bias': dt0 + jnp.log(-jnp.expm1(-dt0)),
        'a_log': jnp.log(jax.random.uniform(ks[9], (DEPTH, SSM_HEADS), f32, 1.0, 16.0)),
        'd_skip': 1.0 + nrm(ks[10], (DEPTH, SSM_HEADS), 0.1),
        'ssm_norm_w': 1.0 + nrm(ks[11], (DEPTH, D_SSM), 0.02),
        'sg_norm_w': 1.0 + nrm(ks[12], (DEPTH, D_SG), 0.02),
        'sg_w': nrm(ks[13], (DEPTH, SG_HEADS, SG_CHUNK, SG_CHUNK), SG_CHUNK ** -0.5),
        'sg_b': 1.0 + nrm(ks[14], (DEPTH, SG_HEADS, SG_CHUNK), 0.1),
        'w_out': nrm(ks[15], (DEPTH, D_MIX, D_MODEL), D_MIX ** -0.5),
        'norm_ffn_w': 1.0 + nrm(ks[16], (DEPTH, D_MODEL), 0.02),
        'w_router_group': nrm(ks[17], (DEPTH, D_MODEL, N_EXPERT_GROUPS), D_MODEL ** -0.5),
        'b_router_group': nrm(ks[18], (DEPTH, N_EXPERT_GROUPS), 0.01),
        'w_router_expert': nrm(ks[19], (DEPTH, D_MODEL, N_EXPERTS), D_MODEL ** -0.5),
        'b_router_expert': nrm(ks[20], (DEPTH, N_EXPERTS), 0.01),
        'w_gate': nrm(ks[21], (DEPTH, N_EXPERTS, D_MODEL, D_FF_EXPERT), D_MODEL ** -0.5),
        'w_up': nrm(ks[22], (DEPTH, N_EXPERTS, D_MODEL, D_FF_EXPERT), D_MODEL ** -0.5),
        'w_down': nrm(ks[23], (DEPTH, N_EXPERTS, D_FF_EXPERT, D_MODEL), D_FF_EXPERT ** -0.5),
        'norm_final_w': 1.0 + nrm(jax.random.fold_in(key, 99), (D_MODEL,), 0.02),
    }

def reference(x_prompt, x_sample, state_conv, state_ssm, norm_mix_w, w_in, conv_w, conv_b, dt_bias, a_log,
              d_skip, ssm_norm_w, sg_norm_w, sg_w, sg_b, w_out, norm_ffn_w, w_router_group, b_router_group,
              w_router_expert, b_router_expert, w_gate, w_up, w_down, norm_final_w):
    yp, ys = x_prompt, x_sample
    bp = x_prompt.shape[0]
    conv_p, ssm_p, conv_s, ssm_s, v_s = [], [], [], [], []
    for l in range(DEPTH):
        lp = (norm_mix_w[l], w_in[l], conv_w[l], conv_b[l], dt_bias[l], a_log[l], d_skip[l], ssm_norm_w[l],
              sg_norm_w[l], sg_w[l], sg_b[l], w_out[l], norm_ffn_w[l], w_router_group[l], b_router_group[l],
              w_router_expert[l], b_router_expert[l], w_gate[l], w_up[l], w_down[l])
        conv0 = jnp.zeros((bp, CONV_K - 1, C_CONV), x_prompt.dtype)
        ssm0 = jnp.zeros((bp,) + state_ssm.shape[2:], state_ssm.dtype)
        yp, cp, sp, _ = decoder_layer(yp, conv0, ssm0, *lp)
        ys, cs, ss, vs = decoder_layer(ys, state_conv[l], state_ssm[l], *lp)
        conv_p.append(cp)
        ssm_p.append(sp)
        conv_s.append(cs)
        ssm_s.append(ss)
        v_s.append(vs)
    y_prompt = rms_norm(yp, norm_final_w)
    y_sample = rms_norm(ys, norm_final_w)
    return (y_prompt, y_sample, jnp.stack(conv_p), jnp.stack(ssm_p), jnp.stack(conv_s), jnp.stack(ssm_s), jnp.stack(v_s))


_drawn_inputs = setup_inputs


def setup_inputs(seed=0):
    import zlib

    import numpy as np

    out = dict(_drawn_inputs(seed))
    spreads = {}
    factors = {'ssm_norm_w': 7.823,
     'sg_norm_w': 8.254,
     'b_router_group': 12.846,
     'b_router_expert': 15.257,
     'norm_final_w': 8.153,
     'norm_ffn_w': 2.856}
    for name, (base, spread) in spreads.items():
        noise = np.random.default_rng([zlib.crc32(name.encode()), seed]).standard_normal(out[name].shape)
        drawn = base * np.exp(spread * noise) if base else spread * noise
        out[name] = __import__('jax').numpy.asarray(drawn.astype(out[name].dtype))
    for name, factor in factors.items():
        out[name] = (out[name] * factor).astype(out[name].dtype)
    return out
```

```python
from contextlib import ExitStack

import concourse.bass as bass
from concourse import mybir

ALU = mybir.AluOpType
ACT = mybir.ActivationFunctionType
AX = mybir.AxisListType
F32 = mybir.dt.float32
I32 = mybir.dt.int32
U32 = mybir.dt.uint32

P = 128
D = 1024
KT = D // P
SEQ = 1024
DEC_B, DEC_S = 8, 4
TS = DEC_B * DEC_S
T = SEQ + TS
NT = SEQ // P
HEADS, HD, NSTATE, GROUPS = 16, 64, 128, 2
CONV_K = 4
C_CONV = D + 2 * GROUPS * NSTATE
SGH = 8
E, EG, EPG = 32, 4, 8
FF = D // 2
EPS = 1e-6
MAXBLK = -(-2 * T // P) + E
MINBLK = -(-2 * T // P)

COL_Z, COL_X, COL_DT, COL_U = 0, D, D + C_CONV, D + C_CONV + HEADS
M_X, M_B, M_C, M_U, M_V, M_END = 8, 16, 18, 20, 28, 36
NB3 = 3
TB = T // NB3
CT_N = M_U - M_X


def wait(eng, sem, value):
    if not (isinstance(value, int) and value <= 0):
        eng.wait_ge(sem, value)


def then_own(eng, ins, sem, value):
    ins.then_inc(sem, 1)
    eng.wait_ge(sem, value)


def rows_of(t):
    return TS if isinstance(t, int) and t == NT else P


def make_constants(nc, pool, C):
    made = [0]

    def done(ins):
        made[0] += 1
        ins.then_inc(C["const_made"], 1)

    def after(ins):
        done(ins)
        pool.wait_ge(C["const_made"], made[0])

    def select(t, pattern, base, mult, op=ALU.is_ge, fill=0.0):
        after(nc.gpsimd.affine_select(out=t, in_=t, compare_op=op, fill=fill, base=base, pattern=pattern,
                                      channel_multiplier=mult))

    after(nc.gpsimd.memset(C["ident"][:], 0.0))
    select(C["ident"][:], [[-1, P]], 0, 1, ALU.not_equal, 1.0)
    done(nc.gpsimd.memset(C["eps"][:], EPS))
    done(nc.gpsimd.memset(C["ones"][:], 1.0))
    for name, step, mult, op in (("le", 1, -1, ALU.is_ge), ("lt", 1, -1, ALU.is_gt), ("gt", -1, 1, ALU.is_gt)):
        after(nc.gpsimd.memset(C[name][:], 1.0))
        select(C[name][:], [[step, P]], 0, mult, op)
    after(nc.gpsimd.memset(C["same"][:], 1.0))
    v = C["same"][:].rearrange("p (b s) -> p b s", s=DEC_S)
    select(v, [[-DEC_S, DEC_B], [0, DEC_S]], 0, 1)
    select(v, [[DEC_S, DEC_B], [0, DEC_S]], DEC_S - 1, -1)
    after(nc.gpsimd.memset(C["of_seq"][:], 1.0))
    select(C["of_seq"][:], [[-DEC_S, DEC_B], [1, TS]], 0, 0)
    select(C["of_seq"][:], [[DEC_S, DEC_B], [-1, TS]], DEC_S - 1, 0)
    after(nc.gpsimd.memset(C["repeat"][:], 0.0))
    select(C["repeat"][:].rearrange("p (b s) -> p b s", s=DEC_S), [[0, DEC_B], [-1, DEC_S]], 0, 1, ALU.not_equal, 1.0)
    done(nc.gpsimd.iota(C["expert_no"][:], [[1, E]], base=0, channel_multiplier=0, allow_small_or_imprecise_dtypes=True))
    done(nc.gpsimd.iota(C["row_step"][:], [[P, NT + 1]], base=0, channel_multiplier=0, allow_small_or_imprecise_dtypes=True))
    done(nc.gpsimd.iota(C["block_no"][:], [[1, MAXBLK]], base=0, channel_multiplier=0, allow_small_or_imprecise_dtypes=True))
    done(nc.gpsimd.iota(C["token_slot"][:, :, :, 0], [[P, NT + 1], [0, 2]], base=0, channel_multiplier=1))
    done(nc.gpsimd.iota(C["token_slot"][:, :, :, 1], [[2 * P, NT + 1], [1, 2]], base=0, channel_multiplier=2))
    assert made[0] == N_CONST


N_CONST = 23


def projections(nc, A, S, C, bank):
    with ExitStack() as ctx:
        def sb(name, shape, dt=F32):
            return ctx.enter_context(nc.sbuf_tensor(name, shape, dt))

        def sem(name):
            return ctx.enter_context(nc.semaphore(name))

        xin = [sb(f"xin{j}", [P, D]) for j in range(2)]
        xsq = sb("xsq", [P, D])
        stat = [sb(f"stat{j}", [P, 4]) for j in range(2)]
        xT = sb("xT", [P, KT, T])
        w = [sb(f"w{j}", [P, KT, P]) for j in range(2)]
        feat = [sb(f"feat{j}", [P, T]) for j in range(2)]
        raw = [sb(f"raw{j}", [P, 3 + SEQ + 1 + DEC_B * 7]) for j in range(2)]
        conv = [sb(f"conv{j}", [P, T]) for j in range(2)]
        stage = [sb(f"stage{j}", [P, NT + 1, P]) for j in range(2)]
        old_conv = sb("old_conv", [P, CT_N, DEC_B, CONV_K - 1])
        tail = sb("tail", [P, CT_N, DEC_B + 1, CONV_K - 1])
        w_dt = sb("w_dt", [P, KT, HEADS])
        nmw = sb("nmw", [P, KT])
        cw = sb("cw", [P, CONV_K, CT_N])
        cb = sb("cb", [P, CT_N])
        hcol = sb("hcol", [HEADS, 4])
        dtw = sb("dtw", [HEADS, 6, T])

        prompt_raw = [raw[j][:, 0:3 + SEQ] for j in range(2)]
        sample_raw = [raw[j][:, 4 + SEQ:4 + SEQ + DEC_B * 7].rearrange("p (b s) -> p b s", s=7) for j in range(2)]

        setup_loaded = sem("setup_loaded")
        x_loaded = [sem(f"x_loaded{j}") for j in range(2)]
        x_squared, x_rms, x_rinv, x_normed = sem("x_squared"), sem("x_rms"), sem("x_rinv"), sem("x_normed")
        xT_psum, xT_done = sem("xT_psum"), sem("xT_done")
        w_loaded = [sem(f"w_loaded{j}") for j in range(2)]
        acc_ready, acc_free = sem("acc_ready"), sem("acc_free")
        feat_ready = sem("feat_ready")
        feat_stored = [sem(f"feat_stored{j}") for j in range(2)]
        tr_psum, tr_free, stage_ready = sem("tr_psum"), sem("tr_free"), sem("stage_ready")
        stage_stored = [sem(f"stage_stored{j}") for j in range(2)]
        old_placed = sem("old_placed")
        raw_ready, conv_chain, conv_done, conv_used = sem("raw_ready"), sem("conv_chain"), sem("conv_done"), sem("conv_used")
        tail_ready, tail_stored = sem("tail_ready"), sem("tail_stored")
        dt_act, dt_chain, dt_ready, dt_psum, dt_done = sem("dt_act"), sem("dt_chain"), sem("dt_ready"), sem("dt_psum"), sem("dt_done")
        pad_zero = sem("pad_zero")

        xp = A["x_prompt"][0]
        xs = A["x_sample"].rearrange("b s d -> (b s) d")
        N_SETUP = 7

        block = ctx.enter_context(nc.Block())

        @block.sync
        def _(sp):
            def load_w(m, j):
                sp.dma_start(w[j][:], A["w_in_tiles"][bass.ds(m, 1)].rearrange("m p k c -> (m p) k c")).then_inc(w_loaded[j], 16)

            def load_x(t, j):
                r = rows_of(t)
                src = xs if r == TS else xp[bass.ds(t * P, P), :]
                sp.dma_start(xin[j][0:r, :], src).then_inc(x_loaded[j], 16)

            load_x(0, 0)
            load_x(1, 1)
            sp.dma_start(nmw[:], A["norm_mix_w"]).then_inc(setup_loaded, 16)
            load_w(0, 0)
            load_w(1, 1)
            for dst, name in ((cw, "conv_w"), (cb, "conv_b"), (old_conv, "state_conv"), (w_dt, "w_dt")):
                sp.dma_start(dst[:], A[name]).then_inc(setup_loaded, 16)
            sp.dma_start(hcol[:, 0:1], A["dt_bias"]).then_inc(setup_loaded, 16)
            sp.dma_start(hcol[:, 1:2], A["a_log"]).then_inc(setup_loaded, 16)

            for t in (2, 3):
                sp.wait_ge(xT_psum, 2 * (t - 1))
                load_x(t, t % 2)
            with sp.Fori(2, NT // 2) as a:
                for j in range(2):
                    t = a * 2 + j
                    sp.wait_ge(xT_psum, a * 4 + (2 * j - 2))
                    load_x(t, j)
            sp.wait_ge(xT_psum, 2 * (NT - 1))
            load_x(NT, 0)

            with sp.Fori(1, M_U // 2) as a:
                for j in range(2):
                    sp.wait_ge(acc_ready, a * 6 + (3 * j - 3))
                    load_w(a * 2 + j, j)
            for m in (M_U, M_U + 1):
                sp.wait_ge(acc_ready, 3 * (m - 1))
                load_w(m, m % 2)
            with sp.Fori(M_U // 2 + 1, M_END // 2) as a:
                for j in range(2):
                    sp.wait_ge(acc_ready, a * 6 + 3 * j)
                    load_w(a * 2 + j, j)

        @block.tensor
        def _(pe):
            def turn_x(t, j):
                r = rows_of(t)
                pe.wait_ge(x_normed, t + 1)
                for h in range(2):
                    wait(pe, xT_done, t * 2 + (h - 1))
                    for q in range(4):
                        k = 4 * h + q
                        last = nc.tensor.transpose(bank[6 + h][:, q * P:q * P + r], xin[j][0:r, k * P:(k + 1) * P],
                                                   C["ident"][0:r, 0:r])
                    last.then_inc(xT_psum, 1)

            def products(n, j, w_at):
                wait(pe, w_loaded[j], w_at)
                for b in range(NB3):
                    wait(pe, acc_free, n * 3 + (b - 2))
                    for k in range(KT):
                        last = nc.tensor.matmul(bank[b][:, 0:TB], w[j][:, k, :], xT[:, k, b * TB:(b + 1) * TB],
                                                start=(k == 0), stop=(k == KT - 1))
                    last.then_inc(acc_ready, 1)

            def turn(q, m, j):
                pe.wait_ge(feat_ready, m + 1)
                for g in range(3):
                    wait(pe, tr_free, q * 3 + (g - 2))
                    for s in range(4 if g < 2 else 1):
                        t = 4 * g + s
                        r = P if t < NT else TS
                        last = nc.tensor.transpose(bank[3 + g][0:r, s * P:(s + 1) * P], feat[j][:, t * P:t * P + r],
                                                   C["ident"][:])
                    last.then_inc(tr_psum, 1)

            pe.wait_ge(C["const_made"], N_CONST)
            turn_x(0, 0)
            turn_x(1, 1)
            with pe.Fori(1, NT // 2) as a:
                turn_x(a * 2, 0)
                turn_x(a * 2 + 1, 1)
            turn_x(NT, 0)
            pe.wait_ge(xT_done, 2 * (NT + 1))
            products(0, 0, 16)
            products(1, 1, 16)
            turn(0, 0, 0)
            products(2, 0, 32)
            turn(1, 1, 1)
            with pe.Fori(1, M_C // 2) as a:
                products(a * 2 + 1, 1, a * 16 + 16)
                turn(a * 2, a * 2, 0)
                products(a * 2 + 2, 0, a * 16 + 32)
                turn(a * 2 + 1, a * 2 + 1, 1)
            products(M_C + 1, 1, 16 * (M_U // 2))
            pe.wait_ge(setup_loaded, 16 * N_SETUP)
            for b in range(NB3):
                pe.wait_ge(acc_free, 3 * M_U + b - 2)
                for k in range(KT):
                    last = nc.tensor.matmul(bank[b][0:HEADS, 0:TB], w_dt[:, k, :], xT[:, k, b * TB:(b + 1) * TB],
                                            start=(k == 0), stop=(k == KT - 1))
                last.then_inc(acc_ready, 1)
            with pe.Fori(M_U // 2, M_V // 2) as a:
                products(a * 2 + 1, 0, a * 16 + 16)
                products(a * 2 + 2, 1, a * 16 + 16)
            products(M_V + 1, 0, 16 * (M_V // 2 + 1))
            pe.wait_ge(dt_ready, 1)
            for t in range(NT + 1):
                r = P if t < NT else TS
                nc.tensor.transpose(bank[6][0:r, 32 * t:32 * t + 16], dtw[:, 4, t * P:t * P + r], C["ident"][0:16, 0:16])
                last = nc.tensor.transpose(bank[6][0:r, 32 * t + 16:32 * t + 32], dtw[:, 5, t * P:t * P + r],
                                           C["ident"][0:16, 0:16])
            last.then_inc(dt_psum, 1)
            with pe.Fori(M_V // 2, M_END // 2 - 1) as a:
                products(a * 2 + 2, 1, a * 16 + 16)
                turn(a * 2 - (M_V - M_C), a * 2, 0)
                products(a * 2 + 3, 0, a * 16 + 32)
                turn(a * 2 + (1 - M_V + M_C), a * 2 + 1, 1)
            products(M_END, 1, 16 * (M_END // 2))
            turn(M_END - 2 - (M_V - M_C), M_END - 2, 0)
            turn(M_END - 1 - (M_V - M_C), M_END - 1, 1)

        @block.scalar
        def _(act):
            def norm_stats(t, j, at):
                r = rows_of(t)
                act.wait_ge(x_loaded[j], at)
                wait(act, x_normed, t - 1)
                then_own(act, nc.scalar.activation(xsq[0:r, :], xin[j][0:r, :], ACT.Square, accum_out=stat[j][0:r, 0:1]),
                         x_squared, t + 1)
                nc.scalar.activation(stat[j][0:r, 1:2], stat[j][0:r, 0:1], ACT.Sqrt, bias=C["eps"][0:r, :],
                                     scale=1.0 / D).then_inc(x_rms, 1)

            act.wait_ge(C["const_made"], N_CONST)
            norm_stats(0, 0, 16)
            norm_stats(1, 1, 16)
            with act.Fori(1, NT // 2) as a:
                norm_stats(a * 2, 0, a * 16 + 16)
                norm_stats(a * 2 + 1, 1, a * 16 + 16)
            norm_stats(NT, 0, 16 * (NT // 2 + 1))

            def activate(n, m, j, func):
                for b in range(NB3):
                    act.wait_ge(acc_ready, n * 3 + (b + 1))
                    ins = nc.scalar.activation(feat[j][:, b * TB:(b + 1) * TB], bank[b][:, 0:TB], func)
                    ins.then_inc(acc_free, 1)
                act.wait_ge(acc_free, n * 3 + 3)
                nc.scalar.sem_inc(feat_ready, 1)

            def to_conv(m, j):
                for b in range(NB3):
                    act.wait_ge(acc_ready, m * 3 + (b + 1))
                    if b < 2:
                        nc.scalar.copy(raw[j][:, 3 + b * TB:3 + (b + 1) * TB], bank[b][:, 0:TB]).then_inc(acc_free, 1)
                    else:
                        nc.scalar.copy(raw[j][:, 3 + 2 * TB:3 + SEQ], bank[b][:, 0:SEQ - 2 * TB]).then_inc(raw_ready, 1)
                        nc.scalar.copy(sample_raw[j][:, :, 3:7],
                                       bank[b][:, SEQ - 2 * TB:TB].rearrange("p (b s) -> p b s", s=DEC_S)).then_inc(acc_free, 1)
                act.wait_ge(conv_done, m - (M_X - 1))

            def silu_conv(m, j):
                nc.scalar.activation(feat[j][:], conv[j][:], ACT.Silu, bias=cb[:, bass.ds(m - M_X, 1)]).then_inc(feat_ready, 1)

            for m in (0, 1):
                activate(m, m, m, ACT.Silu)
            with act.Fori(1, M_X // 2) as a:
                for j in range(2):
                    act.wait_ge(tr_psum, a * 6 + (3 * j - 3))
                    activate(a * 2 + j, a * 2 + j, j, ACT.Silu)
            act.wait_ge(setup_loaded, 16 * N_SETUP)
            for c in (0, 1):
                m = M_X + c
                to_conv(m, c)
                act.wait_ge(tr_psum, 3 * (m - 1))
                silu_conv(m, c)
            with act.Fori(M_X // 2 + 1, M_C // 2) as a:
                for j in range(2):
                    act.wait_ge(conv_done, a * 2 + (j - M_X - 1))
                    act.wait_ge(tail_ready, a * 4 + 2 * (j - M_X - 1))
                    to_conv(a * 2 + j, j)
                    act.wait_ge(tr_psum, a * 6 + (3 * j - 3))
                    silu_conv(a * 2 + j, j)
            for m in (M_C, M_C + 1):
                act.wait_ge(conv_done, m - M_X - 1)
                act.wait_ge(tail_ready, 2 * (m - M_X - 1))
                to_conv(m, m % 2)
                act.wait_ge(tr_psum, 3 * (m - 1))
                act.wait_ge(feat_stored[m % 2], 16)
                silu_conv(m, m % 2)
            for b in range(NB3):
                act.wait_ge(acc_ready, 3 * M_U + b + 1)
                s = slice(b * TB, (b + 1) * TB)
                nc.scalar.activation(dtw[:, 0, s], bank[b][0:HEADS, 0:TB], ACT.Abs, bias=hcol[:, 0:1]).then_inc(dt_act, 1)
                nc.scalar.activation(dtw[:, 1, s], bank[b][0:HEADS, 0:TB], ACT.Relu, bias=hcol[:, 0:1]).then_inc(acc_free, 1)
            act.wait_ge(dt_act, NB3)
            then_own(act, nc.scalar.activation(dtw[:, 2, :], dtw[:, 0, :], ACT.Exp, scale=-1.0), dt_act, NB3 + 1)
            nc.scalar.activation(dtw[:, 3, :], dtw[:, 2, :], ACT.Ln, bias=1.0).then_inc(dt_act, 1)
            nc.scalar.activation(hcol[:, 2:3], hcol[:, 1:2], ACT.Exp).then_inc(dt_act, 1)
            with act.Fori(M_U // 2, M_V // 2) as a:
                for j in range(2):
                    act.wait_ge(feat_stored[j], a * 16 - 16 * (M_U // 2 - 2))
                    activate(a * 2 + (j + 1), a * 2 + j, j, ACT.Gelu)
            for m in (M_V, M_V + 1):
                act.wait_ge(feat_stored[m % 2], 16 * ((M_V - M_B) // 2))
                activate(m + 1, m, m % 2, ACT.Gelu)
            with act.Fori(M_V // 2 + 1, M_END // 2) as a:
                for j in range(2):
                    act.wait_ge(tr_psum, a * 6 + (3 * (j - 1) - 3 * (M_V - M_C)))
                    activate(a * 2 + (j + 1), a * 2 + j, j, ACT.Gelu)

        @block.vector
        def _(dve):
            for j in range(2):
                nc.vector.memset(raw[j][:, 0:3], 0.0).then_inc(pad_zero, 1)

            def normalise(t, j):
                r = rows_of(t)
                dve.wait_ge(x_rms, t + 1)
                then_own(dve, nc.vector.reciprocal(stat[j][0:r, 2:3], stat[j][0:r, 1:2]), x_rinv, t + 1)
                nc.vector.tensor_scalar(xin[j][0:r, :], xin[j][0:r, :], stat[j][0:r, 2:3], None, ALU.mult).then_inc(x_normed, 1)

            def scale_xT(t):
                r = rows_of(t)
                for h in range(2):
                    dve.wait_ge(xT_psum, t * 2 + (h + 1))
                    nc.vector.tensor_tensor(
                        xT[:, 4 * h:4 * h + 4, bass.ds(t * P, r)],
                        bank[6 + h][:].rearrange("p (k t) -> p k t", k=4)[:, :, 0:r],
                        nmw[:, 4 * h:4 * h + 4].unsqueeze(2).to_broadcast([P, 4, r]), ALU.mult).then_inc(xT_done, 1)

            dve.wait_ge(setup_loaded, 16 * N_SETUP)
            normalise(0, 0)
            with dve.Fori(0, NT // 2 - 1) as a:
                normalise(a * 2 + 1, 1)
                scale_xT(a * 2)
                normalise(a * 2 + 2, 0)
                scale_xT(a * 2 + 1)
            normalise(NT - 1, 1)
            scale_xT(NT - 2)
            normalise(NT, 0)
            scale_xT(NT - 1)
            scale_xT(NT)

            def unload(q, j):
                for g in range(3):
                    dve.wait_ge(tr_psum, q * 3 + (g + 1))
                    if g < 2:
                        ins = nc.vector.tensor_copy(stage[j][:, 4 * g:4 * g + 4, :],
                                                    bank[3 + g][:].rearrange("p (t c) -> p t c", t=4))
                    else:
                        ins = nc.vector.tensor_copy(stage[j][0:TS, NT, :], bank[5][0:TS, 0:P])
                    ins.then_inc(tr_free, 1)
                dve.wait_ge(tr_free, q * 3 + 3)
                nc.vector.sem_inc(stage_ready, 1)

            def convolve(c, j):
                then_own(dve, nc.vector.tensor_copy(sample_raw[j][:, :, 0:3],
                                                    old_conv[:, bass.ds(c, 1)].rearrange("p c b k -> p (c b) k")),
                         old_placed, c + 1)
                dve.wait_ge(raw_ready, c + 1)
                dve.wait_ge(acc_free, c * 3 + (3 * M_X + 3))
                wait(dve, feat_ready, c + (M_X - 1))
                outs = (conv[j][:, 0:SEQ], conv[j][:, SEQ:T].rearrange("p (b s) -> p b s", s=DEC_S))
                for k in range(CONV_K):
                    ins = (prompt_raw[j][:, k:k + SEQ], sample_raw[j][:, :, k:k + DEC_S])
                    for part in range(2):
                        tap = cw[:, k, bass.ds(c, 1)]
                        if k == 0:
                            i = nc.vector.tensor_scalar(outs[part], ins[part], tap, None, ALU.mult)
                        else:
                            dve.wait_ge(conv_chain, c * 6 + (2 * (k - 1) + part + 1))
                            i = nc.vector.scalar_tensor_tensor(out=outs[part], in0=ins[part], scalar=tap, in1=outs[part],
                                                               op0=ALU.mult, op1=ALU.add)
                        if k < CONV_K - 1:
                            i.then_inc(conv_chain, 1)
                        elif part == 1:
                            i.then_inc(conv_done, 1)
                nc.vector.tensor_copy(tail[:, bass.ds(c, 1), 0, :], prompt_raw[j][:, SEQ:SEQ + 3].unsqueeze(1)).then_inc(tail_ready, 1)
                nc.vector.tensor_copy(tail[:, bass.ds(c, 1), 1:, :].rearrange("p c b k -> p (c b) k"),
                                      sample_raw[j][:, :, 4:7]).then_inc(tail_ready, 1)

            unload(0, 0)
            unload(1, 1)
            with dve.Fori(1, M_X // 2) as a:
                for j in range(2):
                    dve.wait_ge(stage_stored[j], a * 32)
                    unload(a * 2 + j, j)
            dve.wait_ge(pad_zero, 2)
            for c in (0, 1):
                convolve(c, c)
                dve.wait_ge(stage_stored[c], 32 * (M_X // 2))
                unload(M_X + c, c)
            with dve.Fori(M_X // 2 + 1, M_C // 2) as a:
                for j in range(2):
                    convolve(a * 2 + (j - M_X), j)
                    dve.wait_ge(stage_stored[j], a * 32)
                    unload(a * 2 + j, j)
            for m in (M_C, M_C + 1):
                convolve(m - M_X, m % 2)
            dve.wait_ge(dt_act, NB3 + 3)
            dve.wait_ge(acc_free, 3 * M_U + 3)
            link = [0]

            def chained(ins):
                link[0] += 1
                then_own(dve, ins, dt_chain, link[0])

            chained(nc.vector.tensor_scalar(dtw[:, 4, :], dtw[:, 2, :], 1.0, -1.0, ALU.add, ALU.add))
            chained(nc.vector.tensor_scalar(dtw[:, 5, :], dtw[:, 4, :], 0.0, None, ALU.is_equal))
            chained(nc.vector.tensor_tensor(dtw[:, 4, :], dtw[:, 4, :], dtw[:, 5, :], ALU.add))
            chained(nc.vector.tensor_tensor(dtw[:, 3, :], dtw[:, 3, :], dtw[:, 5, :], ALU.add))
            chained(nc.vector.tensor_tensor(dtw[:, 3, :], dtw[:, 3, :], dtw[:, 2, :], ALU.mult))
            chained(nc.vector.reciprocal(dtw[:, 4, :], dtw[:, 4, :]))
            chained(nc.vector.tensor_tensor(dtw[:, 3, :], dtw[:, 3, :], dtw[:, 4, :], ALU.mult))
            chained(nc.vector.tensor_tensor(dtw[:, 4, :], dtw[:, 3, :], dtw[:, 1, :], ALU.add))
            nc.vector.tensor_scalar(dtw[:, 5, :], dtw[:, 4, :], hcol[:, 2:3], -1.0, ALU.mult, ALU.mult).then_inc(dt_ready, 1)
            dve.wait_ge(dt_psum, 1)
            nc.vector.tensor_copy(S["dtk"][:, 0:NT, :], bank[6][:, 0:32 * NT].rearrange("p (t c) -> p t c", t=NT)).then_inc(dt_done, 1)
            nc.vector.tensor_copy(S["dtk"][0:TS, NT, :], bank[6][0:TS, 32 * NT:32 * NT + 32]).then_inc(dt_done, 1)
            with dve.Fori(M_C // 2, M_C // 2 + (M_END - M_V) // 2) as a:
                for j in range(2):
                    dve.wait_ge(stage_stored[j], a * 32)
                    unload(a * 2 + j, j)
            dve.wait_ge(dt_done, 2)

        @block.gpsimd
        def _(pool):
            def store_turned(q, j, dst, col):
                pool.wait_ge(stage_ready, q + 1)
                pool.dma_start(dst[0:SEQ, bass.ds(col, P)].rearrange("(t p) c -> p t c", p=P),
                               stage[j][:, 0:NT, :]).then_inc(stage_stored[j], 16)
                pool.dma_start(dst[SEQ:T, bass.ds(col, P)], stage[j][0:TS, NT, :]).then_inc(stage_stored[j], 16)

            def store_feat(m, j, dst, row):
                pool.wait_ge(feat_ready, m + 1)
                pool.dma_start(dst[bass.ds(row, P), :], feat[j][:]).then_inc(feat_stored[j], 16)

            make_constants(nc, pool, C)
            with pool.Fori(0, M_X // 2) as a:
                for j in range(2):
                    store_turned(a * 2 + j, j, S["z"], a * (2 * P) + j * P)
            with pool.Fori(M_X // 2, M_B // 2) as a:
                for j in range(2):
                    store_turned(a * 2 + j, j, S["xb"], a * (2 * P) + (j - M_X) * P)
            for m in (M_B, M_B + 1):
                store_feat(m, m % 2, S["bct"], (m - M_B) * P)
                store_turned(m, m % 2, S["xb"], (m - M_X) * P)
            for m in (M_C, M_C + 1):
                store_feat(m, m % 2, S["bct"], (m - M_B) * P)
            pool.wait_ge(tail_ready, 2 * CT_N)
            pool.dma_start(A["conv_tail"], tail[:]).then_inc(tail_stored, 16)
            with pool.Fori(M_U // 2, M_V // 2) as a:
                for j in range(2):
                    store_feat(a * 2 + j, j, S["uT"], a * (2 * P) + (j - M_U) * P)
            with pool.Fori(M_V // 2, M_END // 2) as a:
                for j in range(2):
                    store_turned(a * 2 + (j + M_C - M_V), j, S["v"], a * (2 * P) + (j - M_V) * P)
            for j in range(2):
                pool.wait_ge(feat_stored[j], 16 * ((M_V - M_B) // 2))
                pool.wait_ge(stage_stored[j], 32 * ((M_C + M_END - M_V) // 2))
            pool.wait_ge(tail_stored, 16)


def held(eng, value):
    return value if isinstance(value, int) else eng.snap(value)


class Links:

    def __init__(self, eng, sem, per):
        self.eng, self.sem, self.per, self.base, self.k = eng, sem, per, 0, 0

    def begin(self, tile):
        self.base, self.k = tile * self.per, 0

    def __call__(self, ins):
        self.k += 1
        assert self.k <= self.per or (isinstance(self.base, int) and self.base == self.per * NT)
        ins.then_inc(self.sem, 1)
        self.eng.wait_ge(self.sem, self.base + self.k)

    def settle(self):
        self.k += 1
        self.eng.sem_inc(self.sem, 1)


def mixer(nc, A, S, C, bank):
    with ExitStack() as ctx:
        def sb(name, shape, dt=F32):
            return ctx.enter_context(nc.sbuf_tensor(name, shape, dt))

        def sem(name):
            return ctx.enter_context(nc.semaphore(name))

        w_out = S["w_out"]
        xb = sb("xb", [P, D + GROUPS * NSTATE])
        bct = sb("bct", [P, 2 * GROUPS, P])
        uT = sb("uT_t", [P, SGH, P])
        v = sb("v_t", [P, D])
        z = sb("z_t", [P, D])
        x = sb("x_t", [P, D])
        seg_lhs = sb("seg_lhs", [P, HEADS, P])
        M = sb("M", [P, HEADS, P])
        cbm = sb("cbm", [P, GROUPS, P])
        decay = sb("decay", [P, 3, HEADS])
        xdt = sb("xdt", [P, D])
        xdtE = sb("xdtE", [P, D])
        xD = sb("xD", [P, D])
        y = sb("y", [P, D])
        yT = sb("yT", [P, KT, P])
        ysgT = sb("ysgT", [P, SGH, P])
        state = sb("state", [P, D])
        h = sb("h_t", [P, D])
        hn = sb("hn_t", [P, D])
        hnT = sb("hnT", [P, KT, P])
        junk = sb("junk", [P, D])
        ssm_w, sg_w_row, ffn_w = sb("ssm_w", [P, D]), sb("sg_w_row", [P, D]), sb("ffn_w", [P, D])
        sgWT = sb("sgWT", [P, SGH, P])
        sgWT_s = sb("sgWT_s", [TS, SGH, TS])
        sgb = sb("sgb", [P, SGH, P])
        d_skip = sb("d_skip", [P, HEADS])
        w_router = sb("w_router", [P, KT, EG + E])
        b_router = sb("b_router", [P, EG + E])
        st_v, st_h = sb("st_v", [P, 4]), sb("st_h", [P, 4])
        st_y = sb("st_y", [P, 6])
        lg = sb("lg", [P, EG + E])
        r8 = sb("r8", [P, 8, 8])
        idx = sb("idx", [P, 2, 8], U32)
        pick = sb("pick", [P, EG, EPG])
        chosen = sb("chosen", [P, E])
        run = S["run"]
        le_s, gt_s = sb("le_s", [TS, TS]), sb("gt_s", [TS, TS])
        dta_s = sb("dta_s", [TS, DEC_B, HEADS])
        decay_s = sb("decay_s", [P, DEC_B, HEADS])
        c_of = [sb(f"c_of{j}", [P, GROUPS, TS]) for j in range(2)]
        b_of = [sb(f"b_of{j}", [TS, GROUPS * NSTATE]) for j in range(2)]
        old = [sb(f"old{j}", [P, D]) for j in range(2)]

        consts_loaded, consts_done = sem("consts_loaded"), sem("consts_done")
        xb_loaded, bct_loaded, u_loaded = sem("xb_loaded"), sem("bct_loaded"), sem("u_loaded")
        v_loaded, z_loaded, xr_loaded = sem("v_loaded"), sem("z_loaded"), sem("xr_loaded")
        cb_psum, cbm_ready, decay_ready = sem("cb_psum"), sem("cbm_ready"), sem("decay_ready")
        seg_ready, seg_psum, seg_exp, m_ready = sem("seg_ready"), sem("seg_psum"), sem("seg_exp"), sem("m_ready")
        xdt_ready, xdtE_ready, xD_ready = sem("xdt_ready"), sem("xdtE_ready"), sem("xD_ready")
        vn_ready, sg_psum, sg_sum, sg_ready = sem("vn_ready"), sem("sg_psum"), sem("sg_sum"), sem("sg_ready")
        yd_psum, st_psum, yo_psum = sem("yd_psum"), sem("st_psum"), sem("yo_psum")
        yo_used, yd_used, gated, yn_ready = sem("yo_used"), sem("yd_used"), sem("gated"), sem("yn_ready")
        state_ready = sem("state_ready")
        yT_psum, yT_done = sem("yT_psum"), sem("yT_done")
        sgproj_done, mix_psum, h_ready, hn_ready = sem("sgproj_done"), sem("mix_psum"), sem("h_ready"), sem("hn_ready")
        h_stored, hn_stored = sem("h_stored"), sem("hn_stored")
        hnT_psum, hnT_done, logits_psum = sem("hnT_psum"), sem("hnT_done"), sem("logits_psum")
        assigned, count_psum, counted = sem("assigned"), sem("count_psum"), sem("counted")
        v_sq, v_rms, y_sq, y_rms, h_sq, h_rms = (sem(n) for n in ("v_sq", "v_rms", "y_sq", "y_rms", "h_sq", "h_rms"))
        link1, link2, link3 = sem("link1"), sem("link2"), sem("link3")
        shifted, exped = sem("shifted"), sem("exped")
        old_loaded = [sem(f"old_loaded{j}") for j in range(2)]
        old_stored = [sem(f"old_stored{j}") for j in range(2)]
        of_ready, of_used, new_psum, new_ready = sem("of_ready"), sem("of_used"), sem("new_psum"), sem("new_ready")
        final_stored = sem("final_stored")
        rep_psum = sem("rep_psum")
        addressing = sem("addressing")

        dtk = S["dtk"]
        N_LOADS = 10
        N_CONSTS = 7

        def heads(t, r):
            return t[0:r, 0:D].rearrange("p (h d) -> p h d", d=HD)

        block = ctx.enter_context(nc.Block())

        @block.sync
        def _(sp):
            for dst, src in ((sg_w_row, A["sg_norm_w"][0].partition_broadcast(P)), (sgWT, A["sg_w"]),
                             (sgb, A["sg_b"][0].partition_broadcast(P)), (d_skip, A["d_skip"][0].partition_broadcast(P))):
                sp.dma_start(dst[:], src).then_inc(consts_loaded, 16)

            def step(I, s1, s2):
                i = I - 1
                r, r2 = rows_of(I), rows_of(i)
                I1, I2, i2, i22, i1 = (held(sp, q) for q in (I, I * 2, i * 2, i * 2 + 2, i + 1))
                at, at2 = held(sp, I * P), held(sp, i * P)
                now, before = bass.ds(at, r), bass.ds(at2, r2)
                if s1:
                    wait(sp, sg_psum, I2)
                    sp.dma_start(v[0:r, :], S["v"][now, :]).then_inc(v_loaded, 16)
                    wait(sp, sg_ready, I2)
                    sp.sem_inc(addressing, 1)
                    sp.dma_start(uT[:, :, 0:r], S["uT"].rearrange("(h p) t -> p h t", p=P)[:, :, now]).then_inc(u_loaded, 16)
                if s2:
                    wait(sp, h_ready, i2)
                    src = A["x_sample"].rearrange("b s d -> (b s) d") if r2 == TS else A["x_prompt"][0][before, :]
                    sp.dma_start(x[0:r2, :], src).then_inc(xr_loaded, 16)
                if s1:
                    wait(sp, yo_psum, I2)
                    sp.sem_inc(addressing, 1)
                    sp.dma_start(bct[:, :, 0:r], S["bct"].rearrange("(g p) t -> p g t", p=P)[:, :, now]).then_inc(bct_loaded, 16)
                    wait(sp, st_psum, I2)
                    wait(sp, xD_ready, I1)
                    sp.dma_start(xb[0:r, :], S["xb"][now, :]).then_inc(xb_loaded, 16)
                    wait(sp, gated, I1)
                    sp.dma_start(z[0:r, :], S["z"][now, :]).then_inc(z_loaded, 16)
                if s2:
                    sp.wait_ge(h_ready, i22)
                    sp.dma_start(S["h"][before, :], h[0:r2, :]).then_inc(h_stored, 16)
                    sp.wait_ge(hn_ready, i1)
                    sp.dma_start(S["hn"][before, :], hn[0:r2, :]).then_inc(hn_stored, 16)

            step(0, True, False)
            for dst, name in ((ssm_w, "ssm_norm_w"), (ffn_w, "norm_ffn_w"), (b_router, "b_router")):
                sp.dma_start(dst[:], A[name][0].partition_broadcast(P)).then_inc(consts_loaded, 16)
            sp.dma_start(w_router[:], A["w_router"]).then_inc(consts_loaded, 16)
            sp.dma_start(w_out[:, 0:KT, :], A["w_out"][:, 0:KT, :]).then_inc(consts_loaded, 16)
            step(1, True, True)
            with sp.Fori(2, NT) as I:
                step(I, True, True)
            for j in range(2):
                sp.dma_start(old[j][:], A["state_ssm"][j]).then_inc(old_loaded[j], 16)
            step(NT, True, True)
            sp.wait_ge(state_ready, 2 * NT)
            sp.dma_start(A["ssm_prompt"], state[:]).then_inc(final_stored, 16)
            sp.wait_ge(vn_ready, NT + 1)
            sp.dma_start(A["sg_v_sample"], v[0:TS, :]).then_inc(final_stored, 16)
            for b in range(DEC_B):
                j = b % 2
                sp.wait_ge(new_ready, 2 * (b + 1))
                sp.dma_start(A["ssm_sample"][b], old[j][:]).then_inc(old_stored[j], 16)
                if b + 2 < DEC_B:
                    sp.wait_ge(old_stored[j], 16 * (b // 2 + 1))
                    sp.dma_start(old[j][:], A["state_ssm"][b + 2]).then_inc(old_loaded[j], 16)
            step(NT + 1, False, True)
            for s in old_stored:
                sp.wait_ge(s, 16 * (DEC_B // 2))
            sp.wait_ge(final_stored, 32)
            sp.wait_ge(h_stored, 16 * (NT + 1))
            sp.wait_ge(hn_stored, 16 * (NT + 1))

        @block.gpsimd
        def _(pool):
            pool.wait_ge(consts_loaded, 16 * N_LOADS)

            def step(i):
                r = rows_of(i)
                gt = C["gt"] if r == P else gt_s
                wait(pool, seg_psum, i * 4)
                nc.gpsimd.tensor_tensor(seg_lhs[0:r, :, 0:r], gt[0:r, 0:r].unsqueeze(1).to_broadcast([r, HEADS, r]),
                                        dtk[0:r, bass.ds(i, 1), HEADS:2 * HEADS].rearrange("p o h -> p (o h)").unsqueeze(2).to_broadcast([r, HEADS, r]),
                                        ALU.mult).then_inc(seg_ready, 1)
                pool.wait_ge(xb_loaded, i * 16 + 16)
                wait(pool, gated, i)
                nc.gpsimd.tensor_tensor(heads(xD, r), heads(xb, r), d_skip[0:r, :].unsqueeze(2).to_broadcast([r, HEADS, HD]),
                                        ALU.mult).then_inc(xD_ready, 1)
                pool.wait_ge(decay_ready, i + 1)
                pool.wait_ge(xdt_ready, i + 1)
                wait(pool, st_psum, i * 2)
                nc.gpsimd.tensor_tensor(heads(xdtE, r), heads(xdt, r), decay[0:r, 2, :].unsqueeze(2).to_broadcast([r, HEADS, HD]),
                                        ALU.mult).then_inc(xdtE_ready, 1)

            step(0)
            with pool.Fori(1, NT) as i:
                step(i)
            pool.wait_ge(consts_done, N_CONSTS)
            step(NT)

        @block.tensor
        def _(pe):
            def sg_projection(i, k0, k1):
                r = rows_of(i)
                for k in range(k0, k1):
                    for n in range(2):
                        last = nc.tensor.matmul(bank[6 + n][0:r, :], ysgT[:, k, 0:r], w_out[:, KT + k, n * 512:(n + 1) * 512],
                                                start=(k == 0), stop=False)
                return last

            def turn_hn(i, half):
                r = rows_of(i)
                pe.wait_ge(hn_ready, i + 1)
                if half == 0:
                    pe.wait_ge(yo_used, min(2 * i + 4, 2 * NT + 2) if isinstance(i, int) else i * 2 + 4)
                    if isinstance(i, int) and i > 0 or not isinstance(i, int):
                        pe.wait_ge(counted, i)
                else:
                    pe.wait_ge(hnT_done, i * 2 + 1)
                for q in range(4):
                    k = 4 * half + q
                    last = nc.tensor.transpose(bank[5][:, q * P:q * P + r], hn[0:r, k * P:(k + 1) * P], C["ident"][0:r, 0:r])
                last.then_inc(hnT_psum, 1)

            def step(I, s1, s2, s3):
                if s2:
                    i2 = I - 1
                    pe.wait_ge(sg_ready, i2 * 2 + 2)
                    wait(pe, h_ready, i2 * 2)
                    sg_projection(i2, 0, KT // 2)
                if s3:
                    turn_hn(I - 2, 0)
                if s2:
                    sg_projection(i2, KT // 2, KT).then_inc(sgproj_done, 1)
                if s3:
                    turn_hn(I - 2, 1)
                if s1:
                    r = rows_of(I)
                    le, gt = (C["le"], C["gt"]) if r == P else (le_s, gt_s)
                    dta = dtk[0:r, bass.ds(I, 1), HEADS:2 * HEADS].rearrange("p o h -> p (o h)")
                    pe.wait_ge(bct_loaded, I * 16 + 16)
                    wait(pe, yo_used, I * 2)
                    for g in range(GROUPS):
                        nc.tensor.matmul(bank[2][0:r, g * P:g * P + r], bct[:, g, 0:r], bct[:, GROUPS + g, 0:r],
                                         start=True, stop=True)
                    nc.tensor.matmul(bank[2][0:r, 256:272], le[0:r, 0:r], dta, start=True, stop=True)
                    if r == P:
                        nc.tensor.matmul(bank[2][:, 272:288], C["ones"][:], dta, start=True, stop=True)
                    nc.tensor.matmul(bank[2][0:r, 288:304], gt[0:r, 0:r], dta, start=True, stop=True).then_inc(cb_psum, 1)
                    if r == TS:
                        pe.wait_ge(link1, LINK1 * NT + 2)
                        nc.tensor.matmul(bank[2][:, 304:304 + DEC_B * HEADS], C["ones"][0:TS, :],
                                         dta_s[:].rearrange("p b h -> p (b h)"), start=True, stop=True).then_inc(cb_psum, 1)
                    pe.wait_ge(seg_ready, I + 1)
                    wait(pe, state_ready, I * 2)
                    for q in range(4):
                        if q >= 2:
                            pe.wait_ge(seg_exp, I * 4 + (q - 1))
                        for hh in range(4):
                            last = nc.tensor.matmul(bank[q % 2][0:r, hh * P:hh * P + r], seg_lhs[0:r, 4 * q + hh, 0:r],
                                                    le[0:r, 0:r], start=True, stop=True)
                        last.then_inc(seg_psum, 1)
                if s3:
                    i3 = I - 2
                    r3 = rows_of(i3)
                    pe.wait_ge(hnT_done, i3 * 2 + 2)
                    for k in range(KT):
                        last = nc.tensor.matmul(bank[5][0:r3, 0:EG + E], hnT[:, k, 0:r3], w_router[:, k, :],
                                                start=(k == 0), stop=(k == KT - 1))
                    last.then_inc(logits_psum, 1)
                if s2:
                    r2 = rows_of(i2)
                    pe.wait_ge(yn_ready, i2 + 1)
                    for half in range(2):
                        for q in range(4):
                            k = 4 * half + q
                            last = nc.tensor.transpose(bank[3 + half][:, q * P:q * P + r2], y[0:r2, k * P:(k + 1) * P],
                                                       C["ident"][0:r2, 0:r2])
                        last.then_inc(yT_psum, 1)
                if s1:
                    W = sgWT if r == P else sgWT_s
                    pe.wait_ge(vn_ready, I + 1)
                    for q in range(2):
                        pe.wait_ge(seg_exp, I * 4 + (3 + q))
                        for hh in range(4):
                            hd = 4 * q + hh
                            last = nc.tensor.matmul(bank[q][:, hh * P:hh * P + r], v[0:r, hd * P:(hd + 1) * P],
                                                    W[0:r, hd, 0:r], start=True, stop=True)
                        last.then_inc(sg_psum, 1)
                if s2:
                    for half in range(2):
                        pe.wait_ge(yT_done, i2 * 2 + (half + 1))
                        for k in range(4 * half, 4 * half + 4):
                            for n in range(2):
                                last = nc.tensor.matmul(bank[6 + n][0:r2, :], yT[:, k, 0:r2], w_out[:, k, n * 512:(n + 1) * 512],
                                                        start=False, stop=(k == KT - 1))
                    last.then_inc(mix_psum, 1)
                if s3:
                    pe.wait_ge(assigned, i3 + 1)
                    nc.tensor.matmul(bank[5][0:r3, 64:64 + E], C["lt"][0:r3, 0:r3], chosen[0:r3, :], start=True, stop=True)
                    nc.tensor.matmul(bank[5][:, 96:96 + E], C["ones"][0:r3, :], chosen[0:r3, :], start=True, stop=True).then_inc(count_psum, 1)
                if s1:
                    pe.wait_ge(xdt_ready, I + 1)
                    wait(pe, yT_done, I * 2)
                    for g in range(GROUPS):
                        pe.wait_ge(m_ready, I * 4 + (2 * g + 2))
                        for hh in range(8):
                            hd = 8 * g + hh
                            last = nc.tensor.matmul(bank[3 + g][0:r, hh * HD:(hh + 1) * HD], M[0:r, hd, 0:r],
                                                    xdt[0:r, hd * HD:(hd + 1) * HD], start=True, stop=True)
                        last.then_inc(yd_psum, 1)
                    pe.wait_ge(xdtE_ready, I + 1)
                    if s3:
                        pe.wait_ge(counted, i3 + 1)
                    if r == P:
                        for g in range(GROUPS):
                            pe.wait_ge(sg_sum, I * 2 + (g + 1))
                            nc.tensor.matmul(bank[g][:, :], xb[:, D + g * NSTATE:D + (g + 1) * NSTATE],
                                             xdtE[:, g * 512:(g + 1) * 512], start=True, stop=True).then_inc(st_psum, 1)
                        pe.wait_ge(decay_ready, I + 1)
                        pe.wait_ge(cbm_ready, I + 1)
                        for g in (1, 0):
                            nc.tensor.matmul(bank[2 if g else 5][:, :], bct[:, GROUPS + g, :], state[:, g * 512:(g + 1) * 512],
                                             start=True, stop=True).then_inc(yo_psum, 1)
                    else:
                        pe.wait_ge(sg_sum, I * 2 + 2)
                        pe.wait_ge(decay_ready, I + 1)
                        pe.wait_ge(cbm_ready, I + 1)
                        for b in range(DEC_B):
                            j = b % 2
                            pe.wait_ge(old_loaded[j], 16 * (b // 2 + 1))
                            pe.wait_ge(of_ready, b + 1)
                            for g in (1, 0):
                                last = nc.tensor.matmul(bank[2 if g else 5][0:TS, :], c_of[j][:, g, :], old[j][:, g * 512:(g + 1) * 512],
                                                        start=(b == 0), stop=(b == DEC_B - 1))
                                if b == DEC_B - 1:
                                    last.then_inc(yo_psum, 1)
                            for g in range(GROUPS):
                                wait(pe, new_ready, 2 * (b - 1) + g + 1)
                                nc.tensor.matmul(bank[g][:, :], b_of[j][:, g * NSTATE:(g + 1) * NSTATE],
                                                 xdtE[0:TS, g * 512:(g + 1) * 512], start=True, stop=True).then_inc(new_psum, 1)

            pe.wait_ge(consts_done, 1)
            nc.tensor.matmul(bank[2][0:TS, 0:SGH * DEC_S], C["repeat"][:], sgWT[0:DEC_S, :, 0:DEC_S],
                             start=True, stop=True).then_inc(rep_psum, 1)
            pe.wait_ge(consts_done, N_CONSTS)
            pe.wait_ge(consts_loaded, 16 * N_LOADS)
            step(0, True, False, False)
            step(1, True, True, False)
            with pe.Fori(2, NT) as I:
                step(I, True, True, True)
            step(NT, True, True, True)
            step(NT + 1, False, True, True)
            step(NT + 2, False, False, True)

        @block.scalar
        def _(act):
            def step(I, s1, s2, s3):
                if s3:
                    i3 = I - 2
                    r3 = rows_of(i3)
                    for half in range(2):
                        act.wait_ge(hnT_psum, i3 * 2 + (half + 1))
                        wait(act, logits_psum, i3)
                        nc.scalar.copy(hnT[:, 4 * half:4 * half + 4, 0:r3],
                                       bank[5][:].rearrange("p (k t) -> p k t", k=4)[:, :, 0:r3]).then_inc(hnT_done, 1)
                if s1:
                    r = rows_of(I)
                    if r == P:
                        act.wait_ge(cb_psum, I + 1)
                    else:
                        act.wait_ge(cb_psum, NT + 2)
                        nc.scalar.activation(decay_s[:].rearrange("p b h -> p (b h)"), bank[2][:, 304:304 + DEC_B * HEADS], ACT.Exp)
                    wait(act, xdtE_ready, I)
                    wait(act, state_ready, I * 2)
                    if r == P:
                        nc.scalar.activation(decay[:].rearrange("p a h -> p (a h)"), bank[2][:, 256:304], ACT.Exp).then_inc(decay_ready, 1)
                    else:
                        nc.scalar.activation(decay[0:TS, 0, :], bank[2][0:TS, 256:272], ACT.Exp)
                        nc.scalar.activation(decay[0:TS, 2, :], bank[2][0:TS, 288:304], ACT.Exp).then_inc(decay_ready, 1)
                    wait(act, yd_psum, I * 2)
                    for q in range(4):
                        act.wait_ge(seg_psum, I * 4 + (q + 1))
                        nc.scalar.activation(M[0:r, 4 * q:4 * q + 4, 0:r],
                                             bank[q % 2][:].rearrange("p (h l) -> p h l", h=4)[0:r, :, 0:r],
                                             ACT.Exp).then_inc(seg_exp, 1)
                if s3:
                    act.wait_ge(shifted, i3 * 2 + 1)
                    nc.scalar.activation(r8[0:r3, 1, 0:EG], lg[0:r3, 0:EG], ACT.Exp, bias=r8[0:r3, 0, 1:2],
                                         accum_out=r8[0:r3, 0, 2:3]).then_inc(exped, 1)
                    act.wait_ge(shifted, i3 * 2 + 2)
                    nc.scalar.activation(r8[0:r3, 4, :], r8[0:r3, 3, :], ACT.Exp, bias=r8[0:r3, 0, 4:5],
                                         accum_out=r8[0:r3, 0, 5:6]).then_inc(exped, 1)
                if s1:
                    act.wait_ge(v_loaded, I * 16 + 16)
                    wait(act, vn_ready, I)
                    then_own(act, nc.scalar.activation(junk[0:r, :], v[0:r, :], ACT.Square, accum_out=st_v[0:r, 0:1]), v_sq, I + 1)
                    nc.scalar.activation(st_v[0:r, 1:2], st_v[0:r, 0:1], ACT.Sqrt, bias=C["eps"][0:r, :], scale=1.0 / D).then_inc(v_rms, 1)
                if s2:
                    i2 = I - 1
                    r2 = rows_of(i2)
                    wait(act, mix_psum, i2)
                    for half in range(2):
                        act.wait_ge(yT_psum, i2 * 2 + (half + 1))
                        nc.scalar.copy(yT[:, 4 * half:4 * half + 4, 0:r2],
                                       bank[3 + half][:].rearrange("p (k t) -> p k t", k=4)[:, :, 0:r2]).then_inc(yT_done, 1)
                    act.wait_ge(h_ready, i2 * 2 + 2)
                    wait(act, hn_ready, i2)
                    then_own(act, nc.scalar.activation(junk[0:r2, :], h[0:r2, :], ACT.Square, accum_out=st_h[0:r2, 0:1]), h_sq, i2 + 1)
                    nc.scalar.activation(st_h[0:r2, 1:2], st_h[0:r2, 0:1], ACT.Sqrt, bias=C["eps"][0:r2, :], scale=1.0 / D).then_inc(h_rms, 1)
                if s1:
                    act.wait_ge(gated, I + 1)
                    wait(act, yn_ready, I)
                    for g in range(GROUPS):
                        nc.scalar.activation(junk[0:r, g * 512:(g + 1) * 512], y[0:r, g * 512:(g + 1) * 512], ACT.Square,
                                             accum_out=st_y[0:r, g:g + 1]).then_inc(y_sq, 1)
                    act.wait_ge(y_sq, I * 2 + 2)
                    nc.scalar.activation(st_y[0:r, 2:4], st_y[0:r, 0:2], ACT.Sqrt, bias=C["eps"][0:r, :],
                                         scale=2.0 / D).then_inc(y_rms, 1)

            act.dma_start(w_out[:, KT:2 * KT, :], A["w_out"][:, KT:2 * KT, :]).then_inc(consts_loaded, 16)
            step(0, True, False, False)
            step(1, True, True, False)
            with act.Fori(2, NT) as I:
                step(I, True, True, True)
            step(NT, True, True, True)
            step(NT + 1, False, True, True)
            step(NT + 2, False, False, True)

        @block.vector
        def _(dve):
            l1, l2, l3 = Links(dve, link1, LINK1), Links(dve, link2, LINK2), Links(dve, link3, LINK3)

            def over(t, r, n):
                return t.unsqueeze(2).to_broadcast([r, HEADS, n])

            def halves(t, r, g):
                return t[0:r, g * 512:(g + 1) * 512].rearrange("p (h d) -> p h d", d=HD)

            def route(i, r):
                l3.begin(i)
                dve.wait_ge(logits_psum, i + 1)
                R = r8[0:r]
                l3(nc.vector.tensor_tensor(lg[0:r, :], bank[5][0:r, 0:EG + E], b_router[0:r, :], ALU.add))
                l3(nc.vector.tensor_reduce(R[:, 0, 0:1], lg[0:r, 0:EG], AX.X, ALU.max))
                nc.vector.tensor_scalar(R[:, 0, 1:2], R[:, 0, 0:1], -1.0, None, ALU.mult).then_inc(shifted, 1)
                dve.wait_ge(exped, i * 2 + 1)
                l3(nc.vector.reciprocal(R[:, 0, 0:1], R[:, 0, 2:3]))
                l3(nc.vector.tensor_scalar(R[:, 1, 0:EG], R[:, 1, 0:EG], R[:, 0, 0:1], None, ALU.mult))
                l3.settle()
                l3(nc.vector.max(R[:, 2, :], R[:, 1, :]))
                l3.settle()
                l3(nc.vector.max_index(idx[0:r, 0, :], R[:, 2, :], R[:, 1, :]))
                l3(nc.vector.tensor_copy(R[:, 0, 6:7], idx[0:r, 0, 0:1]))
                l3(nc.vector.tensor_scalar(R[:, 7, 0:EG], C["expert_no"][0:r, 0:EG], R[:, 0, 6:7], None, ALU.is_equal))
                l3(nc.vector.tensor_tensor(pick[0:r], lg[0:r, EG:].rearrange("p (g e) -> p g e", e=EPG),
                                           R[:, 7, 0:EG].unsqueeze(2).to_broadcast([r, EG, EPG]), ALU.mult))
                l3(nc.vector.tensor_reduce(R[:, 3, :], pick[0:r].rearrange("p g e -> p e g"), AX.X, ALU.add))
                l3(nc.vector.tensor_reduce(R[:, 0, 3:4], R[:, 3, :], AX.X, ALU.max))
                nc.vector.tensor_scalar(R[:, 0, 4:5], R[:, 0, 3:4], -1.0, None, ALU.mult).then_inc(shifted, 1)
                dve.wait_ge(exped, i * 2 + 2)
                l3(nc.vector.reciprocal(R[:, 0, 7:8], R[:, 0, 5:6]))
                l3(nc.vector.tensor_scalar(R[:, 4, :], R[:, 4, :], R[:, 0, 7:8], None, ALU.mult))
                l3.settle()
                l3(nc.vector.max(R[:, 5, :], R[:, 4, :]))
                l3.settle()
                l3(nc.vector.max_index(idx[0:r, 1, :], R[:, 5, :], R[:, 4, :]))
                l3(nc.vector.tensor_copy(R[:, 6, 0:2], idx[0:r, 1, 0:2]))
                l3(nc.vector.tensor_scalar(R[:, 0, 3:4], R[:, 0, 6:7], float(EPG), None, ALU.mult))
                l3(nc.vector.tensor_scalar(R[:, 6, 2:4], R[:, 6, 0:2], R[:, 0, 3:4], None, ALU.add))
                l3(nc.vector.tensor_tensor(R[:, 6, 4:5], R[:, 5, 0:1], R[:, 5, 1:2], ALU.add))
                l3(nc.vector.reciprocal(R[:, 6, 5:6], R[:, 6, 4:5]))
                l3(nc.vector.tensor_scalar(S["gate"][0:r, bass.ds(i, 1), :], R[:, 5:6, 0:2], R[:, 2, 0:1], R[:, 6, 5:6],
                                           ALU.mult, ALU.mult))
                hot = S["hot"]
                for k in range(2):
                    l3(nc.vector.tensor_scalar(hot[0:r, bass.ds(i, 1), k, :], C["expert_no"][0:r, :].unsqueeze(1),
                                               R[:, 6, 2 + k:3 + k], None, ALU.is_equal))
                nc.vector.tensor_tensor(chosen[0:r, :].unsqueeze(1), hot[0:r, bass.ds(i, 1), 0, :], hot[0:r, bass.ds(i, 1), 1, :],
                                        ALU.add).then_inc(assigned, 1)

            def step(I, s1, s2, s3):
                if s1:
                    r = rows_of(I)
                    le = C["le"] if r == P else le_s
                    dt_r = dtk[0:r, bass.ds(I, 1), 0:HEADS].rearrange("p o h -> p (o h)")
                    l1.begin(I)
                    if r == TS:
                        l1(nc.vector.tensor_copy(dta_s[:], dtk[0:TS, NT, HEADS:2 * HEADS].unsqueeze(1).to_broadcast([TS, DEC_B, HEADS])))
                        l1(nc.vector.tensor_tensor(dta_s[:], dta_s[:],
                                                   C["same"][:, 0:TS:DEC_S].unsqueeze(2).to_broadcast([TS, DEC_B, HEADS]), ALU.mult))
                    dve.wait_ge(decay_ready, I + 1)
                    nc.vector.tensor_tensor(cbm[0:r, :, 0:r], bank[2][:, 0:2 * P].rearrange("p (g l) -> p g l", g=2)[0:r, :, 0:r],
                                            le[0:r, 0:r].unsqueeze(1).to_broadcast([r, 2, r]), ALU.mult).then_inc(cbm_ready, 1)
                    dve.wait_ge(xb_loaded, I * 16 + 16)
                    wait(dve, yd_psum, I * 2)
                    wait(dve, xdtE_ready, I)
                    nc.vector.tensor_tensor(heads(xdt, r), heads(xb, r), over(dt_r, r, HD), ALU.mult).then_inc(xdt_ready, 1)
                    dve.wait_ge(cbm_ready, I + 1)
                    for q in range(4):
                        dve.wait_ge(seg_exp, I * 4 + (q + 1))
                        nc.vector.tensor_tensor(M[0:r, 4 * q:4 * q + 4, 0:r], M[0:r, 4 * q:4 * q + 4, 0:r],
                                                cbm[0:r, q // 2, 0:r].unsqueeze(1).to_broadcast([r, 4, r]), ALU.mult).then_inc(m_ready, 1)
                if s3:
                    route(I - 2, rows_of(I - 2))
                if s1:
                    dve.wait_ge(v_rms, I + 1)
                    l1(nc.vector.reciprocal(st_v[0:r, 2:3], st_v[0:r, 1:2]))
                    nc.vector.scalar_tensor_tensor(out=v[0:r, :], in0=v[0:r, :], scalar=st_v[0:r, 2:3], in1=sg_w_row[0:r, :],
                                                   op0=ALU.mult, op1=ALU.mult).then_inc(vn_ready, 1)
                    wait(dve, sgproj_done, I)
                    for q in range(2):
                        dve.wait_ge(sg_psum, I * 2 + (q + 1))
                        s = slice(4 * q, 4 * q + 4)
                        got = bank[q][:].rearrange("p (h t) -> p h t", h=4)[:, :, 0:r]
                        if r == P:
                            ins = nc.vector.tensor_tensor(ysgT[:, s, :], got, sgb[:, s, :], ALU.add)
                            ins.then_inc(sg_sum, 1)
                        else:
                            for hh in range(4):
                                seqs = lambda t: t.rearrange("p (b s) -> p b s", s=DEC_S)
                                ins = nc.vector.tensor_tensor(
                                    seqs(ysgT[:, 4 * q + hh, 0:TS]), seqs(got[:, hh, :]),
                                    sgb[:, 4 * q + hh, 0:DEC_S].unsqueeze(1).to_broadcast([P, DEC_B, DEC_S]), ALU.add)
                            ins.then_inc(sg_sum, 1)
                    dve.wait_ge(u_loaded, I * 16 + 16)
                    for q in range(2):
                        s = slice(4 * q, 4 * q + 4)
                        dve.wait_ge(sg_sum, I * 2 + (q + 1))
                        nc.vector.tensor_tensor(ysgT[:, s, 0:r], ysgT[:, s, 0:r], uT[:, s, 0:r], ALU.mult).then_inc(sg_ready, 1)
                if s2:
                    i2 = I - 1
                    r2 = rows_of(i2)
                    l2.begin(i2)
                    dve.wait_ge(mix_psum, i2 + 1)
                    dve.wait_ge(xr_loaded, i2 * 16 + 16)
                    wait(dve, h_stored, i2 * 16)
                    for n in range(2):
                        s = slice(n * 512, (n + 1) * 512)
                        nc.vector.tensor_tensor(h[0:r2, s], bank[6 + n][0:r2, :], x[0:r2, s], ALU.add).then_inc(h_ready, 1)
                    dve.wait_ge(h_rms, i2 + 1)
                    l2(nc.vector.reciprocal(st_h[0:r2, 2:3], st_h[0:r2, 1:2]))
                    wait(dve, hn_stored, i2 * 16)
                    wait(dve, hnT_psum, i2 * 2)
                    dve.wait_ge(h_ready, i2 * 2 + 2)
                    nc.vector.scalar_tensor_tensor(out=hn[0:r2, :], in0=h[0:r2, :], scalar=st_h[0:r2, 2:3], in1=ffn_w[0:r2, :],
                                                   op0=ALU.mult, op1=ALU.mult).then_inc(hn_ready, 1)
                if s3:
                    i3, r3 = I - 2, rows_of(I - 2)
                    dve.wait_ge(count_psum, i3 + 1)
                    l3(nc.vector.tensor_tensor(S["before"][0:r3, bass.ds(i3, 1), :], bank[5][0:r3, 64:64 + E].unsqueeze(1),
                                               run[0:r3, :].unsqueeze(1), ALU.add))
                    nc.vector.tensor_tensor(run[:], bank[5][:, 96:96 + E], run[:], ALU.add).then_inc(counted, 1)
                    dve.wait_ge(counted, i3 + 1)
                if s1:
                    if r == TS:
                        sample_states()
                    wait(dve, yT_psum, I * 2)
                    for n, g in enumerate((1, 0)):
                        dve.wait_ge(yo_psum, I * 2 + (n + 1))
                        nc.vector.tensor_tensor(halves(y, r, g), bank[2 if g else 5][0:r, :].rearrange("p (h d) -> p h d", d=HD),
                                                decay[0:r, 0, 8 * g:8 * g + 8].unsqueeze(2).to_broadcast([r, 8, HD]),
                                                ALU.mult).then_inc(yo_used, 1)
                    for g in range(GROUPS):
                        dve.wait_ge(yd_psum, I * 2 + (g + 1))
                        dve.wait_ge(yo_used, I * 2 + 2)
                        nc.vector.tensor_tensor(halves(y, r, g), halves(y, r, g),
                                                bank[3 + g][0:r, :].rearrange("p (h d) -> p h d", d=HD), ALU.add).then_inc(yd_used, 1)
                    dve.wait_ge(yd_used, I * 2 + 2)
                    dve.wait_ge(xD_ready, I + 1)
                    l1(nc.vector.tensor_tensor(y[0:r, :], y[0:r, :], xD[0:r, :], ALU.add))
                    dve.wait_ge(z_loaded, I * 16 + 16)
                    nc.vector.tensor_tensor(y[0:r, :], y[0:r, :], z[0:r, :], ALU.mult).then_inc(gated, 1)
                    if r == P:
                        l1(nc.vector.tensor_tensor(heads(state, P), heads(state, P), over(decay[:, 1, :], P, HD), ALU.mult))
                        for g in range(GROUPS):
                            dve.wait_ge(st_psum, I * 2 + (g + 1))
                            s = slice(g * 512, (g + 1) * 512)
                            nc.vector.tensor_tensor(state[:, s], state[:, s], bank[g][:, :], ALU.add).then_inc(state_ready, 1)
                    dve.wait_ge(gated, I + 1)
                    if r == P:
                        dve.wait_ge(state_ready, I * 2 + 2)
                    dve.wait_ge(y_rms, I + 1)
                    l1(nc.vector.reciprocal(st_y[0:r, 4:6], st_y[0:r, 2:4]))
                    for g in range(GROUPS):
                        s = slice(g * 512, (g + 1) * 512)
                        ins = nc.vector.scalar_tensor_tensor(out=y[0:r, s], in0=y[0:r, s], scalar=st_y[0:r, 4 + g:5 + g],
                                                             in1=ssm_w[0:r, s], op0=ALU.mult, op1=ALU.mult)
                    ins.then_inc(yn_ready, 1)

            def sample_states():
                dve.wait_ge(bct_loaded, 16 * (NT + 1))
                dve.wait_ge(decay_ready, NT + 1)

                def mask(b):
                    j = b % 2
                    wait(dve, new_psum, 2 * (b - 1))
                    for g in range(GROUPS):
                        nc.vector.tensor_tensor(c_of[j][:, g, :], bct[:, GROUPS + g, 0:TS], C["of_seq"][:, b, :], ALU.mult)
                    nc.vector.tensor_scalar(b_of[j][:], xb[0:TS, D:], C["same"][:, DEC_S * b:DEC_S * b + 1], None,
                                            ALU.mult).then_inc(of_ready, 1)

                mask(0)
                mask(1)
                for b in range(DEC_B):
                    j = b % 2
                    dve.wait_ge(new_psum, 2 * b + 2)
                    l1(nc.vector.tensor_tensor(heads(old[j], P), heads(old[j], P), over(decay_s[:, b, :], P, HD), ALU.mult))
                    for g in range(GROUPS):
                        s = slice(g * 512, (g + 1) * 512)
                        nc.vector.tensor_tensor(old[j][:, s], old[j][:, s], bank[g][:, :], ALU.add).then_inc(new_ready, 1)
                    if b + 2 < DEC_B:
                        mask(b + 2)

            for t in (S["hot"], S["before"]):
                nc.vector.memset(t[:, NT:NT + 1], 0.0)
            nc.vector.memset(run[:], 0.0)
            nc.vector.memset(state[:], 0.0)
            nc.vector.memset(r8[:], -1.0)
            dve.wait_ge(consts_loaded, 16 * N_LOADS)
            nc.vector.tensor_tensor(sgWT[:], sgWT[:], C["le"][:].unsqueeze(1).to_broadcast([P, SGH, P]), ALU.mult).then_inc(consts_done, 1)
            nc.vector.tensor_tensor(le_s[:], C["le"][0:TS, 0:TS], C["same"][:], ALU.mult).then_inc(consts_done, 1)
            nc.vector.tensor_tensor(gt_s[:], C["gt"][0:TS, 0:TS], C["same"][:], ALU.mult).then_inc(consts_done, 1)
            dve.wait_ge(rep_psum, 1)
            for b in range(DEC_B):
                ins = nc.vector.tensor_copy(sgWT_s[:, :, b * DEC_S:(b + 1) * DEC_S],
                                            bank[2][0:TS, 0:SGH * DEC_S].rearrange("p (h t) -> p h t", h=SGH))
            ins.then_inc(consts_done, 1)
            dve.wait_ge(consts_done, 4)
            nc.vector.tensor_tensor(sgWT_s[:], sgWT_s[:], C["same"][:].unsqueeze(1).to_broadcast([TS, SGH, TS]),
                                    ALU.mult).then_inc(consts_done, 1)
            nc.vector.memset(st_v[:], 1.0).then_inc(consts_done, 1)
            nc.vector.memset(st_y[:], 1.0).then_inc(consts_done, 1)
            dve.wait_ge(consts_done, N_CONSTS)
            step(0, True, False, False)
            step(1, True, True, False)
            with dve.Fori(2, NT) as I:
                step(I, True, True, True)
            step(NT, True, True, True)
            step(NT + 1, False, True, True)
            step(NT + 2, False, False, True)


LINK1, LINK2, LINK3 = 4, 1, 28


def experts(nc, A, S, C, bank):
    with ExitStack() as ctx:
        def sb(name, shape, dt=F32):
            return ctx.enter_context(nc.sbuf_tensor(name, shape, dt))

        def sem(name):
            return ctx.enter_context(nc.semaphore(name))

        over = sb("over", [P, E, NT + 1])
        n_blk, blk_end, row0 = sb("n_blk", [P, E]), sb("blk_end", [P, E]), sb("row0", [P, E])
        place = sb("place", [P, NT + 1, 2, E])
        row_f = sb("row_f", [P, NT + 1, 2])
        before_end = sb("before_end", [1, MAXBLK, E])
        blk_f = sb("blk_f", [1, MAXBLK + 1])
        blk_i = sb("blk_i", [1, MAXBLK + 1], I32)
        unfilled = sb("unfilled", [P, MAXBLK, 2], I32)
        row_i = sb("row_i", [P, NT + 1, 2], I32)
        src, dst = sb("src", [P, 2], I32), sb("dst", [P, 2], I32)
        xg = sb("xg", [P, D])
        xT = sb("xT_blk", [P, KT, P])
        wg, wu = sb("wg", [P, KT, FF]), sb("wu", [P, KT, FF])
        wd = sb("wd", [P, FF // P, D])
        act_g, hid = sb("act_g", [P, FF]), sb("hid", [P, FF])
        hT = sb("hT", [P, FF // P, P])
        yb = sb("yb", [P, D])

        chain, table_ready = sem("chain"), sem("table_ready")
        zeroed, filled, scattered = sem("zeroed"), sem("filled"), sem("scattered")
        gate_loaded = [sem(f"gate_loaded{p}") for p in range(4)]
        up_loaded = [sem(f"up_loaded{p}") for p in range(4)]
        down_loaded = [sem(f"down_loaded{p}") for p in range(4)]
        src_loaded, dst_loaded, xg_loaded = sem("src_loaded"), sem("dst_loaded"), sem("xg_loaded")
        gu_used, down_used = sem("gu_used"), sem("down_used")
        silu_done, hid_ready = sem("silu_done"), sem("hid_ready")
        xT_psum, xT_done = sem("xTb_psum"), sem("xTb_done")
        hT_psum, hT_done = sem("hT_psum"), sem("hT_done")
        y_done, y_stored = sem("y_done"), sem("y_stored")
        holder = sem("holder")

        block = ctx.enter_context(nc.Block())

        def blocks_but_two(eng):
            eng.wait_ge(table_ready, 2)
            return eng.value_load(blk_i[0:1, MAXBLK:MAXBLK + 1], min_val=MINBLK - 2, max_val=MAXBLK - 2)

        @block.sync
        def _(sp):
            def expert(i):
                e = sp.value_load(blk_i[0:1, bass.ds(i, 1)], min_val=0, max_val=E - 1)
                return bass.ds(e, 1)

            def load_gate_up(i):
                e = expert(i)
                at = [held(sp, i * 4 + (p - 3)) for p in range(4)]
                for p in range(4):
                    wait(sp, gu_used, at[p])
                    rows = slice(2 * p * P, (2 * p + 2) * P)
                    for t, name, s in ((wg, "w_gate", gate_loaded), (wu, "w_up", up_loaded)):
                        sp.dma_start(t[:, 2 * p:2 * p + 2, :], A[name][e, rows, :].rearrange("e (k p) f -> p (e k) f", p=P)).then_inc(s[p], 16)

            def load_down(i):
                e = expert(i)
                at = [held(sp, i * 4 + (p - 3)) for p in range(4)]
                for p in range(4):
                    wait(sp, down_used, at[p])
                    sp.dma_start(wd[:, p, :], A["w_down"][e, p * P:(p + 1) * P, :].rearrange("e p d -> p (e d)")).then_inc(down_loaded[p], 16)

            m = blocks_but_two(sp)
            load_gate_up(0)
            load_gate_up(1)
            load_down(0)
            with sp.Fori(1, m + 1) as i:
                load_gate_up(i + 1)
                load_down(i)
            load_down(m + 1)
            sp.wait_ge(y_stored, m * 16 + 32)
            sp.sem_inc(holder, 1)

        @block.gpsimd
        def _(pool):
            nc.gpsimd.memset(unfilled[:, :, 0:1], 0).then_inc(zeroed, 1)
            nc.gpsimd.memset(unfilled[:, :, 1:2], 2 * T).then_inc(zeroed, 1)
            pool.wait_ge(zeroed, 2)
            pool.dma_start(S["of_row"].rearrange("(p n) o -> p n o", n=MAXBLK), unfilled[:]).then_inc(filled, 16)
            pool.wait_ge(filled, 16)
            pool.wait_ge(table_ready, 1)
            for t in range(NT + 1):
                r = P if t < NT else TS
                for k in range(2):
                    pool.indirect_dma_start(out=S["of_row"], out_offset=bass.IndirectOffsetOnAxis(ap=row_i[0:r, t, k:k + 1], axis=0),
                                            in_=C["token_slot"][0:r, t, k, :], in_offset=None).then_inc(scattered, 16)
            pool.wait_ge(scattered, 32 * (NT + 1))
            m = blocks_but_two(pool)

            def gather(i):
                wait(pool, xg_loaded, i * 16)
                pool.dma_start(src[:], S["of_row"][bass.ds(i * P, P), :]).then_inc(src_loaded, 16)
                pool.wait_ge(src_loaded, i * 16 + 16)
                wait(pool, xT_psum, i * 2)
                pool.sem_inc(holder, 1)
                pool.indirect_dma_start(out=xg[:], out_offset=None, in_=S["hn"],
                                        in_offset=bass.IndirectOffsetOnAxis(ap=src[:, 0:1], axis=0)).then_inc(xg_loaded, 16)

            def scatter(i):
                wait(pool, y_stored, i * 16)
                pool.dma_start(dst[:], S["of_row"][bass.ds(i * P, P), :]).then_inc(dst_loaded, 16)
                pool.wait_ge(dst_loaded, i * 16 + 16)
                pool.wait_ge(y_done, i * 2 + 2)
                pool.sem_inc(holder, 1)
                pool.indirect_dma_start(out=S["picked"], out_offset=bass.IndirectOffsetOnAxis(ap=dst[:, 1:2], axis=0),
                                        in_=yb[:], in_offset=None, bounds_check=2 * T - 1, oob_is_err=False).then_inc(y_stored, 16)

            gather(0)
            gather(1)
            with pool.Fori(1, m + 1) as i:
                gather(i + 1)
                scatter(i - 1)
            scatter(m)
            scatter(m + 1)

        @block.tensor
        def _(pe):
            def turn_x(i):
                pe.wait_ge(xg_loaded, i * 16 + 16)
                for half in range(2):
                    wait(pe, xT_done, i * 2 + (half - 1))
                    for q in range(4):
                        last = nc.tensor.transpose(bank[4 + half][:, q * P:(q + 1) * P], xg[:, (4 * half + q) * P:(4 * half + q + 1) * P],
                                                   C["ident"][:])
                    last.then_inc(xT_psum, 1)

            def gate_up(i):
                wait(pe, hid_ready, i)
                for k in range(KT):
                    if k % 2 == 0:
                        pe.wait_ge(gate_loaded[k // 2], i * 16 + 16)
                        pe.wait_ge(up_loaded[k // 2], i * 16 + 16)
                    if k % 4 == 0:
                        pe.wait_ge(xT_done, i * 2 + (k // 4 + 1))
                    for n, w in ((0, wg), (1, wu)):
                        last = nc.tensor.matmul(bank[n][:, :], xT[:, k, :], w[:, k, :], start=(k == 0), stop=(k == KT - 1))
                    if k % 2:
                        last.then_inc(gu_used, 1)

            def turn_hid(i):
                pe.wait_ge(hid_ready, i + 1)
                for f in range(FF // P):
                    last = nc.tensor.transpose(bank[6][:, f * P:(f + 1) * P], hid[:, f * P:(f + 1) * P], C["ident"][:])
                last.then_inc(hT_psum, 1)

            def down(i):
                pe.wait_ge(hT_done, i + 1)
                wait(pe, y_done, i * 2)
                for f in range(FF // P):
                    pe.wait_ge(down_loaded[f], i * 16 + 16)
                    for n in range(2):
                        last = nc.tensor.matmul(bank[2 + n][:, :], hT[:, f, :], wd[:, f, n * 512:(n + 1) * 512],
                                                start=(f == 0), stop=(f == FF // P - 1))
                    last.then_inc(down_used, 1)

            m = blocks_but_two(pe)
            turn_x(0)
            gate_up(0)
            turn_x(1)
            turn_hid(0)
            with pe.Fori(1, m + 1) as i:
                gate_up(i)
                turn_x(i + 1)
                down(i - 1)
                turn_hid(i)
            gate_up(m + 1)
            down(m)
            turn_hid(m + 1)
            down(m + 1)

        @block.scalar
        def _(act):
            def unload_x(i):
                for half in range(2):
                    act.wait_ge(xT_psum, i * 2 + (half + 1))
                    wait(act, gu_used, i * 4)
                    nc.scalar.copy(xT[:, 4 * half:4 * half + 4, :], bank[4 + half][:].rearrange("p (k t) -> p k t", k=4)).then_inc(xT_done, 1)

            def silu(i):
                act.wait_ge(gu_used, i * 4 + 4)
                wait(act, hid_ready, i)
                nc.scalar.activation(act_g[:], bank[0][:, :], ACT.Silu).then_inc(silu_done, 1)

            def unload_hid(i):
                act.wait_ge(hT_psum, i + 1)
                wait(act, down_used, i * 4)
                nc.scalar.copy(hT[:], bank[6][:].rearrange("p (k t) -> p k t", k=4)).then_inc(hT_done, 1)

            m = blocks_but_two(act)
            unload_x(0)
            silu(0)
            unload_x(1)
            unload_hid(0)
            with act.Fori(1, m + 1) as i:
                silu(i)
                unload_x(i + 1)
                unload_hid(i)
            silu(m + 1)
            unload_hid(m + 1)

        @block.vector
        def _(dve):
            links = [0]

            def after(ins):
                links[0] += 1
                then_own(dve, ins, chain, links[0])

            after(nc.vector.tensor_tensor(over[:], S["run"][:].unsqueeze(2).to_broadcast([P, E, NT + 1]),
                                          C["row_step"][:].unsqueeze(1).to_broadcast([P, E, NT + 1]), ALU.is_gt))
            after(nc.vector.tensor_reduce(n_blk[:], over[:], AX.X, ALU.add))
            after(nc.vector.tensor_tensor_scan(blk_end[:], C["ones"][:, 0:E], n_blk[:], 0.0, ALU.mult, ALU.add))
            after(nc.vector.tensor_tensor(row0[:], blk_end[:], n_blk[:], ALU.subtract))
            after(nc.vector.tensor_scalar(row0[:], row0[:], float(P), None, ALU.mult))
            after(nc.vector.tensor_tensor(S["before"][:], S["before"][:], row0[:].unsqueeze(1).to_broadcast([P, NT + 1, E]), ALU.add))
            for k in range(2):
                after(nc.vector.tensor_tensor(place[:, :, k, :], S["before"][:], S["hot"][:, :, k, :], ALU.mult))
            after(nc.vector.tensor_reduce(row_f[:], place[:], AX.X, ALU.add))
            nc.vector.tensor_copy(row_i[:], row_f[:]).then_inc(table_ready, 1)
            after(nc.vector.tensor_tensor(before_end[:], blk_end[0:1, :].unsqueeze(1).to_broadcast([1, MAXBLK, E]),
                                          C["block_no"][:].unsqueeze(2).to_broadcast([1, MAXBLK, E]), ALU.is_le))
            after(nc.vector.tensor_reduce(blk_f[:, 0:MAXBLK], before_end[:], AX.X, ALU.add))
            after(nc.vector.tensor_scalar(blk_f[:, 0:MAXBLK], blk_f[:, 0:MAXBLK], float(E - 1), None, ALU.min))
            after(nc.vector.tensor_scalar(blk_f[:, MAXBLK:], blk_end[0:1, E - 1:E], -2.0, None, ALU.add))
            nc.vector.tensor_copy(blk_i[:], blk_f[:]).then_inc(table_ready, 1)

            def gated(i):
                dve.wait_ge(silu_done, i + 1)
                wait(dve, hT_psum, i)
                nc.vector.tensor_tensor(hid[:], act_g[:], bank[1][:, :], ALU.mult).then_inc(hid_ready, 1)

            def unload_y(i):
                wait(dve, y_stored, i * 16)
                dve.wait_ge(down_used, i * 4 + 4)
                for n in range(2):
                    nc.vector.tensor_copy(yb[:, n * 512:(n + 1) * 512], bank[2 + n][:, :]).then_inc(y_done, 1)

            m = blocks_but_two(dve)
            gated(0)
            with dve.Fori(1, m + 1) as i:
                gated(i)
                unload_y(i - 1)
            gated(m + 1)
            unload_y(m)
            unload_y(m + 1)


def combine(nc, A, S, C):
    with ExitStack() as ctx:
        def sb(name, shape, dt=F32):
            return ctx.enter_context(nc.sbuf_tensor(name, shape, dt))

        def sem(name):
            return ctx.enter_context(nc.semaphore(name))

        B = 2
        yy = [sb(f"yy{j}", [P, 2, D]) for j in range(B)]
        h = [sb(f"hf{j}", [P, D]) for j in range(B)]
        junk, w = sb("junkf", [P, D]), sb("w_final", [P, D])
        st = sb("st_f", [P, 4])
        w_loaded = sem("wf_loaded")
        y_loaded = [sem(f"yf_loaded{j}") for j in range(B)]
        h_loaded = [sem(f"hf_loaded{j}") for j in range(B)]
        out_stored = [sem(f"out_stored{j}") for j in range(B)]
        part, summed, squared, rms, rinv, out_ready = (sem(n) for n in ("part", "summed", "squared", "rms", "rinv", "out_ready"))

        block = ctx.enter_context(nc.Block())

        @block.sync
        def _(sp):
            sp.dma_start(w[:], A["norm_final_w"][0].partition_broadcast(P)).then_inc(w_loaded, 16)

            def load(t, j, at):
                r = rows_of(t)
                wait(sp, out_stored[j], at)
                sp.dma_start(h[j][0:r, :], S["h"][bass.ds(t * P, r), :]).then_inc(h_loaded[j], 16)
                sp.dma_start(yy[j][0:r], S["picked"].rearrange("(t k) d -> t k d", k=2)[bass.ds(t * P, r)]).then_inc(y_loaded[j], 16)

            def store(t, j):
                r = rows_of(t)
                sp.wait_ge(out_ready, t + 1)
                dst = A["y_sample"] if r == TS else A["y_prompt"][bass.ds(t * P, r), :]
                sp.dma_start(dst, h[j][0:r, :]).then_inc(out_stored[j], 16)

            load(0, 0, 0)
            load(1, 1, 0)
            with sp.Fori(1, NT // 2) as a:
                for j in range(2):
                    store(a * 2 + (j - 2), j)
                    load(a * 2 + j, j, a * 16)
            store(NT - 2, 0)
            load(NT, 0, 16 * (NT // 2))
            store(NT - 1, 1)
            store(NT, 0)
            sp.wait_ge(out_stored[0], 16 * (NT // 2 + 1))
            sp.wait_ge(out_stored[1], 16 * (NT // 2))

        @block.scalar
        def _(act):
            def stats(t, j):
                r = rows_of(t)
                act.wait_ge(summed, t + 1)
                wait(act, out_ready, t)
                then_own(act, nc.scalar.activation(junk[0:r, :], h[j][0:r, :], ACT.Square, accum_out=st[0:r, 0:1]), squared, t + 1)
                nc.scalar.activation(st[0:r, 1:2], st[0:r, 0:1], ACT.Sqrt, bias=C["eps"][0:r, :], scale=1.0 / D).then_inc(rms, 1)

            stats(0, 0)
            stats(1, 1)
            with act.Fori(1, NT // 2) as a:
                stats(a * 2, 0)
                stats(a * 2 + 1, 1)
            stats(NT, 0)

        @block.vector
        def _(dve):
            def tile(t, j, a):
                r = rows_of(t)
                dve.wait_ge(y_loaded[j], a * 16 + 16)
                g = S["gate"]
                nc.vector.tensor_scalar(yy[j][0:r, 0, :], yy[j][0:r, 0, :], g[0:r, bass.ds(t, 1), 0:1].rearrange("p a b -> p (a b)"),
                                        None, ALU.mult).then_inc(part, 1)
                dve.wait_ge(part, t * 2 + 1)
                nc.vector.scalar_tensor_tensor(out=yy[j][0:r, 1, :], in0=yy[j][0:r, 1, :],
                                               scalar=g[0:r, bass.ds(t, 1), 1:2].rearrange("p a b -> p (a b)"),
                                               in1=yy[j][0:r, 0, :], op0=ALU.mult, op1=ALU.add).then_inc(part, 1)
                dve.wait_ge(part, t * 2 + 2)
                dve.wait_ge(h_loaded[j], a * 16 + 16)
                nc.vector.tensor_tensor(h[j][0:r, :], h[j][0:r, :], yy[j][0:r, 1, :], ALU.add).then_inc(summed, 1)
                dve.wait_ge(rms, t + 1)
                then_own(dve, nc.vector.reciprocal(st[0:r, 2:3], st[0:r, 1:2]), rinv, t + 1)
                nc.vector.scalar_tensor_tensor(out=h[j][0:r, :], in0=h[j][0:r, :], scalar=st[0:r, 2:3], in1=w[0:r, :],
                                               op0=ALU.mult, op1=ALU.mult).then_inc(out_ready, 1)

            dve.wait_ge(w_loaded, 16)
            tile(0, 0, 0)
            tile(1, 1, 0)
            with dve.Fori(1, NT // 2) as a:
                tile(a * 2, 0, a)
                tile(a * 2 + 1, 1, a)
            tile(NT, 0, NT // 2)


OUTPUTS = {
    "y_prompt": (SEQ, D), "y_sample": (TS, D), "conv_tail": (P, CT_N, DEC_B + 1, CONV_K - 1),
    "ssm_prompt": (NSTATE, D), "ssm_sample": (DEC_B, NSTATE, D), "sg_v_sample": (TS, D),
}
SCRATCH = {
    "z": (T, D), "xb": (T, D + GROUPS * NSTATE), "bct": (2 * GROUPS * NSTATE, T), "uT": (D, T), "v": (T, D),
    "h": (T, D), "hn": (T, D), "picked": (2 * T, D),
}


def program(nc, A, S):
    with ExitStack() as ctx:
        def sb(name, shape, dt=F32):
            return ctx.enter_context(nc.sbuf_tensor(name, shape, dt))

        C = {
            "ident": sb("ident", [P, P]), "eps": sb("eps", [P, 1]), "ones": sb("ones", [P, P]), "le": sb("le", [P, P]),
            "lt": sb("lt", [P, P]), "gt": sb("gt", [P, P]), "same": sb("same", [TS, TS]),
            "of_seq": sb("of_seq", [P, DEC_B, TS]), "repeat": sb("repeat", [DEC_S, TS]),
            "expert_no": sb("expert_no", [P, E]), "row_step": sb("row_step", [P, NT + 1]),
            "block_no": sb("block_no", [1, MAXBLK]), "token_slot": sb("token_slot", [P, NT + 1, 2, 2], I32),
            "const_made": ctx.enter_context(nc.semaphore("const_made")),
        }
        S["dtk"] = sb("dtk", [P, NT + 1, 2 * HEADS])
        bank = [ctx.enter_context(nc.psum_tensor(f"bank{b}", [P, 512], F32)) for b in range(8)]
        S["gate"] = sb("gate", [P, NT + 1, 2])
        S["hot"] = sb("hot", [P, NT + 1, 2, E])
        S["before"] = sb("before", [P, NT + 1, E])
        S["run"] = sb("run", [P, E])
        projections(nc, A, S, C, bank)
        with nc.sbuf_tensor("w_out", [P, 2 * KT, D], F32) as w_out:
            S["w_out"] = w_out
            mixer(nc, A, S, C, bank)
        experts(nc, A, S, C, bank)
        combine(nc, A, S, C)


def laid_out(np, x_prompt, x_sample, state_conv, state_ssm, norm_mix_w, w_in, conv_w, conv_b, dt_bias, a_log, d_skip,
             ssm_norm_w, sg_norm_w, sg_w, sg_b, w_out, norm_ffn_w, w_router_group, b_router_group, w_router_expert,
             b_router_expert, w_gate, w_up, w_down, norm_final_w):
    w = w_in[0]
    columns = np.concatenate([w[:, :COL_DT], w[:, COL_U:]], axis=1)
    return {
        "x_prompt": x_prompt, "x_sample": x_sample,
        "state_conv": state_conv[0].reshape(DEC_B, CONV_K - 1, CT_N, P).transpose(3, 2, 0, 1),
        "state_ssm": state_ssm[0].reshape(DEC_B, D, NSTATE).transpose(0, 2, 1),
        "norm_mix_w": norm_mix_w[0].reshape(KT, P).T,
        "w_in_tiles": columns.reshape(KT, P, M_END, P).transpose(2, 1, 0, 3),
        "w_dt": w[:, COL_DT:COL_U].reshape(KT, P, HEADS).transpose(1, 0, 2),
        "conv_w": conv_w[0].reshape(CONV_K, CT_N, P).transpose(2, 0, 1),
        "conv_b": conv_b[0].reshape(CT_N, P).T,
        "dt_bias": dt_bias.T, "a_log": a_log.T, "d_skip": d_skip, "ssm_norm_w": ssm_norm_w, "sg_norm_w": sg_norm_w,
        "sg_w": sg_w[0].transpose(2, 0, 1), "sg_b": sg_b,
        "w_out": w_out[0].reshape(2 * KT, P, D).transpose(1, 0, 2), "norm_ffn_w": norm_ffn_w,
        "w_router": np.concatenate([w_router_group[0], w_router_expert[0]], axis=1).reshape(KT, P, EG + E).transpose(1, 0, 2),
        "b_router": np.concatenate([b_router_group, b_router_expert], axis=1),
        "w_gate": w_gate[0], "w_up": w_up[0], "w_down": w_down[0], "norm_final_w": norm_final_w[None],
    }


def kernel(**inputs):
    import numpy as _np
    import concourse.bacc as _bacc
    from concourse import mybir as _mybir
    from concourse.bass_utils import run_bass_kernel_spmd as _run

    nc = _bacc.Bacc("TRN2", target_bir_lowering=False, num_devices=1)
    arrays, A = {}, {}
    for name, a in laid_out(_np, **inputs).items():
        arrays[f"in_{name}"] = _np.ascontiguousarray(a)
        A[name] = nc.dram_tensor(f"in_{name}", a.shape, _mybir.dt.from_np(a.dtype), kind="ExternalInput").ap()
    for name, shape in OUTPUTS.items():
        A[name] = nc.dram_tensor(f"out_{name}", shape, F32, kind="ExternalOutput").ap()
    S = {name: nc.dram_tensor(f"scratch_{name}", shape, F32, kind='Internal').ap() for name, shape in SCRATCH.items()}
    S["of_row"] = nc.dram_tensor("scratch_of_row", (MAXBLK * P, 2), I32, kind='Internal').ap()
    program(nc, A, S)
    r = _run(nc, [arrays], core_ids=[0])
    got = {name: r.results[0][f"out_{name}"] for name in OUTPUTS}
    tail = got["conv_tail"].transpose(2, 3, 1, 0).reshape(1, DEC_B + 1, CONV_K - 1, C_CONV)
    state = (GROUPS, HEADS // GROUPS, HD, NSTATE)
    return (got["y_prompt"].reshape(1, SEQ, D), got["y_sample"].reshape(DEC_B, DEC_S, D), tail[:, 0:1],
            got["ssm_prompt"].T.reshape(1, 1, *state), tail[:, 1:],
            got["ssm_sample"].transpose(0, 2, 1).reshape(1, DEC_B, *state),
            got["sg_v_sample"].reshape(1, DEC_B, DEC_S, D))
```

```python
from contextlib import ExitStack

import concourse.bass as bass
from concourse import mybir

ALU = mybir.AluOpType
ACT = mybir.ActivationFunctionType
AX = mybir.AxisListType
F32 = mybir.dt.float32
I32 = mybir.dt.int32
U32 = mybir.dt.uint32
F32R = mybir.dt.float32r

P = 128
D = 1024
KT = D // P
SEQ = 1024
DEC_B, DEC_S = 8, 4
TS = DEC_B * DEC_S
T = SEQ + TS
NT = SEQ // P
HEADS, HD, NSTATE, GROUPS = 16, 64, 128, 2
CONV_K = 4
C_CONV = D + 2 * GROUPS * NSTATE
SGH = 8
E, EG, EPG = 32, 4, 8
FF = D // 2
EPS = 1e-6
MAXBLK = -(-2 * T // P) + E
MINBLK = -(-2 * T // P)

COL_Z, COL_X, COL_DT, COL_U = 0, D, D + C_CONV, D + C_CONV + HEADS
M_X, M_B, M_C, M_U, M_V, M_END = 8, 16, 18, 20, 28, 36
NB3 = 3
TB = T // NB3
CT_N = M_U - M_X


def wait(eng, sem, value):
    if not (isinstance(value, int) and value <= 0):
        eng.wait_ge(sem, value)


def then_own(eng, ins, sem, value):
    ins.then_inc(sem, 1)
    eng.wait_ge(sem, value)


def rows_of(t):
    return TS if isinstance(t, int) and t == NT else P


def split_product(nc, acc, parts_l, parts_r, start, stop):
    (lh, ll), (rh, rl) = parts_l, parts_r
    nc.tensor.matmul(acc, lh, rh, start=start, stop=False)
    nc.tensor.matmul(acc, lh, rl, start=False, stop=False)
    return nc.tensor.matmul(acc, ll, rh, start=False, stop=stop)


def make_constants(nc, pool, C):
    made = [0]

    def done(ins):
        made[0] += 1
        ins.then_inc(C["const_made"], 1)

    def after(ins):
        done(ins)
        pool.wait_ge(C["const_made"], made[0])

    def select(t, pattern, base, mult, op=ALU.is_ge, fill=0.0):
        after(nc.gpsimd.affine_select(out=t, in_=t, compare_op=op, fill=fill, base=base, pattern=pattern,
                                      channel_multiplier=mult))

    after(nc.gpsimd.memset(C["ident"][:], 0.0))
    select(C["ident"][:], [[-1, P]], 0, 1, ALU.not_equal, 1.0)
    done(nc.gpsimd.memset(C["eps"][:], EPS))
    done(nc.gpsimd.memset(C["ones"][:], 1.0))
    for name, step, mult, op in (("le", 1, -1, ALU.is_ge), ("lt", 1, -1, ALU.is_gt), ("gt", -1, 1, ALU.is_gt)):
        after(nc.gpsimd.memset(C[name][:], 1.0))
        select(C[name][:], [[step, P]], 0, mult, op)
    after(nc.gpsimd.memset(C["same"][:], 1.0))
    v = C["same"][:].rearrange("p (b s) -> p b s", s=DEC_S)
    select(v, [[-DEC_S, DEC_B], [0, DEC_S]], 0, 1)
    select(v, [[DEC_S, DEC_B], [0, DEC_S]], DEC_S - 1, -1)
    after(nc.gpsimd.memset(C["of_seq"][:], 1.0))
    select(C["of_seq"][:], [[-DEC_S, DEC_B], [1, TS]], 0, 0)
    select(C["of_seq"][:], [[DEC_S, DEC_B], [-1, TS]], DEC_S - 1, 0)
    after(nc.gpsimd.memset(C["repeat"][:], 0.0))
    select(C["repeat"][:].rearrange("p (b s) -> p b s", s=DEC_S), [[0, DEC_B], [-1, DEC_S]], 0, 1, ALU.not_equal, 1.0)
    done(nc.gpsimd.iota(C["expert_no"][:], [[1, E]], base=0, channel_multiplier=0, allow_small_or_imprecise_dtypes=True))
    done(nc.gpsimd.iota(C["row_step"][:], [[P, NT + 1]], base=0, channel_multiplier=0, allow_small_or_imprecise_dtypes=True))
    done(nc.gpsimd.iota(C["block_no"][:], [[1, MAXBLK]], base=0, channel_multiplier=0, allow_small_or_imprecise_dtypes=True))
    done(nc.gpsimd.iota(C["block_row"][:], [[P, MAXBLK + 1]], base=0, channel_multiplier=0, allow_small_or_imprecise_dtypes=True))
    done(nc.gpsimd.iota(C["column_no"][:], [[1, P]], base=0, channel_multiplier=0, allow_small_or_imprecise_dtypes=True))
    for o, pattern in enumerate(([[P, NT + 1], [0, 2]], [[2 * P, NT + 1], [1, 2]])):
        done(nc.gpsimd.iota(C["token_slot"][:, :, o].rearrange("p (t k) -> p t k", k=2), pattern, base=-(1 + o) * T,
                            channel_multiplier=1 + o, allow_small_or_imprecise_dtypes=True))
    assert made[0] == N_CONST


N_CONST = 25


def projections(nc, A, S, C, bank):
    with ExitStack() as ctx:
        def sb(name, shape, dt=F32):
            return ctx.enter_context(nc.sbuf_tensor(name, shape, dt))

        def sem(name):
            return ctx.enter_context(nc.semaphore(name))

        work = sb("work", [P, 6 * T])
        xin = [work[:, j * D:(j + 1) * D] for j in range(2)]
        xn = [work[:, (2 + j) * D:(3 + j) * D] for j in range(2)]
        xsq = work[:, 4 * D:5 * D]
        x32 = [work[:, 5 * D + j * 512:5 * D + (j + 1) * 512].rearrange("p (k t) -> p k t", k=4) for j in range(2)]
        dtw = work[0:HEADS, :].rearrange("p (a t) -> p a t", a=6)
        stat = [sb(f"stat{j}", [P, 4]) for j in range(2)]
        xh, xl = sb("xh", [P, KT, T], F32R), sb("xl", [P, KT, T], F32R)
        w = [sb(f"w{j}", [P, KT, P]) for j in range(2)]
        wh = [sb(f"wh{j}", [P, KT, P], F32R) for j in range(2)]
        wl = [sb(f"wl{j}", [P, KT, P], F32R) for j in range(2)]
        feat = [sb(f"feat{j}", [P, T]) for j in range(2)]
        raw = [sb(f"raw{j}", [P, 3 + SEQ + 1 + DEC_B * 7]) for j in range(2)]
        conv = [sb(f"conv{j}", [P, T]) for j in range(2)]
        stage = [sb(f"stage{j}", [P, NT + 1, P]) for j in range(2)]
        old_conv = sb("old_conv", [P, CT_N, DEC_B, CONV_K - 1])
        tail = sb("tail", [P, CT_N, DEC_B + 1, CONV_K - 1])
        w_dt = sb("w_dt", [P, KT, HEADS])
        w_dt_h, w_dt_l = sb("w_dt_h", [P, KT, HEADS], F32R), sb("w_dt_l", [P, KT, HEADS], F32R)
        nmw = sb("nmw", [P, KT])
        cw = sb("cw", [P, CONV_K, CT_N])
        cb = sb("cb", [P, CT_N])
        hcol = sb("hcol", [HEADS, 4])

        prompt_raw = [raw[j][:, 0:3 + SEQ] for j in range(2)]
        sample_raw = [raw[j][:, 4 + SEQ:4 + SEQ + DEC_B * 7].rearrange("p (b s) -> p b s", s=7) for j in range(2)]

        setup_loaded, nmw_loaded = sem("setup_loaded"), sem("nmw_loaded")
        x_loaded = [sem(f"x_loaded{j}") for j in range(2)]
        x_squared, x_rms, x_rinv, x_normed = sem("x_squared"), sem("x_rms"), sem("x_rinv"), sem("x_normed")
        xT_psum, x_scaled, x_high, xT_done = sem("xT_psum"), sem("x_scaled"), sem("x_high"), sem("xT_done")
        w_high, w_split, w_dt_high, w_dt_split = sem("w_high"), sem("w_split"), sem("w_dt_high"), sem("w_dt_split")
        w_loaded = [sem(f"w_loaded{j}") for j in range(2)]
        acc_ready, acc_free = sem("acc_ready"), sem("acc_free")
        feat_ready = sem("feat_ready")
        feat_stored = [sem(f"feat_stored{j}") for j in range(2)]
        tr_psum, tr_free, stage_ready = sem("tr_psum"), sem("tr_free"), sem("stage_ready")
        stage_stored = [sem(f"stage_stored{j}") for j in range(2)]
        old_placed = sem("old_placed")
        raw_ready, conv_chain, conv_done, conv_used = sem("raw_ready"), sem("conv_chain"), sem("conv_done"), sem("conv_used")
        tail_ready, tail_stored = sem("tail_ready"), sem("tail_stored")
        dt_act, dt_chain, dt_ready, dt_psum, dt_done = sem("dt_act"), sem("dt_chain"), sem("dt_ready"), sem("dt_psum"), sem("dt_done")
        pad_zero = sem("pad_zero")

        xp = A["x_prompt"][0]
        xs = A["x_sample"].rearrange("b s d -> (b s) d")
        N_SETUP = 6

        block = ctx.enter_context(nc.Block())

        @block.sync
        def _(sp):
            def load_w(m, j):
                sp.dma_start(w[j][:], A["w_in_tiles"][bass.ds(m, 1)].rearrange("m p k c -> (m p) k c")).then_inc(w_loaded[j], 16)

            def load_x(t, j):
                r = rows_of(t)
                src = xs if r == TS else xp[bass.ds(t * P, P), :]
                sp.dma_start(xin[j][0:r, :], src).then_inc(x_loaded[j], 16)

            load_x(0, 0)
            load_x(1, 1)
            sp.dma_start(nmw[:], A["norm_mix_w"]).then_inc(nmw_loaded, 16)
            load_w(0, 0)
            load_w(1, 1)
            for dst, name in ((cw, "conv_w"), (cb, "conv_b"), (old_conv, "state_conv"), (w_dt, "w_dt")):
                sp.dma_start(dst[:], A[name]).then_inc(setup_loaded, 16)
            sp.dma_start(hcol[:, 0:1], A["dt_bias"]).then_inc(setup_loaded, 16)
            sp.dma_start(hcol[:, 1:2], A["a_log"]).then_inc(setup_loaded, 16)

            with sp.Fori(1, NT // 2) as a:
                for j in range(2):
                    t = a * 2 + j
                    sp.wait_ge(x_normed, a * 2 + (j - 1))
                    load_x(t, j)
            sp.wait_ge(x_normed, NT - 1)
            load_x(NT, 0)

            with sp.Fori(1, M_END // 2) as a:
                for j in range(2):
                    sp.wait_ge(w_split, a * 2 + (j - 1))
                    load_w(a * 2 + j, j)
            sp.dma_start(S["w_out_sg"][:], A["w_out"][:, KT:, :]).then_inc(S["w_out_loaded"], 16)

        @block.tensor
        def _(pe):
            def turn_x(t, j):
                r = rows_of(t)
                pe.wait_ge(x_normed, t + 1)
                for h in range(2):
                    wait(pe, x_scaled, t * 2 + (h - 1))
                    for q in range(4):
                        k = 4 * h + q
                        last = nc.tensor.transpose(bank[6 + h][:, q * P:q * P + r], xn[j][0:r, k * P:(k + 1) * P],
                                                   C["ident"][0:r, 0:r])
                    last.then_inc(xT_psum, 1)

            def products(n, m, j):
                pe.wait_ge(w_split, m + 1)
                for b in range(NB3):
                    wait(pe, acc_free, n * 3 + (b - 2))
                    cols = slice(b * TB, (b + 1) * TB)
                    for k in range(KT):
                        last = split_product(nc, bank[b][:, 0:TB], (wh[j][:, k, :], wl[j][:, k, :]), (xh[:, k, cols], xl[:, k, cols]),
                                             start=(k == 0), stop=(k == KT - 1))
                    last.then_inc(acc_ready, 1)

            def turn(q, m, j):
                pe.wait_ge(feat_ready, m + 1)
                for g in range(3):
                    wait(pe, tr_free, q * 3 + (g - 2))
                    for s in range(4 if g < 2 else 1):
                        t = 4 * g + s
                        r = P if t < NT else TS
                        last = nc.tensor.transpose(bank[3 + g][0:r, s * P:(s + 1) * P], feat[j][:, t * P:t * P + r],
                                                   C["ident"][:])
                    last.then_inc(tr_psum, 1)

            pe.wait_ge(C["const_made"], N_CONST)
            turn_x(0, 0)
            turn_x(1, 1)
            with pe.Fori(1, NT // 2) as a:
                turn_x(a * 2, 0)
                turn_x(a * 2 + 1, 1)
            turn_x(NT, 0)
            pe.wait_ge(xT_done, 2 * (NT + 1))
            products(0, 0, 0)
            products(1, 1, 1)
            turn(0, 0, 0)
            products(2, 2, 0)
            turn(1, 1, 1)
            with pe.Fori(1, M_C // 2) as a:
                products(a * 2 + 1, a * 2 + 1, 1)
                turn(a * 2, a * 2, 0)
                products(a * 2 + 2, a * 2 + 2, 0)
                turn(a * 2 + 1, a * 2 + 1, 1)
            products(M_C + 1, M_C + 1, 1)
            pe.wait_ge(w_dt_split, 1)
            for b in range(NB3):
                pe.wait_ge(acc_free, 3 * M_U + b - 2)
                cols = slice(b * TB, (b + 1) * TB)
                for k in range(KT):
                    last = split_product(nc, bank[b][0:HEADS, 0:TB], (w_dt_h[:, k, :], w_dt_l[:, k, :]),
                                         (xh[:, k, cols], xl[:, k, cols]), start=(k == 0), stop=(k == KT - 1))
                last.then_inc(acc_ready, 1)
            with pe.Fori(M_U // 2, M_V // 2) as a:
                products(a * 2 + 1, a * 2, 0)
                products(a * 2 + 2, a * 2 + 1, 1)
            products(M_V + 1, M_V, 0)
            pe.wait_ge(dt_ready, 1)
            for t in range(NT + 1):
                r = P if t < NT else TS
                nc.tensor.transpose(bank[6][0:r, 32 * t:32 * t + 16], dtw[:, 4, t * P:t * P + r], C["ident"][0:16, 0:16])
                last = nc.tensor.transpose(bank[6][0:r, 32 * t + 16:32 * t + 32], dtw[:, 5, t * P:t * P + r],
                                           C["ident"][0:16, 0:16])
            last.then_inc(dt_psum, 1)
            with pe.Fori(M_V // 2, M_END // 2 - 1) as a:
                products(a * 2 + 2, a * 2 + 1, 1)
                turn(a * 2 - (M_V - M_C), a * 2, 0)
                products(a * 2 + 3, a * 2 + 2, 0)
                turn(a * 2 + (1 - M_V + M_C), a * 2 + 1, 1)
            products(M_END, M_END - 1, 1)
            turn(M_END - 2 - (M_V - M_C), M_END - 2, 0)
            turn(M_END - 1 - (M_V - M_C), M_END - 1, 1)

        @block.scalar
        def _(act):
            def norm_stats(t, j, at):
                r = rows_of(t)
                act.wait_ge(x_loaded[j], at)
                wait(act, x_normed, t - 1)
                then_own(act, nc.scalar.activation(xsq[0:r, :], xin[j][0:r, :], ACT.Square, accum_out=stat[j][0:r, 0:1]),
                         x_squared, t + 1)
                nc.scalar.activation(stat[j][0:r, 1:2], stat[j][0:r, 0:1], ACT.Sqrt, bias=C["eps"][0:r, :],
                                     scale=1.0 / D).then_inc(x_rms, 1)

            act.wait_ge(C["const_made"], N_CONST)
            def high_x(t):
                r = rows_of(t)
                for h in range(2):
                    act.wait_ge(x_scaled, t * 2 + (h + 1))
                    nc.scalar.copy(xh[:, 4 * h:4 * h + 4, bass.ds(t * P, r)], x32[h][:, :, 0:r]).then_inc(x_high, 1)

            def high_w(j, at):
                act.wait_ge(w_loaded[j], at)
                nc.scalar.copy(wh[j][:], w[j][:]).then_inc(w_high, 1)

            norm_stats(0, 0, 16)
            norm_stats(1, 1, 16)
            high_w(0, 16)
            high_w(1, 16)
            with act.Fori(0, NT // 2 - 1) as a:
                high_x(a * 2)
                norm_stats(a * 2 + 2, 0, a * 16 + 32)
                high_x(a * 2 + 1)
                norm_stats(a * 2 + 3, 1, a * 16 + 32)
            high_x(NT - 2)
            norm_stats(NT, 0, 16 * (NT // 2 + 1))
            high_x(NT - 1)
            high_x(NT)

            def activate(n, m, j, func):
                for b in range(NB3):
                    act.wait_ge(acc_ready, n * 3 + (b + 1))
                    ins = nc.scalar.activation(feat[j][:, b * TB:(b + 1) * TB], bank[b][:, 0:TB], func)
                    ins.then_inc(acc_free, 1)
                act.wait_ge(acc_free, n * 3 + 3)
                nc.scalar.sem_inc(feat_ready, 1)

            def to_conv(m, j, at):
                for b in range(NB3):
                    act.wait_ge(acc_ready, m * 3 + (b + 1))
                    if b < 2:
                        nc.scalar.copy(raw[j][:, 3 + b * TB:3 + (b + 1) * TB], bank[b][:, 0:TB]).then_inc(acc_free, 1)
                    else:
                        nc.scalar.copy(raw[j][:, 3 + 2 * TB:3 + SEQ], bank[b][:, 0:SEQ - 2 * TB]).then_inc(raw_ready, 1)
                        nc.scalar.copy(sample_raw[j][:, :, 3:7],
                                       bank[b][:, SEQ - 2 * TB:TB].rearrange("p (b s) -> p b s", s=DEC_S)).then_inc(acc_free, 1)
                high_w(j, at)
                act.wait_ge(conv_done, m - (M_X - 1))

            def silu_conv(m, j):
                nc.scalar.activation(feat[j][:], conv[j][:], ACT.Silu, bias=cb[:, bass.ds(m - M_X, 1)]).then_inc(feat_ready, 1)

            for m in (0, 1):
                activate(m, m, m, ACT.Silu)
                high_w(m, 32)
            with act.Fori(1, M_X // 2) as a:
                for j in range(2):
                    act.wait_ge(tr_psum, a * 6 + (3 * j - 3))
                    activate(a * 2 + j, a * 2 + j, j, ACT.Silu)
                    high_w(j, a * 16 + 32)
            act.wait_ge(setup_loaded, 16 * N_SETUP)
            nc.scalar.copy(w_dt_h[:], w_dt[:]).then_inc(w_dt_high, 1)
            for c in (0, 1):
                m = M_X + c
                to_conv(m, c, 16 * (M_X // 2 + 2))
                act.wait_ge(tr_psum, 3 * (m - 1))
                silu_conv(m, c)
            with act.Fori(M_X // 2 + 1, M_C // 2) as a:
                for j in range(2):
                    act.wait_ge(conv_done, a * 2 + (j - M_X - 1))
                    act.wait_ge(tail_ready, a * 4 + 2 * (j - M_X - 1))
                    to_conv(a * 2 + j, j, a * 16 + 32)
                    act.wait_ge(tr_psum, a * 6 + (3 * j - 3))
                    silu_conv(a * 2 + j, j)
            for m in (M_C, M_C + 1):
                act.wait_ge(conv_done, m - M_X - 1)
                act.wait_ge(tail_ready, 2 * (m - M_X - 1))
                to_conv(m, m % 2, 16 * (M_C // 2 + 2))
                act.wait_ge(tr_psum, 3 * (m - 1))
                act.wait_ge(feat_stored[m % 2], 16)
                silu_conv(m, m % 2)
            for b in range(NB3):
                act.wait_ge(acc_ready, 3 * M_U + b + 1)
                s = slice(b * TB, (b + 1) * TB)
                nc.scalar.activation(dtw[:, 0, s], bank[b][0:HEADS, 0:TB], ACT.Abs, bias=hcol[:, 0:1]).then_inc(dt_act, 1)
                nc.scalar.activation(dtw[:, 1, s], bank[b][0:HEADS, 0:TB], ACT.Relu, bias=hcol[:, 0:1]).then_inc(acc_free, 1)
            act.wait_ge(dt_act, NB3)
            then_own(act, nc.scalar.activation(dtw[:, 2, :], dtw[:, 0, :], ACT.Exp, scale=-1.0), dt_act, NB3 + 1)
            nc.scalar.activation(dtw[:, 3, :], dtw[:, 2, :], ACT.Ln, bias=1.0).then_inc(dt_act, 1)
            nc.scalar.activation(hcol[:, 2:3], hcol[:, 1:2], ACT.Exp).then_inc(dt_act, 1)
            with act.Fori(M_U // 2, M_V // 2) as a:
                for j in range(2):
                    act.wait_ge(feat_stored[j], a * 16 - 16 * (M_U // 2 - 2))
                    activate(a * 2 + (j + 1), a * 2 + j, j, ACT.Gelu)
                    high_w(j, a * 16 + 32)
            for m in (M_V, M_V + 1):
                act.wait_ge(feat_stored[m % 2], 16 * ((M_V - M_B) // 2))
                activate(m + 1, m, m % 2, ACT.Gelu)
                high_w(m % 2, 16 * (M_V // 2 + 2))
            with act.Fori(M_V // 2 + 1, M_END // 2 - 1) as a:
                for j in range(2):
                    act.wait_ge(tr_psum, a * 6 + (3 * (j - 1) - 3 * (M_V - M_C)))
                    activate(a * 2 + (j + 1), a * 2 + j, j, ACT.Gelu)
                    high_w(j, a * 16 + 32)
            for m in (M_END - 2, M_END - 1):
                act.wait_ge(tr_psum, 3 * (m - 1 - (M_V - M_C)))
                activate(m + 1, m, m % 2, ACT.Gelu)

        @block.vector
        def _(dve):
            for j in range(2):
                nc.vector.memset(raw[j][:, 0:3], 0.0).then_inc(pad_zero, 1)

            def normalise(t, j):
                r = rows_of(t)
                dve.wait_ge(x_rms, t + 1)
                then_own(dve, nc.vector.reciprocal(stat[j][0:r, 2:3], stat[j][0:r, 1:2]), x_rinv, t + 1)
                nc.vector.tensor_scalar(xn[j][0:r, :], xin[j][0:r, :], stat[j][0:r, 2:3], None, ALU.mult).then_inc(x_normed, 1)

            def scale_xT(t):
                r = rows_of(t)
                for h in range(2):
                    dve.wait_ge(xT_psum, t * 2 + (h + 1))
                    wait(dve, xT_done, t * 2 + (h - 1))
                    nc.vector.tensor_tensor(
                        x32[h][:, :, 0:r],
                        bank[6 + h][:].rearrange("p (k t) -> p k t", k=4)[:, :, 0:r],
                        nmw[:, 4 * h:4 * h + 4].unsqueeze(2).to_broadcast([P, 4, r]), ALU.mult).then_inc(x_scaled, 1)

            normalise(0, 0)
            dve.wait_ge(nmw_loaded, 16)
            normalise(1, 1)
            scale_xT(0)
            normalise(2, 0)
            scale_xT(1)
            with dve.Fori(1, NT // 2 - 1) as a:
                normalise(a * 2 + 1, 1)
                scale_xT(a * 2)
                normalise(a * 2 + 2, 0)
                scale_xT(a * 2 + 1)
            normalise(NT - 1, 1)
            scale_xT(NT - 2)
            normalise(NT, 0)
            scale_xT(NT - 1)
            scale_xT(NT)

            def unload(q, j):
                for g in range(3):
                    dve.wait_ge(tr_psum, q * 3 + (g + 1))
                    if g < 2:
                        ins = nc.vector.tensor_copy(stage[j][:, 4 * g:4 * g + 4, :],
                                                    bank[3 + g][:].rearrange("p (t c) -> p t c", t=4))
                    else:
                        ins = nc.vector.tensor_copy(stage[j][0:TS, NT, :], bank[5][0:TS, 0:P])
                    ins.then_inc(tr_free, 1)
                dve.wait_ge(tr_free, q * 3 + 3)
                nc.vector.sem_inc(stage_ready, 1)

            def convolve(c, j):
                then_own(dve, nc.vector.tensor_copy(sample_raw[j][:, :, 0:3],
                                                    old_conv[:, bass.ds(c, 1)].rearrange("p c b k -> p (c b) k")),
                         old_placed, c + 1)
                dve.wait_ge(raw_ready, c + 1)
                dve.wait_ge(acc_free, c * 3 + (3 * M_X + 3))
                wait(dve, feat_ready, c + (M_X - 1))
                outs = (conv[j][:, 0:SEQ], conv[j][:, SEQ:T].rearrange("p (b s) -> p b s", s=DEC_S))
                for k in range(CONV_K):
                    ins = (prompt_raw[j][:, k:k + SEQ], sample_raw[j][:, :, k:k + DEC_S])
                    for part in range(2):
                        tap = cw[:, k, bass.ds(c, 1)]
                        if k == 0:
                            i = nc.vector.tensor_scalar(outs[part], ins[part], tap, None, ALU.mult)
                        else:
                            dve.wait_ge(conv_chain, c * 6 + (2 * (k - 1) + part + 1))
                            i = nc.vector.scalar_tensor_tensor(out=outs[part], in0=ins[part], scalar=tap, in1=outs[part],
                                                               op0=ALU.mult, op1=ALU.add)
                        if k < CONV_K - 1:
                            i.then_inc(conv_chain, 1)
                        elif part == 1:
                            i.then_inc(conv_done, 1)
                nc.vector.tensor_copy(tail[:, bass.ds(c, 1), 0, :], prompt_raw[j][:, SEQ:SEQ + 3].unsqueeze(1)).then_inc(tail_ready, 1)
                nc.vector.tensor_copy(tail[:, bass.ds(c, 1), 1:, :].rearrange("p c b k -> p (c b) k"),
                                      sample_raw[j][:, :, 4:7]).then_inc(tail_ready, 1)

            unload(0, 0)
            unload(1, 1)
            with dve.Fori(1, M_X // 2) as a:
                for j in range(2):
                    dve.wait_ge(stage_stored[j], a * 32)
                    unload(a * 2 + j, j)
            dve.wait_ge(pad_zero, 2)
            dve.wait_ge(setup_loaded, 16 * N_SETUP)
            for c in (0, 1):
                convolve(c, c)
                dve.wait_ge(stage_stored[c], 32 * (M_X // 2))
                unload(M_X + c, c)
            with dve.Fori(M_X // 2 + 1, M_C // 2) as a:
                for j in range(2):
                    convolve(a * 2 + (j - M_X), j)
                    dve.wait_ge(stage_stored[j], a * 32)
                    unload(a * 2 + j, j)
            for m in (M_C, M_C + 1):
                convolve(m - M_X, m % 2)
            dve.wait_ge(dt_act, NB3 + 3)
            dve.wait_ge(acc_free, 3 * M_U + 3)
            link = [0]

            def chained(ins):
                link[0] += 1
                then_own(dve, ins, dt_chain, link[0])

            chained(nc.vector.tensor_scalar(dtw[:, 4, :], dtw[:, 2, :], 1.0, -1.0, ALU.add, ALU.add))
            chained(nc.vector.tensor_scalar(dtw[:, 5, :], dtw[:, 4, :], 0.0, None, ALU.is_equal))
            chained(nc.vector.tensor_tensor(dtw[:, 4, :], dtw[:, 4, :], dtw[:, 5, :], ALU.add))
            chained(nc.vector.tensor_tensor(dtw[:, 3, :], dtw[:, 3, :], dtw[:, 5, :], ALU.add))
            chained(nc.vector.tensor_tensor(dtw[:, 3, :], dtw[:, 3, :], dtw[:, 2, :], ALU.mult))
            chained(nc.vector.reciprocal(dtw[:, 4, :], dtw[:, 4, :]))
            chained(nc.vector.tensor_tensor(dtw[:, 3, :], dtw[:, 3, :], dtw[:, 4, :], ALU.mult))
            chained(nc.vector.tensor_tensor(dtw[:, 4, :], dtw[:, 3, :], dtw[:, 1, :], ALU.add))
            nc.vector.tensor_scalar(dtw[:, 5, :], dtw[:, 4, :], hcol[:, 2:3], -1.0, ALU.mult, ALU.mult).then_inc(dt_ready, 1)
            dve.wait_ge(dt_psum, 1)
            nc.vector.tensor_copy(S["dtk"][:, 0:NT, :], bank[6][:, 0:32 * NT].rearrange("p (t c) -> p t c", t=NT)).then_inc(dt_done, 1)
            nc.vector.tensor_copy(S["dtk"][0:TS, NT, :], bank[6][0:TS, 32 * NT:32 * NT + 32]).then_inc(dt_done, 1)
            with dve.Fori(M_C // 2, M_C // 2 + (M_END - M_V) // 2) as a:
                for j in range(2):
                    dve.wait_ge(stage_stored[j], a * 32)
                    unload(a * 2 + j, j)
            dve.wait_ge(dt_done, 2)

        @block.gpsimd
        def _(pool):
            def store_turned(q, j, dst, col):
                pool.wait_ge(stage_ready, q + 1)
                pool.dma_start(dst[0:SEQ, bass.ds(col, P)].rearrange("(t p) c -> p t c", p=P),
                               stage[j][:, 0:NT, :]).then_inc(stage_stored[j], 16)
                pool.dma_start(dst[SEQ:T, bass.ds(col, P)], stage[j][0:TS, NT, :]).then_inc(stage_stored[j], 16)

            def store_feat(m, j, dst, row):
                pool.wait_ge(feat_ready, m + 1)
                pool.dma_start(dst[bass.ds(row, P), :], feat[j][:]).then_inc(feat_stored[j], 16)

            def low_w(m, j):
                pool.wait_ge(w_high, m + 1)
                nc.gpsimd.tensor_tensor(wl[j][:], w[j][:], wh[j][:].bitcast(F32), ALU.subtract).then_inc(w_split, 1)

            def low_x(t):
                r = rows_of(t)
                for h in range(2):
                    pool.wait_ge(x_high, t * 2 + (h + 1))
                    at = (slice(None), slice(4 * h, 4 * h + 4), bass.ds(t * P, r))
                    nc.gpsimd.tensor_tensor(xl[at], x32[h][:, :, 0:r], xh[at].bitcast(F32), ALU.subtract).then_inc(xT_done, 1)

            make_constants(nc, pool, C)
            low_w(0, 0)
            low_w(1, 1)
            with pool.Fori(0, NT) as t:
                low_x(t)
            low_x(NT)
            with pool.Fori(0, M_X // 2) as a:
                for j in range(2):
                    low_w(a * 2 + (j + 2), j)
                    store_turned(a * 2 + j, j, S["z"], a * (2 * P) + j * P)
            pool.wait_ge(w_dt_high, 1)
            nc.gpsimd.tensor_tensor(w_dt_l[:], w_dt[:], w_dt_h[:].bitcast(F32), ALU.subtract).then_inc(w_dt_split, 1)
            with pool.Fori(M_X // 2, M_B // 2) as a:
                for j in range(2):
                    low_w(a * 2 + (j + 2), j)
                    store_turned(a * 2 + j, j, S["xb"], a * (2 * P) + (j - M_X) * P)
            for m in (M_B, M_B + 1):
                low_w(m + 2, m % 2)
                store_feat(m, m % 2, S["bct"], (m - M_B) * P)
                store_turned(m, m % 2, S["xb"], (m - M_X) * P)
            for m in (M_C, M_C + 1):
                low_w(m + 2, m % 2)
                store_feat(m, m % 2, S["bct"], (m - M_B) * P)
            pool.wait_ge(tail_ready, 2 * CT_N)
            pool.dma_start(A["conv_tail"], tail[:]).then_inc(tail_stored, 16)
            with pool.Fori(M_U // 2, M_V // 2) as a:
                for j in range(2):
                    low_w(a * 2 + (j + 2), j)
                    store_feat(a * 2 + j, j, S["uT"], a * (2 * P) + (j - M_U) * P)
            with pool.Fori(M_V // 2, M_END // 2 - 1) as a:
                for j in range(2):
                    low_w(a * 2 + (j + 2), j)
                    store_turned(a * 2 + (j + M_C - M_V), j, S["v"], a * (2 * P) + (j - M_V) * P)
            for m in (M_END - 2, M_END - 1):
                store_turned(m + M_C - M_V, m % 2, S["v"], (m - M_V) * P)
            for j in range(2):
                pool.wait_ge(feat_stored[j], 16 * ((M_V - M_B) // 2))
                pool.wait_ge(stage_stored[j], 32 * ((M_C + M_END - M_V) // 2))
            pool.wait_ge(tail_stored, 16)


def held(eng, value):
    return value if isinstance(value, int) else eng.snap(value)


class Links:

    def __init__(self, eng, sem, per):
        self.eng, self.sem, self.per, self.base, self.k = eng, sem, per, 0, 0

    def begin(self, tile):
        self.base, self.k = tile * self.per, 0

    def __call__(self, ins):
        self.k += 1
        assert self.k <= self.per or (isinstance(self.base, int) and self.base == self.per * NT)
        ins.then_inc(self.sem, 1)
        self.eng.wait_ge(self.sem, self.base + self.k)

    def settle(self):
        self.k += 1
        self.eng.sem_inc(self.sem, 1)


def mixer(nc, A, S, C, bank):
    with ExitStack() as ctx:
        def sb(name, shape, dt=F32):
            return ctx.enter_context(nc.sbuf_tensor(name, shape, dt))

        def sem(name):
            return ctx.enter_context(nc.semaphore(name))

        w_out_sg = S["w_out_sg"]
        w_out_ssm = sb("w_out_ssm", [P, KT, D])
        xb = sb("xb", [P, D + GROUPS * NSTATE])
        bct = sb("bct", [P, 2 * GROUPS, P])
        uT = sb("uT_t", [P, SGH, P])
        v = sb("v_t", [P, D])
        z = sb("z_t", [P, D])
        x = sb("x_t", [P, D])
        seg_lhs = sb("seg_lhs", [P, HEADS, P])
        M = sb("M", [P, HEADS, P])
        cbm = sb("cbm", [P, GROUPS, P])
        decay = sb("decay", [P, 3, HEADS])
        xdt = sb("xdt", [P, D])
        xdtE = sb("xdtE", [P, D])
        xD = sb("xD", [P, D])
        y = sb("y", [P, D])
        yT = sb("yT", [P, KT, P])
        ysgT = sb("ysgT", [P, SGH, P])
        state = sb("state", [P, D])
        h = sb("h_t", [P, D])
        hn = sb("hn_t", [P, D])
        hnT = sb("hnT", [P, KT, P])
        junk = sb("junk", [P, D])
        ssm_w, sg_w_row, ffn_w = sb("ssm_w", [P, D]), sb("sg_w_row", [P, D]), sb("ffn_w", [P, D])
        sgWT = sb("sgWT", [P, SGH, P])
        sgWT_s = sb("sgWT_s", [TS, SGH, TS])
        sgb = sb("sgb", [P, SGH, P])
        d_skip = sb("d_skip", [P, HEADS])
        w_router = sb("w_router", [P, KT, EG + E])
        b_router = sb("b_router", [P, EG + E])
        st_v, st_h = sb("st_v", [P, 4]), sb("st_h", [P, 4])
        st_y = sb("st_y", [P, 6])
        lg = sb("lg", [P, EG + E])
        r8 = sb("r8", [P, 8, 8])
        idx = sb("idx", [P, 2, 8], U32)
        pick = sb("pick", [P, EG, EPG])
        chosen = sb("chosen", [P, E])
        run = S["run"]
        le_s, gt_s = sb("le_s", [TS, TS]), sb("gt_s", [TS, TS])
        dta_s = sb("dta_s", [TS, DEC_B, HEADS])
        decay_s = sb("decay_s", [P, DEC_B, HEADS])
        c_of = [sb(f"c_of{j}", [P, GROUPS, TS]) for j in range(2)]
        b_of = [sb(f"b_of{j}", [TS, GROUPS * NSTATE]) for j in range(2)]
        old = [sb(f"old{j}", [P, D]) for j in range(2)]

        consts_loaded, consts_done = sem("consts_loaded"), sem("consts_done")
        later_loaded, w_out_ssm_loaded = sem("later_loaded"), sem("w_out_ssm_loaded")
        xb_loaded, bct_loaded, u_loaded = sem("xb_loaded"), sem("bct_loaded"), sem("u_loaded")
        v_loaded, z_loaded, xr_loaded = sem("v_loaded"), sem("z_loaded"), sem("xr_loaded")
        cb_psum, cbm_ready, decay_ready = sem("cb_psum"), sem("cbm_ready"), sem("decay_ready")
        seg_ready, seg_psum, seg_exp, m_ready = sem("seg_ready"), sem("seg_psum"), sem("seg_exp"), sem("m_ready")
        xdt_ready, xdtE_ready, xD_ready = sem("xdt_ready"), sem("xdtE_ready"), sem("xD_ready")
        vn_ready, sg_psum, sg_sum, sg_ready = sem("vn_ready"), sem("sg_psum"), sem("sg_sum"), sem("sg_ready")
        yd_psum, st_psum, yo_psum = sem("yd_psum"), sem("st_psum"), sem("yo_psum")
        yo_used, yd_used, gated, yn_ready = sem("yo_used"), sem("yd_used"), sem("gated"), sem("yn_ready")
        state_ready = sem("state_ready")
        yT_psum, yT_done = sem("yT_psum"), sem("yT_done")
        sgproj_done, mix_psum, h_ready, hn_ready = sem("sgproj_done"), sem("mix_psum"), sem("h_ready"), sem("hn_ready")
        h_stored, hn_stored = sem("h_stored"), sem("hn_stored")
        hnT_psum, hnT_done, logits_psum = sem("hnT_psum"), sem("hnT_done"), sem("logits_psum")
        assigned, count_psum, counted = sem("assigned"), sem("count_psum"), sem("counted")
        v_sq, v_rms, y_sq, y_rms, h_sq, h_rms = (sem(n) for n in ("v_sq", "v_rms", "y_sq", "y_rms", "h_sq", "h_rms"))
        link1, link2, link3 = sem("link1"), sem("link2"), sem("link3")
        shifted, exped = sem("shifted"), sem("exped")
        old_loaded = [sem(f"old_loaded{j}") for j in range(2)]
        old_stored = [sem(f"old_stored{j}") for j in range(2)]
        of_ready, of_used, new_psum, new_ready = sem("of_ready"), sem("of_used"), sem("new_psum"), sem("new_ready")
        final_stored = sem("final_stored")
        rep_psum = sem("rep_psum")
        addressing = C["holder"]

        dtk = S["dtk"]
        N_CONSTS = 7

        def heads(t, r):
            return t[0:r, 0:D].rearrange("p (h d) -> p h d", d=HD)

        block = ctx.enter_context(nc.Block())

        @block.sync
        def _(sp):
            for dst, src in ((sg_w_row, A["sg_norm_w"][0].partition_broadcast(P)), (sgWT, A["sg_w"]),
                             (sgb, A["sg_b"][0].partition_broadcast(P)), (d_skip, A["d_skip"][0].partition_broadcast(P))):
                sp.dma_start(dst[:], src).then_inc(consts_loaded, 16)

            def step(I, s1, s2):
                i = I - 1
                r, r2 = rows_of(I), rows_of(i)
                I1, I2, i2, i22, i1 = (held(sp, q) for q in (I, I * 2, i * 2, i * 2 + 2, i + 1))
                at, at2 = held(sp, I * P), held(sp, i * P)
                now, before = bass.ds(at, r), bass.ds(at2, r2)
                if s1:
                    wait(sp, sg_psum, I2)
                    sp.dma_start(v[0:r, :], S["v"][now, :]).then_inc(v_loaded, 16)
                    wait(sp, sg_ready, I2)
                    sp.sem_inc(addressing, 1)
                    sp.dma_start(uT[:, :, 0:r], S["uT"].rearrange("(h p) t -> p h t", p=P)[:, :, now]).then_inc(u_loaded, 16)
                if s2:
                    wait(sp, h_ready, i2)
                    src = A["x_sample"].rearrange("b s d -> (b s) d") if r2 == TS else A["x_prompt"][0][before, :]
                    sp.dma_start(x[0:r2, :], src).then_inc(xr_loaded, 16)
                if s1:
                    wait(sp, yo_psum, I2)
                    sp.sem_inc(addressing, 1)
                    sp.dma_start(bct[:, :, 0:r], S["bct"].rearrange("(g p) t -> p g t", p=P)[:, :, now]).then_inc(bct_loaded, 16)
                    wait(sp, st_psum, I2)
                    wait(sp, xD_ready, I1)
                    sp.dma_start(xb[0:r, :], S["xb"][now, :]).then_inc(xb_loaded, 16)
                    wait(sp, gated, I1)
                    sp.dma_start(z[0:r, :], S["z"][now, :]).then_inc(z_loaded, 16)
                if s2:
                    sp.wait_ge(h_ready, i22)
                    sp.dma_start(S["h"][before, :], h[0:r2, :]).then_inc(h_stored, 16)
                    sp.wait_ge(hn_ready, i1)
                    sp.dma_start(S["hn"][before, :], hn[0:r2, :]).then_inc(hn_stored, 16)

            step(0, True, False)
            for dst, name in ((ssm_w, "ssm_norm_w"), (ffn_w, "norm_ffn_w"), (b_router, "b_router")):
                sp.dma_start(dst[:], A[name][0].partition_broadcast(P)).then_inc(later_loaded, 16)
            sp.dma_start(w_router[:], A["w_router"]).then_inc(later_loaded, 16)
            sp.dma_start(w_out_ssm[:], A["w_out"][:, 0:KT, :]).then_inc(w_out_ssm_loaded, 16)
            step(1, True, True)
            with sp.Fori(2, NT) as I:
                step(I, True, True)
            for j in range(2):
                sp.dma_start(old[j][:], A["state_ssm"][j]).then_inc(old_loaded[j], 16)
            step(NT, True, True)
            sp.wait_ge(state_ready, 2 * NT)
            sp.dma_start(A["ssm_prompt"], state[:]).then_inc(final_stored, 16)
            sp.wait_ge(vn_ready, NT + 1)
            sp.dma_start(A["sg_v_sample"], v[0:TS, :]).then_inc(final_stored, 16)
            for b in range(DEC_B):
                j = b % 2
                sp.wait_ge(new_ready, 2 * (b + 1))
                sp.dma_start(A["ssm_sample"][b], old[j][:]).then_inc(old_stored[j], 16)
                if b + 2 < DEC_B:
                    sp.wait_ge(old_stored[j], 16 * (b // 2 + 1))
                    sp.dma_start(old[j][:], A["state_ssm"][b + 2]).then_inc(old_loaded[j], 16)
            step(NT + 1, False, True)
            for s in old_stored:
                sp.wait_ge(s, 16 * (DEC_B // 2))
            sp.wait_ge(final_stored, 32)
            sp.wait_ge(h_stored, 16 * (NT + 1))
            sp.wait_ge(hn_stored, 16 * (NT + 1))

        @block.gpsimd
        def _(pool):
            pool.wait_ge(consts_loaded, 16 * 4)

            def step(i):
                r = rows_of(i)
                gt = C["gt"] if r == P else gt_s
                wait(pool, seg_psum, i * 4)
                nc.gpsimd.tensor_tensor(seg_lhs[0:r, :, 0:r], gt[0:r, 0:r].unsqueeze(1).to_broadcast([r, HEADS, r]),
                                        dtk[0:r, bass.ds(i, 1), HEADS:2 * HEADS].rearrange("p o h -> p (o h)").unsqueeze(2).to_broadcast([r, HEADS, r]),
                                        ALU.mult).then_inc(seg_ready, 1)
                pool.wait_ge(xb_loaded, i * 16 + 16)
                wait(pool, gated, i)
                nc.gpsimd.tensor_tensor(heads(xD, r), heads(xb, r), d_skip[0:r, :].unsqueeze(2).to_broadcast([r, HEADS, HD]),
                                        ALU.mult).then_inc(xD_ready, 1)
                pool.wait_ge(decay_ready, i + 1)
                pool.wait_ge(xdt_ready, i + 1)
                wait(pool, st_psum, i * 2)
                nc.gpsimd.tensor_tensor(heads(xdtE, r), heads(xdt, r), decay[0:r, 2, :].unsqueeze(2).to_broadcast([r, HEADS, HD]),
                                        ALU.mult).then_inc(xdtE_ready, 1)

            step(0)
            with pool.Fori(1, NT) as i:
                step(i)
            pool.wait_ge(consts_done, N_CONSTS)
            step(NT)

        @block.tensor
        def _(pe):
            def sg_projection(i, k0, k1):
                r = rows_of(i)
                for k in range(k0, k1):
                    for n in range(2):
                        last = nc.tensor.matmul(bank[6 + n][0:r, :], ysgT[:, k, 0:r], w_out_sg[:, k, n * 512:(n + 1) * 512],
                                                start=(k == 0), stop=False)
                return last

            def turn_hn(i, half):
                r = rows_of(i)
                pe.wait_ge(hn_ready, i + 1)
                if half == 0:
                    pe.wait_ge(yo_used, min(2 * i + 4, 2 * NT + 2) if isinstance(i, int) else i * 2 + 4)
                    if isinstance(i, int) and i > 0 or not isinstance(i, int):
                        pe.wait_ge(counted, i)
                else:
                    pe.wait_ge(hnT_done, i * 2 + 1)
                for q in range(4):
                    k = 4 * half + q
                    last = nc.tensor.transpose(bank[5][:, q * P:q * P + r], hn[0:r, k * P:(k + 1) * P], C["ident"][0:r, 0:r])
                last.then_inc(hnT_psum, 1)

            def step(I, s1, s2, s3):
                if s2:
                    i2 = I - 1
                    pe.wait_ge(sg_ready, i2 * 2 + 2)
                    wait(pe, h_ready, i2 * 2)
                    sg_projection(i2, 0, KT // 2)
                if s3:
                    turn_hn(I - 2, 0)
                if s2:
                    sg_projection(i2, KT // 2, KT).then_inc(sgproj_done, 1)
                if s3:
                    turn_hn(I - 2, 1)
                if s1:
                    r = rows_of(I)
                    le, gt = (C["le"], C["gt"]) if r == P else (le_s, gt_s)
                    dta = dtk[0:r, bass.ds(I, 1), HEADS:2 * HEADS].rearrange("p o h -> p (o h)")
                    pe.wait_ge(bct_loaded, I * 16 + 16)
                    wait(pe, yo_used, I * 2)
                    for g in range(GROUPS):
                        nc.tensor.matmul(bank[2][0:r, g * P:g * P + r], bct[:, g, 0:r], bct[:, GROUPS + g, 0:r],
                                         start=True, stop=True)
                    nc.tensor.matmul(bank[2][0:r, 256:272], le[0:r, 0:r], dta, start=True, stop=True)
                    if r == P:
                        nc.tensor.matmul(bank[2][:, 272:288], C["ones"][:], dta, start=True, stop=True)
                    nc.tensor.matmul(bank[2][0:r, 288:304], gt[0:r, 0:r], dta, start=True, stop=True).then_inc(cb_psum, 1)
                    if r == TS:
                        pe.wait_ge(link1, LINK1 * NT + 2)
                        nc.tensor.matmul(bank[2][:, 304:304 + DEC_B * HEADS], C["ones"][0:TS, :],
                                         dta_s[:].rearrange("p b h -> p (b h)"), start=True, stop=True).then_inc(cb_psum, 1)
                    pe.wait_ge(seg_ready, I + 1)
                    wait(pe, state_ready, I * 2)
                    for q in range(4):
                        if q >= 2:
                            pe.wait_ge(seg_exp, I * 4 + (q - 1))
                        for hh in range(4):
                            last = nc.tensor.matmul(bank[q % 2][0:r, hh * P:hh * P + r], seg_lhs[0:r, 4 * q + hh, 0:r],
                                                    le[0:r, 0:r], start=True, stop=True)
                        last.then_inc(seg_psum, 1)
                if s3:
                    i3 = I - 2
                    r3 = rows_of(i3)
                    pe.wait_ge(hnT_done, i3 * 2 + 2)
                    for k in range(KT):
                        last = nc.tensor.matmul(bank[5][0:r3, 0:EG + E], hnT[:, k, 0:r3], w_router[:, k, :],
                                                start=(k == 0), stop=(k == KT - 1))
                    last.then_inc(logits_psum, 1)
                if s2:
                    r2 = rows_of(i2)
                    pe.wait_ge(yn_ready, i2 + 1)
                    for half in range(2):
                        for q in range(4):
                            k = 4 * half + q
                            last = nc.tensor.transpose(bank[3 + half][:, q * P:q * P + r2], y[0:r2, k * P:(k + 1) * P],
                                                       C["ident"][0:r2, 0:r2])
                        last.then_inc(yT_psum, 1)
                if s1:
                    W = sgWT if r == P else sgWT_s
                    pe.wait_ge(vn_ready, I + 1)
                    for q in range(2):
                        pe.wait_ge(seg_exp, I * 4 + (3 + q))
                        for hh in range(4):
                            hd = 4 * q + hh
                            last = nc.tensor.matmul(bank[q][:, hh * P:hh * P + r], v[0:r, hd * P:(hd + 1) * P],
                                                    W[0:r, hd, 0:r], start=True, stop=True)
                        last.then_inc(sg_psum, 1)
                if s2:
                    if isinstance(i2, int) and i2 == 0:
                        pe.wait_ge(w_out_ssm_loaded, 16)
                    for half in range(2):
                        pe.wait_ge(yT_done, i2 * 2 + (half + 1))
                        for k in range(4 * half, 4 * half + 4):
                            for n in range(2):
                                last = nc.tensor.matmul(bank[6 + n][0:r2, :], yT[:, k, 0:r2], w_out_ssm[:, k, n * 512:(n + 1) * 512],
                                                        start=False, stop=(k == KT - 1))
                    last.then_inc(mix_psum, 1)
                if s3:
                    pe.wait_ge(assigned, i3 + 1)
                    nc.tensor.matmul(bank[5][0:r3, 64:64 + E], C["lt"][0:r3, 0:r3], chosen[0:r3, :], start=True, stop=True)
                    nc.tensor.matmul(bank[5][:, 96:96 + E], C["ones"][0:r3, :], chosen[0:r3, :], start=True, stop=True).then_inc(count_psum, 1)
                if s1:
                    pe.wait_ge(xdt_ready, I + 1)
                    wait(pe, yT_done, I * 2)
                    for g in range(GROUPS):
                        pe.wait_ge(m_ready, I * 4 + (2 * g + 2))
                        for hh in range(8):
                            hd = 8 * g + hh
                            last = nc.tensor.matmul(bank[3 + g][0:r, hh * HD:(hh + 1) * HD], M[0:r, hd, 0:r],
                                                    xdt[0:r, hd * HD:(hd + 1) * HD], start=True, stop=True)
                        last.then_inc(yd_psum, 1)
                    pe.wait_ge(xdtE_ready, I + 1)
                    if s3:
                        pe.wait_ge(counted, i3 + 1)
                    if r == P:
                        for g in range(GROUPS):
                            pe.wait_ge(sg_sum, I * 2 + (g + 1))
                            nc.tensor.matmul(bank[g][:, :], xb[:, D + g * NSTATE:D + (g + 1) * NSTATE],
                                             xdtE[:, g * 512:(g + 1) * 512], start=True, stop=True).then_inc(st_psum, 1)
                        pe.wait_ge(decay_ready, I + 1)
                        pe.wait_ge(cbm_ready, I + 1)
                        for g in (1, 0):
                            nc.tensor.matmul(bank[2 if g else 5][:, :], bct[:, GROUPS + g, :], state[:, g * 512:(g + 1) * 512],
                                             start=True, stop=True).then_inc(yo_psum, 1)
                    else:
                        pe.wait_ge(sg_sum, I * 2 + 2)
                        pe.wait_ge(decay_ready, I + 1)
                        pe.wait_ge(cbm_ready, I + 1)
                        for b in range(DEC_B):
                            j = b % 2
                            pe.wait_ge(old_loaded[j], 16 * (b // 2 + 1))
                            pe.wait_ge(of_ready, b + 1)
                            for g in (1, 0):
                                last = nc.tensor.matmul(bank[2 if g else 5][0:TS, :], c_of[j][:, g, :], old[j][:, g * 512:(g + 1) * 512],
                                                        start=(b == 0), stop=(b == DEC_B - 1))
                                if b == DEC_B - 1:
                                    last.then_inc(yo_psum, 1)
                            for g in range(GROUPS):
                                wait(pe, new_ready, 2 * (b - 1) + g + 1)
                                nc.tensor.matmul(bank[g][:, :], b_of[j][:, g * NSTATE:(g + 1) * NSTATE],
                                                 xdtE[0:TS, g * 512:(g + 1) * 512], start=True, stop=True).then_inc(new_psum, 1)

            pe.wait_ge(consts_done, 1)
            nc.tensor.matmul(bank[2][0:TS, 0:SGH * DEC_S], C["repeat"][:], sgWT[0:DEC_S, :, 0:DEC_S],
                             start=True, stop=True).then_inc(rep_psum, 1)
            pe.wait_ge(consts_done, N_CONSTS)
            step(0, True, False, False)
            pe.wait_ge(S["w_out_loaded"], 16)
            pe.wait_ge(later_loaded, 16 * 4)
            step(1, True, True, False)
            with pe.Fori(2, NT) as I:
                step(I, True, True, True)
            step(NT, True, True, True)
            step(NT + 1, False, True, True)
            step(NT + 2, False, False, True)

        @block.scalar
        def _(act):
            def step(I, s1, s2, s3):
                if s3:
                    i3 = I - 2
                    r3 = rows_of(i3)
                    for half in range(2):
                        act.wait_ge(hnT_psum, i3 * 2 + (half + 1))
                        wait(act, logits_psum, i3)
                        nc.scalar.copy(hnT[:, 4 * half:4 * half + 4, 0:r3],
                                       bank[5][:].rearrange("p (k t) -> p k t", k=4)[:, :, 0:r3]).then_inc(hnT_done, 1)
                if s1:
                    r = rows_of(I)
                    if r == P:
                        act.wait_ge(cb_psum, I + 1)
                    else:
                        act.wait_ge(cb_psum, NT + 2)
                        nc.scalar.activation(decay_s[:].rearrange("p b h -> p (b h)"), bank[2][:, 304:304 + DEC_B * HEADS], ACT.Exp)
                    wait(act, xdtE_ready, I)
                    wait(act, state_ready, I * 2)
                    if r == P:
                        nc.scalar.activation(decay[:].rearrange("p a h -> p (a h)"), bank[2][:, 256:304], ACT.Exp).then_inc(decay_ready, 1)
                    else:
                        nc.scalar.activation(decay[0:TS, 0, :], bank[2][0:TS, 256:272], ACT.Exp)
                        nc.scalar.activation(decay[0:TS, 2, :], bank[2][0:TS, 288:304], ACT.Exp).then_inc(decay_ready, 1)
                    wait(act, yd_psum, I * 2)
                    for q in range(4):
                        act.wait_ge(seg_psum, I * 4 + (q + 1))
                        nc.scalar.activation(M[0:r, 4 * q:4 * q + 4, 0:r],
                                             bank[q % 2][:].rearrange("p (h l) -> p h l", h=4)[0:r, :, 0:r],
                                             ACT.Exp).then_inc(seg_exp, 1)
                if s1:
                    act.wait_ge(v_loaded, I * 16 + 16)
                    wait(act, vn_ready, I)
                    then_own(act, nc.scalar.activation(junk[0:r, :], v[0:r, :], ACT.Square, accum_out=st_v[0:r, 0:1]), v_sq, I + 1)
                    nc.scalar.activation(st_v[0:r, 1:2], st_v[0:r, 0:1], ACT.Sqrt, bias=C["eps"][0:r, :], scale=1.0 / D).then_inc(v_rms, 1)
                if s3:
                    act.wait_ge(shifted, i3 * 2 + 1)
                    nc.scalar.activation(r8[0:r3, 1, 0:EG], lg[0:r3, 0:EG], ACT.Exp, bias=r8[0:r3, 0, 1:2],
                                         accum_out=r8[0:r3, 0, 2:3]).then_inc(exped, 1)
                    act.wait_ge(shifted, i3 * 2 + 2)
                    nc.scalar.activation(r8[0:r3, 4, :], r8[0:r3, 3, :], ACT.Exp, bias=r8[0:r3, 0, 4:5],
                                         accum_out=r8[0:r3, 0, 5:6]).then_inc(exped, 1)
                if s2:
                    i2 = I - 1
                    r2 = rows_of(i2)
                    wait(act, mix_psum, i2)
                    for half in range(2):
                        act.wait_ge(yT_psum, i2 * 2 + (half + 1))
                        nc.scalar.copy(yT[:, 4 * half:4 * half + 4, 0:r2],
                                       bank[3 + half][:].rearrange("p (k t) -> p k t", k=4)[:, :, 0:r2]).then_inc(yT_done, 1)
                    act.wait_ge(h_ready, i2 * 2 + 2)
                    wait(act, hn_ready, i2)
                    then_own(act, nc.scalar.activation(junk[0:r2, :], h[0:r2, :], ACT.Square, accum_out=st_h[0:r2, 0:1]), h_sq, i2 + 1)
                    nc.scalar.activation(st_h[0:r2, 1:2], st_h[0:r2, 0:1], ACT.Sqrt, bias=C["eps"][0:r2, :], scale=1.0 / D).then_inc(h_rms, 1)
                if s1:
                    act.wait_ge(gated, I + 1)
                    wait(act, yn_ready, I)
                    for g in range(GROUPS):
                        nc.scalar.activation(junk[0:r, g * 512:(g + 1) * 512], y[0:r, g * 512:(g + 1) * 512], ACT.Square,
                                             accum_out=st_y[0:r, g:g + 1]).then_inc(y_sq, 1)
                    act.wait_ge(y_sq, I * 2 + 2)
                    nc.scalar.activation(st_y[0:r, 2:4], st_y[0:r, 0:2], ACT.Sqrt, bias=C["eps"][0:r, :],
                                         scale=2.0 / D).then_inc(y_rms, 1)

            step(0, True, False, False)
            step(1, True, True, False)
            with act.Fori(2, NT) as I:
                step(I, True, True, True)
            step(NT, True, True, True)
            step(NT + 1, False, True, True)
            step(NT + 2, False, False, True)

        @block.vector
        def _(dve):
            l1, l2, l3 = Links(dve, link1, LINK1), Links(dve, link2, LINK2), Links(dve, link3, LINK3)

            def over(t, r, n):
                return t.unsqueeze(2).to_broadcast([r, HEADS, n])

            def halves(t, r, g):
                return t[0:r, g * 512:(g + 1) * 512].rearrange("p (h d) -> p h d", d=HD)

            def route(i, r):
                l3.begin(i)
                dve.wait_ge(logits_psum, i + 1)
                R = r8[0:r]
                l3(nc.vector.tensor_tensor(lg[0:r, :], bank[5][0:r, 0:EG + E], b_router[0:r, :], ALU.add))
                l3(nc.vector.tensor_reduce(R[:, 0, 0:1], lg[0:r, 0:EG], AX.X, ALU.max))
                nc.vector.tensor_scalar(R[:, 0, 1:2], R[:, 0, 0:1], -1.0, None, ALU.mult).then_inc(shifted, 1)
                dve.wait_ge(exped, i * 2 + 1)
                l3(nc.vector.reciprocal(R[:, 0, 0:1], R[:, 0, 2:3]))
                l3(nc.vector.tensor_scalar(R[:, 1, 0:EG], R[:, 1, 0:EG], R[:, 0, 0:1], None, ALU.mult))
                l3.settle()
                l3(nc.vector.max(R[:, 2, :], R[:, 1, :]))
                l3.settle()
                l3(nc.vector.max_index(idx[0:r, 0, :], R[:, 2, :], R[:, 1, :]))
                l3(nc.vector.tensor_copy(R[:, 0, 6:7], idx[0:r, 0, 0:1]))
                l3(nc.vector.tensor_scalar(R[:, 7, 0:EG], C["expert_no"][0:r, 0:EG], R[:, 0, 6:7], None, ALU.is_equal))
                l3(nc.vector.tensor_tensor(pick[0:r], lg[0:r, EG:].rearrange("p (g e) -> p g e", e=EPG),
                                           R[:, 7, 0:EG].unsqueeze(2).to_broadcast([r, EG, EPG]), ALU.mult))
                l3(nc.vector.tensor_reduce(R[:, 3, :], pick[0:r].rearrange("p g e -> p e g"), AX.X, ALU.add))
                l3(nc.vector.tensor_reduce(R[:, 0, 3:4], R[:, 3, :], AX.X, ALU.max))
                nc.vector.tensor_scalar(R[:, 0, 4:5], R[:, 0, 3:4], -1.0, None, ALU.mult).then_inc(shifted, 1)
                dve.wait_ge(exped, i * 2 + 2)
                l3(nc.vector.reciprocal(R[:, 0, 7:8], R[:, 0, 5:6]))
                l3(nc.vector.tensor_scalar(R[:, 4, :], R[:, 4, :], R[:, 0, 7:8], None, ALU.mult))
                l3.settle()
                l3(nc.vector.max(R[:, 5, :], R[:, 4, :]))
                l3.settle()
                l3(nc.vector.max_index(idx[0:r, 1, :], R[:, 5, :], R[:, 4, :]))
                l3(nc.vector.tensor_copy(R[:, 6, 0:2], idx[0:r, 1, 0:2]))
                l3(nc.vector.tensor_scalar(R[:, 0, 3:4], R[:, 0, 6:7], float(EPG), None, ALU.mult))
                l3(nc.vector.tensor_scalar(R[:, 6, 2:4], R[:, 6, 0:2], R[:, 0, 3:4], None, ALU.add))
                l3(nc.vector.tensor_tensor(R[:, 6, 4:5], R[:, 5, 0:1], R[:, 5, 1:2], ALU.add))
                l3(nc.vector.reciprocal(R[:, 6, 5:6], R[:, 6, 4:5]))
                l3(nc.vector.tensor_scalar(S["gate"][0:r, bass.ds(i, 1), :], R[:, 5:6, 0:2], R[:, 2, 0:1], R[:, 6, 5:6],
                                           ALU.mult, ALU.mult))
                hot = S["hot"]
                for k in range(2):
                    l3(nc.vector.tensor_scalar(hot[0:r, bass.ds(i, 1), k, :], C["expert_no"][0:r, :].unsqueeze(1),
                                               R[:, 6, 2 + k:3 + k], None, ALU.is_equal))
                nc.vector.tensor_tensor(chosen[0:r, :].unsqueeze(1), hot[0:r, bass.ds(i, 1), 0, :], hot[0:r, bass.ds(i, 1), 1, :],
                                        ALU.add).then_inc(assigned, 1)

            def step(I, s1, s2, s3):
                if s1:
                    r = rows_of(I)
                    le = C["le"] if r == P else le_s
                    dt_r = dtk[0:r, bass.ds(I, 1), 0:HEADS].rearrange("p o h -> p (o h)")
                    l1.begin(I)
                    if r == TS:
                        l1(nc.vector.tensor_copy(dta_s[:], dtk[0:TS, NT, HEADS:2 * HEADS].unsqueeze(1).to_broadcast([TS, DEC_B, HEADS])))
                        l1(nc.vector.tensor_tensor(dta_s[:], dta_s[:],
                                                   C["same"][:, 0:TS:DEC_S].unsqueeze(2).to_broadcast([TS, DEC_B, HEADS]), ALU.mult))
                    dve.wait_ge(decay_ready, I + 1)
                    nc.vector.tensor_tensor(cbm[0:r, :, 0:r], bank[2][:, 0:2 * P].rearrange("p (g l) -> p g l", g=2)[0:r, :, 0:r],
                                            le[0:r, 0:r].unsqueeze(1).to_broadcast([r, 2, r]), ALU.mult).then_inc(cbm_ready, 1)
                    dve.wait_ge(xb_loaded, I * 16 + 16)
                    wait(dve, yd_psum, I * 2)
                    wait(dve, xdtE_ready, I)
                    nc.vector.tensor_tensor(heads(xdt, r), heads(xb, r), over(dt_r, r, HD), ALU.mult).then_inc(xdt_ready, 1)
                    dve.wait_ge(cbm_ready, I + 1)
                    for q in range(4):
                        dve.wait_ge(seg_exp, I * 4 + (q + 1))
                        nc.vector.tensor_tensor(M[0:r, 4 * q:4 * q + 4, 0:r], M[0:r, 4 * q:4 * q + 4, 0:r],
                                                cbm[0:r, q // 2, 0:r].unsqueeze(1).to_broadcast([r, 4, r]), ALU.mult).then_inc(m_ready, 1)
                    dve.wait_ge(v_rms, I + 1)
                    l1(nc.vector.reciprocal(st_v[0:r, 2:3], st_v[0:r, 1:2]))
                    nc.vector.scalar_tensor_tensor(out=v[0:r, :], in0=v[0:r, :], scalar=st_v[0:r, 2:3], in1=sg_w_row[0:r, :],
                                                   op0=ALU.mult, op1=ALU.mult).then_inc(vn_ready, 1)
                if s3:
                    route(I - 2, rows_of(I - 2))
                if s1:
                    wait(dve, sgproj_done, I)
                    for q in range(2):
                        dve.wait_ge(sg_psum, I * 2 + (q + 1))
                        s = slice(4 * q, 4 * q + 4)
                        got = bank[q][:].rearrange("p (h t) -> p h t", h=4)[:, :, 0:r]
                        if r == P:
                            ins = nc.vector.tensor_tensor(ysgT[:, s, :], got, sgb[:, s, :], ALU.add)
                            ins.then_inc(sg_sum, 1)
                        else:
                            for hh in range(4):
                                seqs = lambda t: t.rearrange("p (b s) -> p b s", s=DEC_S)
                                ins = nc.vector.tensor_tensor(
                                    seqs(ysgT[:, 4 * q + hh, 0:TS]), seqs(got[:, hh, :]),
                                    sgb[:, 4 * q + hh, 0:DEC_S].unsqueeze(1).to_broadcast([P, DEC_B, DEC_S]), ALU.add)
                            ins.then_inc(sg_sum, 1)
                    dve.wait_ge(u_loaded, I * 16 + 16)
                    for q in range(2):
                        s = slice(4 * q, 4 * q + 4)
                        dve.wait_ge(sg_sum, I * 2 + (q + 1))
                        nc.vector.tensor_tensor(ysgT[:, s, 0:r], ysgT[:, s, 0:r], uT[:, s, 0:r], ALU.mult).then_inc(sg_ready, 1)
                if s2:
                    i2 = I - 1
                    r2 = rows_of(i2)
                    l2.begin(i2)
                    dve.wait_ge(mix_psum, i2 + 1)
                    dve.wait_ge(xr_loaded, i2 * 16 + 16)
                    wait(dve, h_stored, i2 * 16)
                    for n in range(2):
                        s = slice(n * 512, (n + 1) * 512)
                        nc.vector.tensor_tensor(h[0:r2, s], bank[6 + n][0:r2, :], x[0:r2, s], ALU.add).then_inc(h_ready, 1)
                if s3:
                    i3, r3 = I - 2, rows_of(I - 2)
                    dve.wait_ge(count_psum, i3 + 1)
                    l3(nc.vector.tensor_tensor(S["before"][0:r3, bass.ds(i3, 1), :], bank[5][0:r3, 64:64 + E].unsqueeze(1),
                                               run[0:r3, :].unsqueeze(1), ALU.add))
                    nc.vector.tensor_tensor(run[:], bank[5][:, 96:96 + E], run[:], ALU.add).then_inc(counted, 1)
                    dve.wait_ge(counted, i3 + 1)
                if s2:
                    dve.wait_ge(h_rms, i2 + 1)
                    l2(nc.vector.reciprocal(st_h[0:r2, 2:3], st_h[0:r2, 1:2]))
                    wait(dve, hn_stored, i2 * 16)
                    wait(dve, hnT_psum, i2 * 2)
                    dve.wait_ge(h_ready, i2 * 2 + 2)
                    nc.vector.scalar_tensor_tensor(out=hn[0:r2, :], in0=h[0:r2, :], scalar=st_h[0:r2, 2:3], in1=ffn_w[0:r2, :],
                                                   op0=ALU.mult, op1=ALU.mult).then_inc(hn_ready, 1)
                if s1:
                    if r == TS:
                        sample_states()
                    wait(dve, yT_psum, I * 2)
                    for n, g in enumerate((1, 0)):
                        dve.wait_ge(yo_psum, I * 2 + (n + 1))
                        nc.vector.tensor_tensor(halves(y, r, g), bank[2 if g else 5][0:r, :].rearrange("p (h d) -> p h d", d=HD),
                                                decay[0:r, 0, 8 * g:8 * g + 8].unsqueeze(2).to_broadcast([r, 8, HD]),
                                                ALU.mult).then_inc(yo_used, 1)
                    for g in range(GROUPS):
                        dve.wait_ge(yd_psum, I * 2 + (g + 1))
                        dve.wait_ge(yo_used, I * 2 + 2)
                        nc.vector.tensor_tensor(halves(y, r, g), halves(y, r, g),
                                                bank[3 + g][0:r, :].rearrange("p (h d) -> p h d", d=HD), ALU.add).then_inc(yd_used, 1)
                    dve.wait_ge(yd_used, I * 2 + 2)
                    dve.wait_ge(xD_ready, I + 1)
                    l1(nc.vector.tensor_tensor(y[0:r, :], y[0:r, :], xD[0:r, :], ALU.add))
                    dve.wait_ge(z_loaded, I * 16 + 16)
                    nc.vector.tensor_tensor(y[0:r, :], y[0:r, :], z[0:r, :], ALU.mult).then_inc(gated, 1)
                    if r == P:
                        l1(nc.vector.tensor_tensor(heads(state, P), heads(state, P), over(decay[:, 1, :], P, HD), ALU.mult))
                        for g in range(GROUPS):
                            dve.wait_ge(st_psum, I * 2 + (g + 1))
                            s = slice(g * 512, (g + 1) * 512)
                            nc.vector.tensor_tensor(state[:, s], state[:, s], bank[g][:, :], ALU.add).then_inc(state_ready, 1)
                    dve.wait_ge(gated, I + 1)
                    if r == P:
                        dve.wait_ge(state_ready, I * 2 + 2)
                    dve.wait_ge(y_rms, I + 1)
                    l1(nc.vector.reciprocal(st_y[0:r, 4:6], st_y[0:r, 2:4]))
                    if isinstance(I, int) and I == 0:
                        dve.wait_ge(later_loaded, 16 * 4)
                    for g in range(GROUPS):
                        s = slice(g * 512, (g + 1) * 512)
                        ins = nc.vector.scalar_tensor_tensor(out=y[0:r, s], in0=y[0:r, s], scalar=st_y[0:r, 4 + g:5 + g],
                                                             in1=ssm_w[0:r, s], op0=ALU.mult, op1=ALU.mult)
                    ins.then_inc(yn_ready, 1)

            def sample_states():
                dve.wait_ge(bct_loaded, 16 * (NT + 1))
                dve.wait_ge(decay_ready, NT + 1)

                def mask(b):
                    j = b % 2
                    wait(dve, new_psum, 2 * (b - 1))
                    for g in range(GROUPS):
                        nc.vector.tensor_tensor(c_of[j][:, g, :], bct[:, GROUPS + g, 0:TS], C["of_seq"][:, b, :], ALU.mult)
                    nc.vector.tensor_scalar(b_of[j][:], xb[0:TS, D:], C["same"][:, DEC_S * b:DEC_S * b + 1], None,
                                            ALU.mult).then_inc(of_ready, 1)

                mask(0)
                mask(1)
                for b in range(DEC_B):
                    j = b % 2
                    dve.wait_ge(new_psum, 2 * b + 2)
                    l1(nc.vector.tensor_tensor(heads(old[j], P), heads(old[j], P), over(decay_s[:, b, :], P, HD), ALU.mult))
                    for g in range(GROUPS):
                        s = slice(g * 512, (g + 1) * 512)
                        nc.vector.tensor_tensor(old[j][:, s], old[j][:, s], bank[g][:, :], ALU.add).then_inc(new_ready, 1)
                    if b + 2 < DEC_B:
                        mask(b + 2)

            for t in (S["hot"], S["before"]):
                nc.vector.memset(t[:, NT:NT + 1], 0.0)
            nc.vector.memset(run[:], 0.0)
            nc.vector.memset(state[:], 0.0)
            nc.vector.memset(r8[:], -1.0)
            dve.wait_ge(consts_loaded, 16 * 4)
            nc.vector.tensor_tensor(sgWT[:], sgWT[:], C["le"][:].unsqueeze(1).to_broadcast([P, SGH, P]), ALU.mult).then_inc(consts_done, 1)
            nc.vector.tensor_tensor(le_s[:], C["le"][0:TS, 0:TS], C["same"][:], ALU.mult).then_inc(consts_done, 1)
            nc.vector.tensor_tensor(gt_s[:], C["gt"][0:TS, 0:TS], C["same"][:], ALU.mult).then_inc(consts_done, 1)
            dve.wait_ge(rep_psum, 1)
            for b in range(DEC_B):
                ins = nc.vector.tensor_copy(sgWT_s[:, :, b * DEC_S:(b + 1) * DEC_S],
                                            bank[2][0:TS, 0:SGH * DEC_S].rearrange("p (h t) -> p h t", h=SGH))
            ins.then_inc(consts_done, 1)
            dve.wait_ge(consts_done, 4)
            nc.vector.tensor_tensor(sgWT_s[:], sgWT_s[:], C["same"][:].unsqueeze(1).to_broadcast([TS, SGH, TS]),
                                    ALU.mult).then_inc(consts_done, 1)
            nc.vector.memset(st_v[:], 1.0).then_inc(consts_done, 1)
            nc.vector.memset(st_y[:], 1.0).then_inc(consts_done, 1)
            dve.wait_ge(consts_done, N_CONSTS)
            step(0, True, False, False)
            step(1, True, True, False)
            with dve.Fori(2, NT) as I:
                step(I, True, True, True)
            step(NT, True, True, True)
            step(NT + 1, False, True, True)
            step(NT + 2, False, False, True)


LINK1, LINK2, LINK3 = 4, 1, 28


def experts(nc, A, S, C, bank):
    with ExitStack() as ctx:
        def sb(name, shape, dt=F32):
            return ctx.enter_context(nc.sbuf_tensor(name, shape, dt))

        def sem(name):
            return ctx.enter_context(nc.semaphore(name))

        N_ASG = 2 * (NT + 1)
        over = sb("over", [P, E, NT + 1])
        n_blk, blk_end, row0 = sb("n_blk", [P, E]), sb("blk_end", [P, E]), sb("row0", [P, E])
        place = sb("place", [P, NT + 1, 2, E])
        row_f = sb("row_f", [P, NT + 1, 2])
        before_end = sb("before_end", [1, MAXBLK, E])
        blk_f = sb("blk_f", [1, MAXBLK + 1])
        blk_i = sb("blk_i", [1, MAXBLK + 1], I32)
        at_or_past = sb("at_or_past", [P, N_ASG, MAXBLK + 1])
        of_block, in_block = sb("of_block", [P, N_ASG]), sb("in_block", [P, N_ASG])
        of_row_f = sb("of_row_f", [P, 2, MAXBLK])
        of_row = sb("of_row", [P, 2, MAXBLK], I32)
        src, dst = sb("src", [P, 1], I32), sb("dst", [P, 1], I32)
        xg = sb("xg", [P, D])
        xh, xl = sb("xh_blk", [P, KT, P], F32R), sb("xl_blk", [P, KT, P], F32R)
        wg, wu = sb("wg", [P, KT, FF]), sb("wu", [P, KT, FF])
        wd = sb("wd", [P, FF // P, D])
        wg_h, wg_l = sb("wg_h", [P, KT, FF], F32R), sb("wg_l", [P, KT, FF], F32R)
        wu_h, wu_l = sb("wu_h", [P, KT, FF], F32R), sb("wu_l", [P, KT, FF], F32R)
        wd_h, wd_l = sb("wd_h", [P, FF // P, D], F32R), sb("wd_l", [P, FF // P, D], F32R)
        spare = wd[:].rearrange("p f d -> p (f d)")
        place_hot = spare[:, 0:N_ASG * P].rearrange("p (a c) -> p a c", a=N_ASG)
        block_value = spare[:, N_ASG * P:N_ASG * (P + 2 * MAXBLK)].rearrange("p (a o n) -> p a o n", a=N_ASG, o=2)
        act_g, hid = sb("act_g", [P, FF]), sb("hid", [P, FF])
        hT_h, hT_l = sb("hT_h", [P, FF // P, P], F32R), sb("hT_l", [P, FF // P, P], F32R)
        yb = sb("yb", [P, D])

        chain, table_ready = sem("chain"), sem("table_ready")
        zeroed, rows_psum, rows_ready = sem("zeroed"), sem("rows_psum"), sem("rows_ready")
        gate_up_loaded = [sem(f"gate_up_loaded{p}") for p in range(4)]
        down_loaded = [sem(f"down_loaded{p}") for p in range(4)]
        src_ready, dst_ready, xg_loaded = sem("src_ready"), sem("dst_ready"), sem("xg_loaded")
        gu_high, gu_split, gu_used = sem("gu_high"), sem("gu_split"), sem("gu_used")
        down_high, down_split, down_used = sem("down_high"), sem("down_split"), sem("down_used")
        x_high, h_high = sem("xb_high"), sem("h_high")
        silu_done, hid_ready = sem("silu_done"), sem("hid_ready")
        xT_psum, xT_done = sem("xTb_psum"), sem("xTb_done")
        hT_psum, hT_done = sem("hT_psum"), sem("hT_done")
        y_done, y_stored = sem("y_done"), sem("y_stored")
        holder = C["holder"]

        block = ctx.enter_context(nc.Block())

        def blocks_but_three(eng):
            eng.wait_ge(table_ready, 1)
            return eng.value_load(blk_i[0:1, MAXBLK:MAXBLK + 1], min_val=MINBLK - 3, max_val=MAXBLK - 3)

        @block.sync
        def _(sp):
            def expert(i):
                e = sp.value_load(blk_i[0:1, bass.ds(i, 1)], min_val=0, max_val=E - 1)
                return bass.ds(e, 1)

            def load_gate_up(i):
                e = expert(i)
                at = [held(sp, i * 4 + (p - 3)) for p in range(4)]
                for p in range(4):
                    wait(sp, gu_split, at[p])
                    rows = slice(2 * p * P, (2 * p + 2) * P)
                    for t, name in ((wg, "w_gate"), (wu, "w_up")):
                        sp.dma_start(t[:, 2 * p:2 * p + 2, :], A[name][e, rows, :].rearrange("e (k p) f -> p (e k) f", p=P)).then_inc(gate_up_loaded[p], 16)

            def load_down(i):
                e = expert(i)
                at = [held(sp, i * 4 + (p - 3)) for p in range(4)]
                for p in range(4):
                    wait(sp, down_split, at[p])
                    sp.dma_start(wd[:, p, :], A["w_down"][e, p * P:(p + 1) * P, :].rearrange("e p d -> p (e d)")).then_inc(down_loaded[p], 16)

            m = blocks_but_three(sp) + 1
            load_gate_up(0)
            sp.wait_ge(rows_ready, 1)
            load_down(0)
            load_gate_up(1)
            with sp.Fori(0, m) as i:
                load_gate_up(i + 2)
                load_down(i + 1)
            load_down(m + 1)
            sp.wait_ge(y_stored, m * 16 + 32)
            sp.sem_inc(holder, 1)

        @block.gpsimd
        def _(pool):
            nc.gpsimd.memset(xg[:], 0.0).then_inc(zeroed, 1)
            pool.wait_ge(zeroed, 1)
            pool.wait_ge(rows_ready, 1)
            m = blocks_but_three(pool)

            def gather(i):
                wait(pool, xg_loaded, i * 16)
                then_own(pool, nc.gpsimd.tensor_copy(src[:], of_row[:, 0, bass.ds(i, 1)]), src_ready, i + 1)
                wait(pool, xT_psum, i * 2)
                pool.sem_inc(holder, 1)
                pool.indirect_dma_start(out=xg[:], out_offset=None, in_=S["hn"],
                                        in_offset=bass.IndirectOffsetOnAxis(ap=src[:], axis=0),
                                        bounds_check=T - 1, oob_is_err=False).then_inc(xg_loaded, 16)

            def scatter(i):
                wait(pool, y_stored, i * 16)
                then_own(pool, nc.gpsimd.tensor_copy(dst[:], of_row[:, 1, bass.ds(i, 1)]), dst_ready, i + 1)
                pool.wait_ge(y_done, i * 2 + 2)
                pool.sem_inc(holder, 1)
                pool.indirect_dma_start(out=S["picked"], out_offset=bass.IndirectOffsetOnAxis(ap=dst[:], axis=0),
                                        in_=yb[:], in_offset=None, bounds_check=2 * T - 1, oob_is_err=False).then_inc(y_stored, 16)

            def low_down(i):
                for p in range(4):
                    pool.wait_ge(down_high, i * 4 + (p + 1))
                    nc.gpsimd.tensor_tensor(wd_l[:, p, :], wd[:, p, :], wd_h[:, p, :].bitcast(F32), ALU.subtract).then_inc(down_split, 1)

            gather(0)
            gather(1)
            gather(2)
            low_down(0)
            with pool.Fori(1, m + 1) as i:
                gather(i + 2)
                low_down(i)
                scatter(i - 1)
            low_down(m + 1)
            scatter(m)
            low_down(m + 2)
            scatter(m + 1)
            scatter(m + 2)

        @block.tensor
        def _(pe):
            def turn_x(i):
                pe.wait_ge(xg_loaded, i * 16 + 16)
                for half in range(2):
                    wait(pe, xT_done, i * 2 + (half - 1))
                    for q in range(4):
                        last = nc.tensor.transpose(bank[4 + half][:, q * P:(q + 1) * P], xg[:, (4 * half + q) * P:(4 * half + q + 1) * P],
                                                   C["ident"][:])
                    last.then_inc(xT_psum, 1)

            def gate_up(i):
                wait(pe, hid_ready, i)
                for k in range(KT):
                    if k % 2 == 0:
                        pe.wait_ge(gu_split, i * 4 + (k // 2 + 1))
                    if k % 4 == 0:
                        pe.wait_ge(xT_done, i * 2 + (k // 4 + 1))
                    for n, (w_h, w_l) in enumerate(((wg_h, wg_l), (wu_h, wu_l))):
                        last = split_product(nc, bank[n][:, :], (xh[:, k, :], xl[:, k, :]), (w_h[:, k, :], w_l[:, k, :]),
                                             start=(k == 0), stop=(k == KT - 1))
                    if k % 2:
                        last.then_inc(gu_used, 1)

            def turn_hid(i):
                pe.wait_ge(hid_ready, i + 1)
                for f in range(FF // P):
                    last = nc.tensor.transpose(bank[6][:, f * P:(f + 1) * P], hid[:, f * P:(f + 1) * P], C["ident"][:])
                last.then_inc(hT_psum, 1)

            def down(i):
                pe.wait_ge(hT_done, i + 1)
                wait(pe, y_done, i * 2)
                for f in range(FF // P):
                    pe.wait_ge(down_split, i * 4 + (f + 1))
                    for n in range(2):
                        s = slice(n * 512, (n + 1) * 512)
                        last = split_product(nc, bank[2 + n][:, :], (hT_h[:, f, :], hT_l[:, f, :]), (wd_h[:, f, s], wd_l[:, f, s]),
                                             start=(f == 0), stop=(f == FF // P - 1))
                    last.then_inc(down_used, 1)

            pe.wait_ge(table_ready, 2)
            for a in range(N_ASG):
                r = P if a < 2 * NT else TS
                last = nc.tensor.matmul(bank[0][:, 0:2 * MAXBLK], place_hot[0:r, a, :],
                                        block_value[0:r, a].rearrange("p o n -> p (o n)"), start=(a == 0), stop=(a == N_ASG - 1))
            last.then_inc(rows_psum, 1)
            pe.wait_ge(rows_ready, 1)
            m = blocks_but_three(pe) + 1
            turn_x(0)
            gate_up(0)
            turn_x(1)
            turn_hid(0)
            with pe.Fori(1, m + 1) as i:
                gate_up(i)
                turn_x(i + 1)
                down(i - 1)
                turn_hid(i)
            gate_up(m + 1)
            down(m)
            turn_hid(m + 1)
            down(m + 1)

        @block.scalar
        def _(act):
            def high_gate_up(i, pieces):
                for p in pieces:
                    act.wait_ge(gate_up_loaded[p], i * 32 + 32)
                    wait(act, gu_used, i * 4 + (p - 3))
                    s = slice(2 * p, 2 * p + 2)
                    nc.scalar.copy(wg_h[:, s, :], wg[:, s, :])
                    nc.scalar.copy(wu_h[:, s, :], wu[:, s, :]).then_inc(gu_high, 1)

            def high_down(i):
                for p in range(4):
                    act.wait_ge(down_loaded[p], i * 16 + 16)
                    wait(act, down_used, i * 4 + (p - 3))
                    nc.scalar.copy(wd_h[:, p, :], wd[:, p, :]).then_inc(down_high, 1)

            def high_x(i):
                for half in range(2):
                    act.wait_ge(xT_psum, i * 2 + (half + 1))
                    wait(act, gu_used, i * 4)
                    nc.scalar.copy(xh[:, 4 * half:4 * half + 4, :], bank[4 + half][:].rearrange("p (k t) -> p k t", k=4)).then_inc(x_high, 1)

            def silu(i):
                act.wait_ge(gu_used, i * 4 + 4)
                wait(act, hid_ready, i)
                nc.scalar.activation(act_g[:], bank[0][:, :], ACT.Silu).then_inc(silu_done, 1)

            def high_hid(i):
                act.wait_ge(hT_psum, i + 1)
                wait(act, down_used, i * 4)
                nc.scalar.copy(hT_h[:], bank[6][:].rearrange("p (k t) -> p k t", k=4)).then_inc(h_high, 1)

            m = blocks_but_three(act) + 1
            high_x(0)
            high_gate_up(0, range(4))

            def block_of(i):
                high_gate_up(i + 1, range(3))
                silu(i)
                high_x(i + 1)
                high_gate_up(i + 1, range(3, 4))
                high_down(i)
                high_hid(i)

            block_of(0)
            with act.Fori(1, m + 1) as i:
                block_of(i)
            silu(m + 1)
            high_down(m + 1)
            high_hid(m + 1)

        @block.vector
        def _(dve):
            links = [0]

            def after(ins):
                links[0] += 1
                then_own(dve, ins, chain, links[0])

            after(nc.vector.tensor_tensor(over[:], S["run"][:].unsqueeze(2).to_broadcast([P, E, NT + 1]),
                                          C["row_step"][:].unsqueeze(1).to_broadcast([P, E, NT + 1]), ALU.is_gt))
            after(nc.vector.tensor_reduce(n_blk[:], over[:], AX.X, ALU.add))
            after(nc.vector.tensor_tensor_scan(blk_end[:], C["ones"][:, 0:E], n_blk[:], 0.0, ALU.mult, ALU.add))
            after(nc.vector.tensor_tensor(row0[:], blk_end[:], n_blk[:], ALU.subtract))
            after(nc.vector.tensor_scalar(row0[:], row0[:], float(P), None, ALU.mult))
            after(nc.vector.tensor_tensor(before_end[:], blk_end[0:1, :].unsqueeze(1).to_broadcast([1, MAXBLK, E]),
                                          C["block_no"][:].unsqueeze(2).to_broadcast([1, MAXBLK, E]), ALU.is_le))
            after(nc.vector.tensor_reduce(blk_f[:, 0:MAXBLK], before_end[:], AX.X, ALU.add))
            after(nc.vector.tensor_scalar(blk_f[:, 0:MAXBLK], blk_f[:, 0:MAXBLK], float(E - 1), None, ALU.min))
            after(nc.vector.tensor_scalar(blk_f[:, MAXBLK:], blk_end[0:1, E - 1:E], -3.0, None, ALU.add))
            nc.vector.tensor_copy(blk_i[:], blk_f[:]).then_inc(table_ready, 1)
            after(nc.vector.tensor_tensor(S["before"][:], S["before"][:], row0[:].unsqueeze(1).to_broadcast([P, NT + 1, E]), ALU.add))
            for k in range(2):
                after(nc.vector.tensor_tensor(place[:, :, k, :], S["before"][:], S["hot"][:, :, k, :], ALU.mult))
            after(nc.vector.tensor_reduce(row_f[:], place[:], AX.X, ALU.add))
            row = row_f[:].rearrange("p t k -> p (t k)")
            after(nc.vector.tensor_tensor(at_or_past[:], row.unsqueeze(2).to_broadcast([P, N_ASG, MAXBLK + 1]),
                                          C["block_row"][:].unsqueeze(1).to_broadcast([P, N_ASG, MAXBLK + 1]), ALU.is_ge))
            after(nc.vector.tensor_reduce(of_block[:], at_or_past[:, :, 1:], AX.X, ALU.add))
            after(nc.vector.scalar_tensor_tensor(out=in_block[:], in0=of_block[:], scalar=-float(P), in1=row,
                                                 op0=ALU.mult, op1=ALU.add))
            after(nc.vector.tensor_tensor(place_hot, C["column_no"][:].unsqueeze(1).to_broadcast([P, N_ASG, P]),
                                          in_block[:].unsqueeze(2).to_broadcast([P, N_ASG, P]), ALU.is_equal))
            after(nc.vector.tensor_tensor(at_or_past[:, :, 0:MAXBLK], at_or_past[:, :, 0:MAXBLK], at_or_past[:, :, 1:],
                                          ALU.subtract))
            for o in range(2):
                ins = nc.vector.tensor_tensor(block_value[:, :, o, :], at_or_past[:, :, 0:MAXBLK],
                                              C["token_slot"][:, :, o:o + 1].to_broadcast([P, N_ASG, MAXBLK]), ALU.mult)
            ins.then_inc(table_ready, 1)
            dve.wait_ge(rows_psum, 1)
            got = bank[0][:, 0:2 * MAXBLK].rearrange("p (o n) -> p o n", o=2)
            for o in range(2):
                after(nc.vector.tensor_scalar(of_row_f[:, o, :], got[:, o, :], float((1 + o) * T), None, ALU.add))
            nc.vector.tensor_copy(of_row[:], of_row_f[:]).then_inc(rows_ready, 1)

            def gated(i):
                dve.wait_ge(silu_done, i + 1)
                wait(dve, hT_psum, i)
                nc.vector.tensor_tensor(hid[:], act_g[:], bank[1][:, :], ALU.mult).then_inc(hid_ready, 1)

            def unload_y(i):
                wait(dve, y_stored, i * 16)
                dve.wait_ge(down_used, i * 4 + 4)
                for n in range(2):
                    nc.vector.tensor_copy(yb[:, n * 512:(n + 1) * 512], bank[2 + n][:, :]).then_inc(y_done, 1)

            def low_gate_up(i, pieces):
                for p in pieces:
                    dve.wait_ge(gu_high, i * 4 + (p + 1))
                    s = slice(2 * p, 2 * p + 2)
                    nc.vector.tensor_tensor(wg_l[:, s, :], wg[:, s, :], wg_h[:, s, :].bitcast(F32), ALU.subtract)
                    nc.vector.tensor_tensor(wu_l[:, s, :], wu[:, s, :], wu_h[:, s, :].bitcast(F32), ALU.subtract).then_inc(gu_split, 1)

            def low_x(i):
                for half in range(2):
                    dve.wait_ge(x_high, i * 2 + (half + 1))
                    s = slice(4 * half, 4 * half + 4)
                    nc.vector.tensor_tensor(xl[:, s, :], bank[4 + half][:].rearrange("p (k t) -> p k t", k=4),
                                            xh[:, s, :].bitcast(F32), ALU.subtract).then_inc(xT_done, 1)

            def low_hid(i):
                dve.wait_ge(h_high, i + 1)
                nc.vector.tensor_tensor(hT_l[:], bank[6][:].rearrange("p (k t) -> p k t", k=4), hT_h[:].bitcast(F32),
                                        ALU.subtract).then_inc(hT_done, 1)

            m = blocks_but_three(dve) + 1
            low_x(0)
            low_gate_up(0, range(4))

            def block_of(i, first=False):
                low_gate_up(i + 1, range(3))
                gated(i)
                low_x(i + 1)
                low_gate_up(i + 1, range(3, 4))
                if not first:
                    unload_y(i - 1)
                low_hid(i)

            block_of(0, first=True)
            with dve.Fori(1, m + 1) as i:
                block_of(i)
            gated(m + 1)
            unload_y(m)
            low_hid(m + 1)
            unload_y(m + 1)


def combine(nc, A, S, C):
    with ExitStack() as ctx:
        def sb(name, shape, dt=F32):
            return ctx.enter_context(nc.sbuf_tensor(name, shape, dt))

        def sem(name):
            return ctx.enter_context(nc.semaphore(name))

        B = 2
        yy = [sb(f"yy{j}", [P, 2, D]) for j in range(B)]
        h = [sb(f"hf{j}", [P, D]) for j in range(B)]
        junk, w = sb("junkf", [P, D]), sb("w_final", [P, D])
        st = sb("st_f", [P, 4])
        w_loaded = sem("wf_loaded")
        y_loaded = [sem(f"yf_loaded{j}") for j in range(B)]
        h_loaded = [sem(f"hf_loaded{j}") for j in range(B)]
        out_stored = [sem(f"out_stored{j}") for j in range(B)]
        part, summed, squared, rms, rinv, out_ready = (sem(n) for n in ("part", "summed", "squared", "rms", "rinv", "out_ready"))

        block = ctx.enter_context(nc.Block())

        @block.sync
        def _(sp):
            sp.dma_start(w[:], A["norm_final_w"][0].partition_broadcast(P)).then_inc(w_loaded, 16)

            def load(t, j, at):
                r = rows_of(t)
                wait(sp, out_stored[j], at)
                sp.dma_start(h[j][0:r, :], S["h"][bass.ds(t * P, r), :]).then_inc(h_loaded[j], 16)
                sp.dma_start(yy[j][0:r], S["picked"].rearrange("(t k) d -> t k d", k=2)[bass.ds(t * P, r)]).then_inc(y_loaded[j], 16)

            def store(t, j):
                r = rows_of(t)
                sp.wait_ge(out_ready, t + 1)
                dst = A["y_sample"] if r == TS else A["y_prompt"][bass.ds(t * P, r), :]
                sp.dma_start(dst, h[j][0:r, :]).then_inc(out_stored[j], 16)

            load(0, 0, 0)
            load(1, 1, 0)
            with sp.Fori(1, NT // 2) as a:
                for j in range(2):
                    store(a * 2 + (j - 2), j)
                    load(a * 2 + j, j, a * 16)
            store(NT - 2, 0)
            load(NT, 0, 16 * (NT // 2))
            store(NT - 1, 1)
            store(NT, 0)
            sp.wait_ge(out_stored[0], 16 * (NT // 2 + 1))
            sp.wait_ge(out_stored[1], 16 * (NT // 2))

        @block.scalar
        def _(act):
            def stats(t, j):
                r = rows_of(t)
                act.wait_ge(summed, t + 1)
                wait(act, out_ready, t)
                then_own(act, nc.scalar.activation(junk[0:r, :], h[j][0:r, :], ACT.Square, accum_out=st[0:r, 0:1]), squared, t + 1)
                nc.scalar.activation(st[0:r, 1:2], st[0:r, 0:1], ACT.Sqrt, bias=C["eps"][0:r, :], scale=1.0 / D).then_inc(rms, 1)

            stats(0, 0)
            stats(1, 1)
            with act.Fori(1, NT // 2) as a:
                stats(a * 2, 0)
                stats(a * 2 + 1, 1)
            stats(NT, 0)

        @block.vector
        def _(dve):
            def tile(t, j, a):
                r = rows_of(t)
                dve.wait_ge(y_loaded[j], a * 16 + 16)
                g = S["gate"]
                nc.vector.tensor_scalar(yy[j][0:r, 0, :], yy[j][0:r, 0, :], g[0:r, bass.ds(t, 1), 0:1].rearrange("p a b -> p (a b)"),
                                        None, ALU.mult).then_inc(part, 1)
                dve.wait_ge(part, t * 2 + 1)
                nc.vector.scalar_tensor_tensor(out=yy[j][0:r, 1, :], in0=yy[j][0:r, 1, :],
                                               scalar=g[0:r, bass.ds(t, 1), 1:2].rearrange("p a b -> p (a b)"),
                                               in1=yy[j][0:r, 0, :], op0=ALU.mult, op1=ALU.add).then_inc(part, 1)
                dve.wait_ge(part, t * 2 + 2)
                dve.wait_ge(h_loaded[j], a * 16 + 16)
                nc.vector.tensor_tensor(h[j][0:r, :], h[j][0:r, :], yy[j][0:r, 1, :], ALU.add).then_inc(summed, 1)
                dve.wait_ge(rms, t + 1)
                then_own(dve, nc.vector.reciprocal(st[0:r, 2:3], st[0:r, 1:2]), rinv, t + 1)
                nc.vector.scalar_tensor_tensor(out=h[j][0:r, :], in0=h[j][0:r, :], scalar=st[0:r, 2:3], in1=w[0:r, :],
                                               op0=ALU.mult, op1=ALU.mult).then_inc(out_ready, 1)

            dve.wait_ge(w_loaded, 16)
            tile(0, 0, 0)
            tile(1, 1, 0)
            with dve.Fori(1, NT // 2) as a:
                tile(a * 2, 0, a)
                tile(a * 2 + 1, 1, a)
            tile(NT, 0, NT // 2)


OUTPUTS = {
    "y_prompt": (SEQ, D), "y_sample": (TS, D), "conv_tail": (P, CT_N, DEC_B + 1, CONV_K - 1),
    "ssm_prompt": (NSTATE, D), "ssm_sample": (DEC_B, NSTATE, D), "sg_v_sample": (TS, D),
}
SCRATCH = {
    "z": (T, D), "xb": (T, D + GROUPS * NSTATE), "bct": (2 * GROUPS * NSTATE, T), "uT": (D, T), "v": (T, D),
    "h": (T, D), "hn": (T, D), "picked": (2 * T, D),
}


def program(nc, A, S):
    with ExitStack() as ctx:
        def sb(name, shape, dt=F32):
            return ctx.enter_context(nc.sbuf_tensor(name, shape, dt))

        C = {
            "ident": sb("ident", [P, P]), "eps": sb("eps", [P, 1]), "ones": sb("ones", [P, P]), "le": sb("le", [P, P]),
            "lt": sb("lt", [P, P]), "gt": sb("gt", [P, P]), "same": sb("same", [TS, TS]),
            "of_seq": sb("of_seq", [P, DEC_B, TS]), "repeat": sb("repeat", [DEC_S, TS]),
            "expert_no": sb("expert_no", [P, E]), "row_step": sb("row_step", [P, NT + 1]),
            "block_no": sb("block_no", [1, MAXBLK]), "token_slot": sb("token_slot", [P, 2 * (NT + 1), 2]),
            "block_row": sb("block_row", [P, MAXBLK + 1]), "column_no": sb("column_no", [P, P]),
            "const_made": ctx.enter_context(nc.semaphore("const_made")), "holder": ctx.enter_context(nc.semaphore("holder")),
        }
        S["dtk"] = sb("dtk", [P, NT + 1, 2 * HEADS])
        bank = [ctx.enter_context(nc.psum_tensor(f"bank{b}", [P, 512], F32)) for b in range(8)]
        S["gate"] = sb("gate", [P, NT + 1, 2])
        S["hot"] = sb("hot", [P, NT + 1, 2, E])
        S["before"] = sb("before", [P, NT + 1, E])
        S["run"] = sb("run", [P, E])
        S["w_out_loaded"] = ctx.enter_context(nc.semaphore("w_out_loaded"))
        with nc.sbuf_tensor("w_out_sg", [P, KT, D], F32) as w_out_sg:
            S["w_out_sg"] = w_out_sg
            projections(nc, A, S, C, bank)
            mixer(nc, A, S, C, bank)
        experts(nc, A, S, C, bank)
        combine(nc, A, S, C)


def laid_out(np, x_prompt, x_sample, state_conv, state_ssm, norm_mix_w, w_in, conv_w, conv_b, dt_bias, a_log, d_skip,
             ssm_norm_w, sg_norm_w, sg_w, sg_b, w_out, norm_ffn_w, w_router_group, b_router_group, w_router_expert,
             b_router_expert, w_gate, w_up, w_down, norm_final_w):
    w = w_in[0]
    columns = np.concatenate([w[:, :COL_DT], w[:, COL_U:]], axis=1)
    return {
        "x_prompt": x_prompt, "x_sample": x_sample,
        "state_conv": state_conv[0].reshape(DEC_B, CONV_K - 1, CT_N, P).transpose(3, 2, 0, 1),
        "state_ssm": state_ssm[0].reshape(DEC_B, D, NSTATE).transpose(0, 2, 1),
        "norm_mix_w": norm_mix_w[0].reshape(KT, P).T,
        "w_in_tiles": columns.reshape(KT, P, M_END, P).transpose(2, 1, 0, 3),
        "w_dt": w[:, COL_DT:COL_U].reshape(KT, P, HEADS).transpose(1, 0, 2),
        "conv_w": conv_w[0].reshape(CONV_K, CT_N, P).transpose(2, 0, 1),
        "conv_b": conv_b[0].reshape(CT_N, P).T,
        "dt_bias": dt_bias.T, "a_log": a_log.T, "d_skip": d_skip, "ssm_norm_w": ssm_norm_w, "sg_norm_w": sg_norm_w,
        "sg_w": sg_w[0].transpose(2, 0, 1), "sg_b": sg_b,
        "w_out": w_out[0].reshape(2 * KT, P, D).transpose(1, 0, 2), "norm_ffn_w": norm_ffn_w,
        "w_router": np.concatenate([w_router_group[0], w_router_expert[0]], axis=1).reshape(KT, P, EG + E).transpose(1, 0, 2),
        "b_router": np.concatenate([b_router_group, b_router_expert], axis=1),
        "w_gate": w_gate[0], "w_up": w_up[0], "w_down": w_down[0], "norm_final_w": norm_final_w[None],
    }


def kernel(**inputs):
    import numpy as _np
    import concourse.bacc as _bacc
    from concourse import mybir as _mybir
    from concourse.bass_utils import run_bass_kernel_spmd as _run

    nc = _bacc.Bacc("TRN2", target_bir_lowering=False, num_devices=1)
    arrays, A = {}, {}
    for name, a in laid_out(_np, **inputs).items():
        arrays[f"in_{name}"] = _np.ascontiguousarray(a)
        A[name] = nc.dram_tensor(f"in_{name}", a.shape, _mybir.dt.from_np(a.dtype), kind="ExternalInput").ap()
    for name, shape in OUTPUTS.items():
        A[name] = nc.dram_tensor(f"out_{name}", shape, F32, kind="ExternalOutput").ap()
    S = {name: nc.dram_tensor(f"scratch_{name}", shape, F32, kind='Internal').ap() for name, shape in SCRATCH.items()}
    program(nc, A, S)
    r = _run(nc, [arrays], core_ids=[0])
    got = {name: r.results[0][f"out_{name}"] for name in OUTPUTS}
    tail = got["conv_tail"].transpose(2, 3, 1, 0).reshape(1, DEC_B + 1, CONV_K - 1, C_CONV)
    state = (GROUPS, HEADS // GROUPS, HD, NSTATE)
    return (got["y_prompt"].reshape(1, SEQ, D), got["y_sample"].reshape(DEC_B, DEC_S, D), tail[:, 0:1],
            got["ssm_prompt"].T.reshape(1, 1, *state), tail[:, 1:],
            got["ssm_sample"].transpose(0, 2, 1).reshape(1, DEC_B, *state),
            got["sg_v_sample"].reshape(1, DEC_B, DEC_S, D))
```

```python
from contextlib import ExitStack

import concourse.bass as bass
from concourse import mybir

ALU = mybir.AluOpType
ACT = mybir.ActivationFunctionType
AX = mybir.AxisListType
F32 = mybir.dt.float32
I32 = mybir.dt.int32
U32 = mybir.dt.uint32
F32R = mybir.dt.float32r

P = 128
D = 1024
KT = D // P
SEQ = 1024
DEC_B, DEC_S = 8, 4
TS = DEC_B * DEC_S
T = SEQ + TS
NT = SEQ // P
HEADS, HD, NSTATE, GROUPS = 16, 64, 128, 2
CONV_K = 4
C_CONV = D + 2 * GROUPS * NSTATE
SGH = 8
E, EG, EPG = 32, 4, 8
FF = D // 2
EPS = 1e-6
MAXBLK = -(-2 * T // P) + E
MINBLK = -(-2 * T // P)

COL_Z, COL_X, COL_DT, COL_U = 0, D, D + C_CONV, D + C_CONV + HEADS
M_X, M_B, M_C, M_U, M_V, M_END = 8, 16, 18, 20, 28, 36
NB3 = 3
TB = T // NB3
CT_N = M_U - M_X


def wait(eng, sem, value):
    if not (isinstance(value, int) and value <= 0):
        eng.wait_ge(sem, value)


def then_own(eng, ins, sem, value):
    ins.then_inc(sem, 1)
    eng.wait_ge(sem, value)


def rows_of(t):
    return TS if isinstance(t, int) and t == NT else P


def split_product(nc, acc, parts_l, parts_r, start, stop):
    (lh, ll), (rh, rl) = parts_l, parts_r
    nc.tensor.matmul(acc, lh, rh, start=start, stop=False)
    nc.tensor.matmul(acc, lh, rl, start=False, stop=False)
    return nc.tensor.matmul(acc, ll, rh, start=False, stop=stop)


def make_constants(nc, pool, C):
    made = [0]

    def done(ins):
        made[0] += 1
        ins.then_inc(C["const_made"], 1)

    def after(ins):
        done(ins)
        pool.wait_ge(C["const_made"], made[0])

    def select(t, pattern, base, mult, op=ALU.is_ge, fill=0.0):
        after(nc.gpsimd.affine_select(out=t, in_=t, compare_op=op, fill=fill, base=base, pattern=pattern,
                                      channel_multiplier=mult))

    after(nc.gpsimd.memset(C["ident"][:], 0.0))
    select(C["ident"][:], [[-1, P]], 0, 1, ALU.not_equal, 1.0)
    done(nc.gpsimd.memset(C["eps"][:], EPS))
    done(nc.gpsimd.memset(C["ones"][:], 1.0))
    for name, step, mult, op in (("le", 1, -1, ALU.is_ge), ("lt", 1, -1, ALU.is_gt), ("gt", -1, 1, ALU.is_gt)):
        after(nc.gpsimd.memset(C[name][:], 1.0))
        select(C[name][:], [[step, P]], 0, mult, op)
    after(nc.gpsimd.memset(C["same"][:], 1.0))
    v = C["same"][:].rearrange("p (b s) -> p b s", s=DEC_S)
    select(v, [[-DEC_S, DEC_B], [0, DEC_S]], 0, 1)
    select(v, [[DEC_S, DEC_B], [0, DEC_S]], DEC_S - 1, -1)
    after(nc.gpsimd.memset(C["of_seq"][:], 1.0))
    select(C["of_seq"][:], [[-DEC_S, DEC_B], [1, TS]], 0, 0)
    select(C["of_seq"][:], [[DEC_S, DEC_B], [-1, TS]], DEC_S - 1, 0)
    after(nc.gpsimd.memset(C["repeat"][:], 0.0))
    select(C["repeat"][:].rearrange("p (b s) -> p b s", s=DEC_S), [[0, DEC_B], [-1, DEC_S]], 0, 1, ALU.not_equal, 1.0)
    done(nc.gpsimd.iota(C["expert_no"][:], [[1, E]], base=0, channel_multiplier=0, allow_small_or_imprecise_dtypes=True))
    done(nc.gpsimd.iota(C["row_step"][:], [[P, NT + 1]], base=0, channel_multiplier=0, allow_small_or_imprecise_dtypes=True))
    done(nc.gpsimd.iota(C["row_no"][:], [[0, 1]], base=0, channel_multiplier=1, allow_small_or_imprecise_dtypes=True))
    done(nc.gpsimd.iota(C["block_row"][:], [[P, MAXBLK + 1]], base=0, channel_multiplier=0, allow_small_or_imprecise_dtypes=True))
    done(nc.gpsimd.iota(C["column_no"][:], [[1, P]], base=0, channel_multiplier=0, allow_small_or_imprecise_dtypes=True))
    for o, pattern in enumerate(([[P, NT + 1], [0, 2]], [[2 * P, NT + 1], [1, 2]])):
        done(nc.gpsimd.iota(C["token_slot"][:, :, o].rearrange("p (t k) -> p t k", k=2), pattern, base=-(1 + o) * T,
                            channel_multiplier=1 + o, allow_small_or_imprecise_dtypes=True))
    assert made[0] == N_CONST


N_CONST = 25


def projections(nc, A, S, C, bank):
    with ExitStack() as ctx:
        def sb(name, shape, dt=F32):
            return ctx.enter_context(nc.sbuf_tensor(name, shape, dt))

        def sem(name):
            return ctx.enter_context(nc.semaphore(name))

        work = sb("work", [P, 6 * T])
        XB = 3
        xin = [work[:, j * D:(j + 1) * D] for j in range(XB)]
        xn = [work[:, (XB + j) * D:(XB + 1 + j) * D] for j in range(2)]
        x32 = [work[:, 5 * D + j * 512:5 * D + (j + 1) * 512].rearrange("p (k t) -> p k t", k=4) for j in range(2)]
        dtw = work[0:HEADS, :].rearrange("p (a t) -> p a t", a=6)
        stat = [sb(f"stat{j}", [P, 4]) for j in range(2)]
        xh, xl = sb("xh", [P, KT, T], F32R), sb("xl", [P, KT, T], F32R)
        w = [sb(f"w{j}", [P, KT, P]) for j in range(2)]
        wh = [sb(f"wh{j}", [P, KT, P], F32R) for j in range(2)]
        wl = [sb(f"wl{j}", [P, KT, P], F32R) for j in range(2)]
        feat = [sb(f"feat{j}", [P, T]) for j in range(2)]
        raw = [sb(f"raw{j}", [P, 3 + SEQ + 1 + DEC_B * 7]) for j in range(2)]
        conv = [sb(f"conv{j}", [P, T]) for j in range(2)]
        stage = [sb(f"stage{j}", [P, NT + 1, P]) for j in range(2)]
        old_conv = sb("old_conv", [P, CT_N, DEC_B, CONV_K - 1])
        tail = sb("tail", [P, CT_N, DEC_B + 1, CONV_K - 1])
        w_dt = sb("w_dt", [P, KT, HEADS])
        w_dt_h, w_dt_l = sb("w_dt_h", [P, KT, HEADS], F32R), sb("w_dt_l", [P, KT, HEADS], F32R)
        nmw = sb("nmw", [P, KT])
        cw = sb("cw", [P, CONV_K, CT_N])
        cb = sb("cb", [P, CT_N])
        hcol = sb("hcol", [HEADS, 4])

        prompt_raw = [raw[j][:, 0:3 + SEQ] for j in range(2)]
        sample_raw = [raw[j][:, 4 + SEQ:4 + SEQ + DEC_B * 7].rearrange("p (b s) -> p b s", s=7) for j in range(2)]

        setup_loaded, nmw_loaded = sem("setup_loaded"), sem("nmw_loaded")
        x_loaded = [sem(f"x_loaded{j}") for j in range(XB)]
        x_squared, x_rms, x_rinv, x_normed = sem("x_squared"), sem("x_rms"), sem("x_rinv"), sem("x_normed")
        xT_psum, x_scaled, x_high, xT_done = sem("xT_psum"), sem("x_scaled"), sem("x_high"), sem("xT_done")
        w_high, w_split, w_dt_high, w_dt_split = sem("w_high"), sem("w_split"), sem("w_dt_high"), sem("w_dt_split")
        w_loaded = [sem(f"w_loaded{j}") for j in range(2)]
        acc_ready, acc_free = sem("acc_ready"), sem("acc_free")
        feat_ready = sem("feat_ready")
        feat_stored = [sem(f"feat_stored{j}") for j in range(2)]
        tr_psum, tr_free, stage_ready = sem("tr_psum"), sem("tr_free"), sem("stage_ready")
        stage_stored = [sem(f"stage_stored{j}") for j in range(2)]
        raw_ready, conv_chain, conv_done = sem("raw_ready"), sem("conv_chain"), sem("conv_done")
        tail_ready, tail_stored = sem("tail_ready"), sem("tail_stored")
        dt_act, dt_chain, dt_ready, dt_psum = sem("dt_act"), sem("dt_chain"), sem("dt_ready"), sem("dt_psum")
        side_writes = sem("side_writes")

        xp = A["x_prompt"][0]
        xs = A["x_sample"].rearrange("b s d -> (b s) d")
        N_SETUP = 6

        block = ctx.enter_context(nc.Block())

        @block.sync
        def _(sp):
            def load_w(m, j):
                sp.dma_start(w[j][:], A["w_in_tiles"][bass.ds(m, 1)].rearrange("m p k c -> (m p) k c")).then_inc(w_loaded[j], 16)

            def load_x(t):
                r = rows_of(t)
                src = xs if r == TS else xp[t * P:(t + 1) * P, :]
                sp.dma_start(xin[t % XB][0:r, :], src).then_inc(x_loaded[t % XB], 16)

            for t in range(XB):
                load_x(t)
            sp.dma_start(nmw[:], A["norm_mix_w"]).then_inc(nmw_loaded, 16)
            load_w(0, 0)
            load_w(1, 1)
            for dst, name in ((cw, "conv_w"), (cb, "conv_b"), (old_conv, "state_conv"), (w_dt, "w_dt")):
                sp.dma_start(dst[:], A[name]).then_inc(setup_loaded, 16)
            sp.dma_start(hcol[:, 0:1], A["dt_bias"]).then_inc(setup_loaded, 16)
            sp.dma_start(hcol[:, 1:2], A["a_log"]).then_inc(setup_loaded, 16)

            for t in range(XB, NT + 1):
                sp.wait_ge(x_normed, t - XB + 1)
                load_x(t)

            with sp.Fori(1, M_END // 2) as a:
                for j in range(2):
                    sp.wait_ge(w_split, a * 2 + (j - 1))
                    load_w(a * 2 + j, j)
            for dst, src in ((S["sg_w_row"], A["sg_norm_w"][0].partition_broadcast(P)), (S["sgWT"], A["sg_w"]),
                             (S["sgb"], A["sg_b"][0].partition_broadcast(P)), (S["d_skip"], A["d_skip"][0].partition_broadcast(P))):
                sp.dma_start(dst[:], src).then_inc(S["consts_loaded"], 16)
            sp.dma_start(S["w_out_sg"][:], A["w_out"][:, KT:, :]).then_inc(S["w_out_loaded"], 16)

        @block.tensor
        def _(pe):
            def turn_x(t):
                r = rows_of(t)
                pe.wait_ge(x_normed, t + 1)
                for h in range(2):
                    wait(pe, x_scaled, t * 2 + (h - 1))
                    for q in range(4):
                        k = 4 * h + q
                        last = nc.tensor.transpose(bank[6 + h][:, q * P:q * P + r], xn[t % 2][0:r, k * P:(k + 1) * P],
                                                   C["ident"][0:r, 0:r])
                    last.then_inc(xT_psum, 1)

            def products(n, m, j, banks=range(NB3)):
                pe.wait_ge(w_split, m + 1)
                for b in banks:
                    wait(pe, acc_free, n * 3 + (b - 2))
                    cols = slice(b * TB, (b + 1) * TB)
                    for k in range(KT):
                        last = split_product(nc, bank[b][:, 0:TB], (wh[j][:, k, :], wl[j][:, k, :]), (xh[:, k, cols], xl[:, k, cols]),
                                             start=(k == 0), stop=(k == KT - 1))
                    last.then_inc(acc_ready, 1)

            def turn(q, m, j):
                pe.wait_ge(feat_ready, m + 1)
                for g in range(3):
                    wait(pe, tr_free, q * 3 + (g - 2))
                    for s in range(4 if g < 2 else 1):
                        t = 4 * g + s
                        r = P if t < NT else TS
                        last = nc.tensor.transpose(bank[3 + g][0:r, s * P:(s + 1) * P], feat[j][:, t * P:t * P + r],
                                                   C["ident"][:])
                    last.then_inc(tr_psum, 1)

            pe.wait_ge(C["const_made"], N_CONST)
            for t in range(NT + 1):
                turn_x(t)
                for b in range(NB3):
                    last_tile = -(-(b + 1) * TB // P) - 1
                    if t == min(last_tile + 2, NT):
                        pe.wait_ge(xT_done, 2 * (last_tile + 1))
                        products(0, 0, 0, (b,))
            products(1, 1, 1)
            turn(0, 0, 0)
            products(2, 2, 0)
            turn(1, 1, 1)
            with pe.Fori(1, M_C // 2) as a:
                products(a * 2 + 1, a * 2 + 1, 1)
                turn(a * 2, a * 2, 0)
                products(a * 2 + 2, a * 2 + 2, 0)
                turn(a * 2 + 1, a * 2 + 1, 1)
            products(M_C + 1, M_C + 1, 1)
            pe.wait_ge(w_dt_split, 1)
            for b in range(NB3):
                pe.wait_ge(acc_free, 3 * M_U + b - 2)
                cols = slice(b * TB, (b + 1) * TB)
                for k in range(KT):
                    last = split_product(nc, bank[b][0:HEADS, 0:TB], (w_dt_h[:, k, :], w_dt_l[:, k, :]),
                                         (xh[:, k, cols], xl[:, k, cols]), start=(k == 0), stop=(k == KT - 1))
                last.then_inc(acc_ready, 1)
            with pe.Fori(M_U // 2, M_V // 2) as a:
                products(a * 2 + 1, a * 2, 0)
                products(a * 2 + 2, a * 2 + 1, 1)
            products(M_V + 1, M_V, 0)
            pe.wait_ge(dt_ready, 1)
            for t in range(NT + 1):
                r = P if t < NT else TS
                nc.tensor.transpose(bank[6][0:r, 32 * t:32 * t + 16], dtw[:, 4, t * P:t * P + r], C["ident"][0:16, 0:16])
                last = nc.tensor.transpose(bank[6][0:r, 32 * t + 16:32 * t + 32], dtw[:, 5, t * P:t * P + r],
                                           C["ident"][0:16, 0:16])
            last.then_inc(dt_psum, 1)
            with pe.Fori(M_V // 2, M_END // 2 - 1) as a:
                products(a * 2 + 2, a * 2 + 1, 1)
                turn(a * 2 - (M_V - M_C), a * 2, 0)
                products(a * 2 + 3, a * 2 + 2, 0)
                turn(a * 2 + (1 - M_V + M_C), a * 2 + 1, 1)
            products(M_END, M_END - 1, 1)
            turn(M_END - 2 - (M_V - M_C), M_END - 2, 0)
            turn(M_END - 1 - (M_V - M_C), M_END - 1, 1)

        @block.scalar
        def _(act):
            def norm_stats(t):
                r, j = rows_of(t), t % 2
                act.wait_ge(x_loaded[t % XB], 16 * (t // XB + 1))
                wait(act, x_normed, t - 1)
                wait(act, xT_psum, 2 * (t - 1))
                then_own(act, nc.scalar.activation(xn[j][0:r, :], xin[t % XB][0:r, :], ACT.Square, accum_out=stat[j][0:r, 0:1]),
                         x_squared, t + 1)
                nc.scalar.activation(stat[j][0:r, 1:2], stat[j][0:r, 0:1], ACT.Sqrt, bias=C["eps"][0:r, :],
                                     scale=1.0 / D).then_inc(x_rms, 1)

            act.wait_ge(C["const_made"], N_CONST)
            def high_x(t):
                r = rows_of(t)
                for h in range(2):
                    act.wait_ge(x_scaled, t * 2 + (h + 1))
                    nc.scalar.copy(xh[:, 4 * h:4 * h + 4, bass.ds(t * P, r)], x32[h][:, :, 0:r]).then_inc(x_high, 1)

            def high_w(j, at):
                act.wait_ge(w_loaded[j], at)
                nc.scalar.copy(wh[j][:], w[j][:]).then_inc(w_high, 1)

            norm_stats(0)
            norm_stats(1)
            high_w(0, 16)
            for t in range(2, NT + 1):
                norm_stats(t)
                high_x(t - 2)
            high_x(NT - 1)
            high_w(1, 16)
            high_x(NT)

            def activate(n, m, j, func):
                for b in range(NB3):
                    act.wait_ge(acc_ready, n * 3 + (b + 1))
                    ins = nc.scalar.activation(feat[j][:, b * TB:(b + 1) * TB], bank[b][:, 0:TB], func)
                    ins.then_inc(acc_free, 1)
                act.wait_ge(acc_free, n * 3 + 3)
                nc.scalar.sem_inc(feat_ready, 1)

            def to_conv(m, j, at):
                for b in range(NB3):
                    act.wait_ge(acc_ready, m * 3 + (b + 1))
                    if b < 2:
                        nc.scalar.copy(raw[j][:, 3 + b * TB:3 + (b + 1) * TB], bank[b][:, 0:TB]).then_inc(acc_free, 1)
                    else:
                        nc.scalar.copy(raw[j][:, 3 + 2 * TB:3 + SEQ], bank[b][:, 0:SEQ - 2 * TB]).then_inc(raw_ready, 1)
                        nc.scalar.copy(sample_raw[j][:, :, 3:7],
                                       bank[b][:, SEQ - 2 * TB:TB].rearrange("p (b s) -> p b s", s=DEC_S)).then_inc(acc_free, 1)
                high_w(j, at)
                act.wait_ge(conv_done, m - (M_X - 1))

            def silu_conv(m, j):
                nc.scalar.activation(feat[j][:], conv[j][:], ACT.Silu, bias=cb[:, bass.ds(m - M_X, 1)]).then_inc(feat_ready, 1)

            for m in (0, 1):
                activate(m, m, m, ACT.Silu)
                high_w(m, 32)
            with act.Fori(1, M_X // 2) as a:
                for j in range(2):
                    act.wait_ge(tr_psum, a * 6 + (3 * j - 3))
                    activate(a * 2 + j, a * 2 + j, j, ACT.Silu)
                    high_w(j, a * 16 + 32)
            act.wait_ge(setup_loaded, 16 * N_SETUP)
            nc.scalar.copy(w_dt_h[:], w_dt[:]).then_inc(w_dt_high, 1)
            for c in (0, 1):
                m = M_X + c
                to_conv(m, c, 16 * (M_X // 2 + 2))
                act.wait_ge(tr_psum, 3 * (m - 1))
                silu_conv(m, c)
            with act.Fori(M_X // 2 + 1, M_C // 2) as a:
                for j in range(2):
                    act.wait_ge(conv_done, a * 2 + (j - M_X - 1))
                    act.wait_ge(tail_ready, a * 4 + 2 * (j - M_X - 1))
                    to_conv(a * 2 + j, j, a * 16 + 32)
                    act.wait_ge(tr_psum, a * 6 + (3 * j - 3))
                    silu_conv(a * 2 + j, j)
            for m in (M_C, M_C + 1):
                act.wait_ge(conv_done, m - M_X - 1)
                act.wait_ge(tail_ready, 2 * (m - M_X - 1))
                to_conv(m, m % 2, 16 * (M_C // 2 + 2))
                act.wait_ge(tr_psum, 3 * (m - 1))
                act.wait_ge(feat_stored[m % 2], 16)
                silu_conv(m, m % 2)
            for b in range(NB3):
                act.wait_ge(acc_ready, 3 * M_U + b + 1)
                s = slice(b * TB, (b + 1) * TB)
                nc.scalar.activation(dtw[:, 0, s], bank[b][0:HEADS, 0:TB], ACT.Abs, bias=hcol[:, 0:1]).then_inc(dt_act, 1)
                nc.scalar.activation(dtw[:, 1, s], bank[b][0:HEADS, 0:TB], ACT.Relu, bias=hcol[:, 0:1]).then_inc(acc_free, 1)
            act.wait_ge(dt_act, NB3)
            then_own(act, nc.scalar.activation(dtw[:, 2, :], dtw[:, 0, :], ACT.Exp, scale=-1.0), dt_act, NB3 + 1)
            nc.scalar.activation(dtw[:, 3, :], dtw[:, 2, :], ACT.Ln, bias=1.0).then_inc(dt_act, 1)
            nc.scalar.activation(hcol[:, 2:3], hcol[:, 1:2], ACT.Exp).then_inc(dt_act, 1)
            with act.Fori(M_U // 2, M_V // 2) as a:
                for j in range(2):
                    act.wait_ge(feat_stored[j], a * 16 - 16 * (M_U // 2 - 2))
                    activate(a * 2 + (j + 1), a * 2 + j, j, ACT.Gelu)
                    high_w(j, a * 16 + 32)
            for m in (M_V, M_V + 1):
                act.wait_ge(feat_stored[m % 2], 16 * ((M_V - M_B) // 2))
                activate(m + 1, m, m % 2, ACT.Gelu)
                high_w(m % 2, 16 * (M_V // 2 + 2))
            with act.Fori(M_V // 2 + 1, M_END // 2 - 1) as a:
                for j in range(2):
                    act.wait_ge(tr_psum, a * 6 + (3 * (j - 1) - 3 * (M_V - M_C)))
                    activate(a * 2 + (j + 1), a * 2 + j, j, ACT.Gelu)
                    high_w(j, a * 16 + 32)
            for m in (M_END - 2, M_END - 1):
                act.wait_ge(tr_psum, 3 * (m - 1 - (M_V - M_C)))
                activate(m + 1, m, m % 2, ACT.Gelu)

        @block.vector
        def _(dve):
            for j in range(2):
                nc.vector.memset(raw[j][:, 0:3], 0.0).then_inc(side_writes, 1)

            def normalise(t):
                r, j = rows_of(t), t % 2
                dve.wait_ge(x_rms, t + 1)
                then_own(dve, nc.vector.reciprocal(stat[j][0:r, 2:3], stat[j][0:r, 1:2]), x_rinv, t + 1)
                nc.vector.tensor_scalar(xn[j][0:r, :], xin[t % XB][0:r, :], stat[j][0:r, 2:3], None, ALU.mult).then_inc(x_normed, 1)

            def scale_xT(t):
                r = rows_of(t)
                for h in range(2):
                    dve.wait_ge(xT_psum, t * 2 + (h + 1))
                    wait(dve, xT_done, t * 2 + (h - 1))
                    nc.vector.tensor_tensor(
                        x32[h][:, :, 0:r],
                        bank[6 + h][:].rearrange("p (k t) -> p k t", k=4)[:, :, 0:r],
                        nmw[:, 4 * h:4 * h + 4].unsqueeze(2).to_broadcast([P, 4, r]), ALU.mult).then_inc(x_scaled, 1)

            normalise(0)
            normalise(1)
            dve.wait_ge(nmw_loaded, 16)
            for t in range(2, NT + 1):
                scale_xT(t - 2)
                normalise(t)
            scale_xT(NT - 1)
            scale_xT(NT)

            def unload(q, j):
                for g in range(3):
                    dve.wait_ge(tr_psum, q * 3 + (g + 1))
                    if g < 2:
                        ins = nc.vector.tensor_copy(stage[j][:, 4 * g:4 * g + 4, :],
                                                    bank[3 + g][:].rearrange("p (t c) -> p t c", t=4))
                    else:
                        ins = nc.vector.tensor_copy(stage[j][0:TS, NT, :], bank[5][0:TS, 0:P])
                    ins.then_inc(tr_free, 1)
                dve.wait_ge(tr_free, q * 3 + 3)
                nc.vector.sem_inc(stage_ready, 1)

            def convolve(c, j):
                then_own(dve, nc.vector.tensor_copy(sample_raw[j][:, :, 0:3],
                                                    old_conv[:, bass.ds(c, 1)].rearrange("p c b k -> p (c b) k")),
                         conv_chain, c * 7 + 1)
                dve.wait_ge(raw_ready, c + 1)
                dve.wait_ge(acc_free, c * 3 + (3 * M_X + 3))
                wait(dve, feat_ready, c + (M_X - 1))
                outs = (conv[j][:, 0:SEQ], conv[j][:, SEQ:T].rearrange("p (b s) -> p b s", s=DEC_S))
                for k in range(CONV_K):
                    ins = (prompt_raw[j][:, k:k + SEQ], sample_raw[j][:, :, k:k + DEC_S])
                    for part in range(2):
                        tap = cw[:, k, bass.ds(c, 1)]
                        if k == 0:
                            i = nc.vector.tensor_scalar(outs[part], ins[part], tap, None, ALU.mult)
                        else:
                            dve.wait_ge(conv_chain, c * 7 + (2 * k + part))
                            i = nc.vector.scalar_tensor_tensor(out=outs[part], in0=ins[part], scalar=tap, in1=outs[part],
                                                               op0=ALU.mult, op1=ALU.add)
                        if k < CONV_K - 1:
                            i.then_inc(conv_chain, 1)
                        elif part == 1:
                            i.then_inc(conv_done, 1)
                nc.vector.tensor_copy(tail[:, bass.ds(c, 1), 0, :], prompt_raw[j][:, SEQ:SEQ + 3].unsqueeze(1)).then_inc(tail_ready, 1)
                nc.vector.tensor_copy(tail[:, bass.ds(c, 1), 1:, :].rearrange("p c b k -> p (c b) k"),
                                      sample_raw[j][:, :, 4:7]).then_inc(tail_ready, 1)

            unload(0, 0)
            unload(1, 1)
            with dve.Fori(1, M_X // 2) as a:
                for j in range(2):
                    dve.wait_ge(stage_stored[j], a * 32)
                    unload(a * 2 + j, j)
            dve.wait_ge(side_writes, 2)
            dve.wait_ge(setup_loaded, 16 * N_SETUP)
            for c in (0, 1):
                convolve(c, c)
                dve.wait_ge(stage_stored[c], 32 * (M_X // 2))
                unload(M_X + c, c)
            with dve.Fori(M_X // 2 + 1, M_C // 2) as a:
                for j in range(2):
                    convolve(a * 2 + (j - M_X), j)
                    dve.wait_ge(stage_stored[j], a * 32)
                    unload(a * 2 + j, j)
            for m in (M_C, M_C + 1):
                convolve(m - M_X, m % 2)
            dve.wait_ge(dt_act, NB3 + 3)
            dve.wait_ge(acc_free, 3 * M_U + 3)
            link = [0]

            def chained(ins):
                link[0] += 1
                then_own(dve, ins, dt_chain, link[0])

            chained(nc.vector.tensor_scalar(dtw[:, 4, :], dtw[:, 2, :], 1.0, -1.0, ALU.add, ALU.add))
            chained(nc.vector.tensor_scalar(dtw[:, 5, :], dtw[:, 4, :], 0.0, None, ALU.is_equal))
            chained(nc.vector.tensor_tensor(dtw[:, 4, :], dtw[:, 4, :], dtw[:, 5, :], ALU.add))
            chained(nc.vector.tensor_tensor(dtw[:, 3, :], dtw[:, 3, :], dtw[:, 5, :], ALU.add))
            chained(nc.vector.tensor_tensor(dtw[:, 3, :], dtw[:, 3, :], dtw[:, 2, :], ALU.mult))
            chained(nc.vector.reciprocal(dtw[:, 4, :], dtw[:, 4, :]))
            chained(nc.vector.tensor_tensor(dtw[:, 3, :], dtw[:, 3, :], dtw[:, 4, :], ALU.mult))
            chained(nc.vector.tensor_tensor(dtw[:, 4, :], dtw[:, 3, :], dtw[:, 1, :], ALU.add))
            nc.vector.tensor_scalar(dtw[:, 5, :], dtw[:, 4, :], hcol[:, 2:3], -1.0, ALU.mult, ALU.mult).then_inc(dt_ready, 1)
            dve.wait_ge(dt_psum, 1)
            nc.vector.tensor_copy(S["dtk"][:, 0:NT, :], bank[6][:, 0:32 * NT].rearrange("p (t c) -> p t c", t=NT)).then_inc(side_writes, 1)
            nc.vector.tensor_copy(S["dtk"][0:TS, NT, :], bank[6][0:TS, 32 * NT:32 * NT + 32]).then_inc(side_writes, 1)
            with dve.Fori(M_C // 2, M_C // 2 + (M_END - M_V) // 2) as a:
                for j in range(2):
                    dve.wait_ge(stage_stored[j], a * 32)
                    unload(a * 2 + j, j)
            dve.wait_ge(side_writes, 4)

        @block.gpsimd
        def _(pool):
            def store_turned(q, j, dst, col):
                pool.wait_ge(stage_ready, q + 1)
                pool.dma_start(dst[0:SEQ, bass.ds(col, P)].rearrange("(t p) c -> p t c", p=P),
                               stage[j][:, 0:NT, :]).then_inc(stage_stored[j], 16)
                pool.dma_start(dst[SEQ:T, bass.ds(col, P)], stage[j][0:TS, NT, :]).then_inc(stage_stored[j], 16)

            def store_feat(m, j, dst, row):
                pool.wait_ge(feat_ready, m + 1)
                pool.dma_start(dst[bass.ds(row, P), :], feat[j][:]).then_inc(feat_stored[j], 16)

            def low_w(m, j):
                pool.wait_ge(w_high, m + 1)
                nc.gpsimd.tensor_tensor(wl[j][:], w[j][:], wh[j][:].bitcast(F32), ALU.subtract).then_inc(w_split, 1)

            def low_x(t):
                r = rows_of(t)
                for h in range(2):
                    pool.wait_ge(x_high, t * 2 + (h + 1))
                    at = (slice(None), slice(4 * h, 4 * h + 4), bass.ds(t * P, r))
                    nc.gpsimd.tensor_tensor(xl[at], x32[h][:, :, 0:r], xh[at].bitcast(F32), ALU.subtract).then_inc(xT_done, 1)

            make_constants(nc, pool, C)
            low_w(0, 0)
            with pool.Fori(0, NT) as t:
                low_x(t)
            low_w(1, 1)
            low_x(NT)
            with pool.Fori(0, M_X // 2) as a:
                for j in range(2):
                    low_w(a * 2 + (j + 2), j)
                    store_turned(a * 2 + j, j, S["z"], a * (2 * P) + j * P)
            pool.wait_ge(w_dt_high, 1)
            nc.gpsimd.tensor_tensor(w_dt_l[:], w_dt[:], w_dt_h[:].bitcast(F32), ALU.subtract).then_inc(w_dt_split, 1)
            with pool.Fori(M_X // 2, M_B // 2) as a:
                for j in range(2):
                    low_w(a * 2 + (j + 2), j)
                    store_turned(a * 2 + j, j, S["xb"], a * (2 * P) + (j - M_X) * P)
            for m in (M_B, M_B + 1):
                low_w(m + 2, m % 2)
                store_feat(m, m % 2, S["bct"], (m - M_B) * P)
                store_turned(m, m % 2, S["xb"], (m - M_X) * P)
            for m in (M_C, M_C + 1):
                low_w(m + 2, m % 2)
                store_feat(m, m % 2, S["bct"], (m - M_B) * P)
            pool.wait_ge(tail_ready, 2 * CT_N)
            pool.dma_start(A["conv_tail"], tail[:]).then_inc(tail_stored, 16)
            with pool.Fori(M_U // 2, M_V // 2) as a:
                for j in range(2):
                    low_w(a * 2 + (j + 2), j)
                    store_feat(a * 2 + j, j, S["uT"], a * (2 * P) + (j - M_U) * P)
            with pool.Fori(M_V // 2, M_END // 2 - 1) as a:
                for j in range(2):
                    low_w(a * 2 + (j + 2), j)
                    store_turned(a * 2 + (j + M_C - M_V), j, S["v"], a * (2 * P) + (j - M_V) * P)
            for m in (M_END - 2, M_END - 1):
                store_turned(m + M_C - M_V, m % 2, S["v"], (m - M_V) * P)
            for j in range(2):
                pool.wait_ge(feat_stored[j], 16 * ((M_V - M_B) // 2))
                pool.wait_ge(stage_stored[j], 32 * ((M_C + M_END - M_V) // 2))
            pool.wait_ge(tail_stored, 16)


def held(eng, value):
    return value if isinstance(value, int) else eng.snap(value)


class Links:

    def __init__(self, eng, sem, per):
        self.eng, self.sem, self.per, self.base, self.k = eng, sem, per, 0, 0

    def begin(self, tile):
        self.base, self.k = tile * self.per, 0

    def __call__(self, ins):
        self.k += 1
        assert self.k <= self.per or (isinstance(self.base, int) and self.base == self.per * NT)
        ins.then_inc(self.sem, 1)
        self.eng.wait_ge(self.sem, self.base + self.k)

    def settle(self):
        self.k += 1
        self.eng.sem_inc(self.sem, 1)


def mixer(nc, A, S, C, bank):
    with ExitStack() as ctx:
        def sb(name, shape, dt=F32):
            return ctx.enter_context(nc.sbuf_tensor(name, shape, dt))

        def sem(name):
            return ctx.enter_context(nc.semaphore(name))

        w_out_sg = S["w_out_sg"]
        w_out_ssm = sb("w_out_ssm", [P, KT, D])
        xb = sb("xb", [P, D + GROUPS * NSTATE])
        bct = sb("bct", [P, 2 * GROUPS, P])
        uT = sb("uT_t", [P, SGH, P])
        v = sb("v_t", [P, D])
        z = sb("z_t", [P, D])
        x = sb("x_t", [P, D])
        dta_h, dta_l = sb("dta_h", [P, NT + 1, HEADS], F32R), sb("dta_l", [P, NT + 1, HEADS], F32R)
        seg_h, seg_l = sb("seg_h", [P, HEADS, P], F32R), sb("seg_l", [P, HEADS, P], F32R)
        gt_r, gt_s_r = sb("gt_r", [P, P], F32R), sb("gt_s_r", [TS, TS], F32R)
        M = sb("M", [P, HEADS, P])
        cbm = sb("cbm", [P, GROUPS, P])
        decay = sb("decay", [P, 3, HEADS])
        xdt = sb("xdt", [P, D])
        xdtE = sb("xdtE", [P, D])
        xD = sb("xD", [P, D])
        y = sb("y", [P, D])
        yT = sb("yT", [P, KT, P])
        ysgT = sb("ysgT", [P, SGH, P])
        state = sb("state", [P, D])
        h = sb("h_t", [P, D])
        hn = sb("hn_t", [P, D])
        hnT = sb("hnT", [P, KT, P])
        junk = sb("junk", [P, D])
        ssm_w, ffn_w = sb("ssm_w", [P, D]), sb("ffn_w", [P, D])
        sg_w_row, sgWT, sgb, d_skip = (S[n] for n in ("sg_w_row", "sgWT", "sgb", "d_skip"))
        sgWT_s = sb("sgWT_s", [TS, SGH, TS])
        w_router = sb("w_router", [P, KT, EG + E])
        b_router = sb("b_router", [P, EG + E])
        st_v, st_h = sb("st_v", [P, 4]), sb("st_h", [P, 4])
        st_y = sb("st_y", [P, 6])
        lg = sb("lg", [P, EG + E])
        r8 = sb("r8", [P, 8, 8])
        idx = sb("idx", [P, 2, 8], U32)
        pick = sb("pick", [P, EG, EPG])
        chosen = sb("chosen", [P, E])
        run = S["run"]
        le_s, gt_s = sb("le_s", [TS, TS]), sb("gt_s", [TS, TS])
        dta_s = sb("dta_s", [TS, DEC_B, HEADS])
        decay_s = sb("decay_s", [P, DEC_B, HEADS])
        c_of = [sb(f"c_of{j}", [P, GROUPS, TS]) for j in range(2)]
        b_of = [sb(f"b_of{j}", [TS, GROUPS * NSTATE]) for j in range(2)]
        old = [sb(f"old{j}", [P, D]) for j in range(2)]
        new = [M[:, 8 * j:8 * j + 8, :].rearrange("p h l -> p (h l)") for j in range(2)]

        consts_loaded, consts_done = S["consts_loaded"], sem("consts_done")
        later_loaded, w_out_ssm_loaded = sem("later_loaded"), sem("w_out_ssm_loaded")
        xb_loaded, bct_loaded, u_loaded = sem("xb_loaded"), sem("bct_loaded"), sem("u_loaded")
        v_loaded, z_loaded, xr_loaded = sem("v_loaded"), sem("z_loaded"), sem("xr_loaded")
        cb_psum, cbm_ready, decay_ready = sem("cb_psum"), sem("cbm_ready"), sem("decay_ready")
        seg_ready, seg_psum, seg_exp, m_ready = sem("seg_ready"), sem("seg_psum"), sem("seg_exp"), sem("m_ready")
        xdt_ready, xdtE_ready, xD_ready = sem("xdt_ready"), sem("xdtE_ready"), sem("xD_ready")
        vn_ready, sg_psum, sg_sum, sg_ready = sem("vn_ready"), sem("sg_psum"), sem("sg_sum"), sem("sg_ready")
        yd_psum, st_psum, yo_psum = sem("yd_psum"), sem("st_psum"), sem("yo_psum")
        yo_used, yd_used, gated, yn_ready = sem("yo_used"), sem("yd_used"), sem("gated"), sem("yn_ready")
        state_ready = sem("state_ready")
        yT_psum, yT_done = sem("yT_psum"), sem("yT_done")
        sgproj_done, mix_psum, h_ready, hn_ready = sem("sgproj_done"), sem("mix_psum"), sem("h_ready"), sem("hn_ready")
        h_stored, hn_stored = sem("h_stored"), sem("hn_stored")
        hnT_psum, hnT_done, logits_psum = sem("hnT_psum"), sem("hnT_done"), sem("logits_psum")
        assigned, count_psum, counted = sem("assigned"), sem("count_psum"), sem("counted")
        v_sq, v_rms, y_sq, y_rms, h_sq, h_rms = (sem(n) for n in ("v_sq", "v_rms", "y_sq", "y_rms", "h_sq", "h_rms"))
        link1, link2, link3 = sem("link1"), sem("link2"), sem("link3")
        shifted, exped = sem("shifted"), sem("exped")
        old_loaded = [sem(f"old_loaded{j}") for j in range(2)]
        new_stored = [sem(f"new_stored{j}") for j in range(2)]
        of_ready, new_psum, new_ready = sem("of_ready"), sem("new_psum"), sem("new_ready")
        final_stored = sem("final_stored")
        rep_psum = sem("rep_psum")
        addressing = C["holder"]

        dtk = S["dtk"]
        N_CONSTS, N_DTA = 13, 5

        def heads(t, r):
            return t[0:r, 0:D].rearrange("p (h d) -> p h d", d=HD)

        def new_bank(b, g):
            return bank[g + 6 * (b % 2)]

        block = ctx.enter_context(nc.Block())

        @block.sync
        def _(sp):
            def step(I, s1, s2):
                i = I - 1
                r, r2 = rows_of(I), rows_of(i)
                I1, I2, i2, i22, i1 = (held(sp, q) for q in (I, I * 2, i * 2, i * 2 + 2, i + 1))
                at, at2 = held(sp, I * P), held(sp, i * P)
                now, before = bass.ds(at, r), bass.ds(at2, r2)
                first = isinstance(I, int) and I == 0

                def load_bc_x():
                    wait(sp, yo_psum, I2)
                    sp.sem_inc(addressing, 1)
                    sp.dma_start(bct[:, :, 0:r], S["bct"].rearrange("(g p) t -> p g t", p=P)[:, :, now]).then_inc(bct_loaded, 16)
                    wait(sp, st_psum, I2)
                    wait(sp, xD_ready, I1)
                    sp.dma_start(xb[0:r, :], S["xb"][now, :]).then_inc(xb_loaded, 16)

                if first:
                    load_bc_x()
                if s1:
                    wait(sp, sg_psum, I2)
                    sp.dma_start(v[0:r, :], S["v"][now, :]).then_inc(v_loaded, 16)
                    wait(sp, sg_ready, I2)
                    sp.sem_inc(addressing, 1)
                    sp.dma_start(uT[:, :, 0:r], S["uT"].rearrange("(h p) t -> p h t", p=P)[:, :, now]).then_inc(u_loaded, 16)
                if s2:
                    wait(sp, h_ready, i2)
                    src = A["x_sample"].rearrange("b s d -> (b s) d") if r2 == TS else A["x_prompt"][0][before, :]
                    sp.dma_start(x[0:r2, :], src).then_inc(xr_loaded, 16)
                if s1:
                    if not first:
                        load_bc_x()
                    wait(sp, gated, I1)
                    sp.dma_start(z[0:r, :], S["z"][now, :]).then_inc(z_loaded, 16)
                if s2:
                    sp.wait_ge(h_ready, i22)
                    sp.dma_start(S["h"][before, :], h[0:r2, :]).then_inc(h_stored, 16)
                    sp.wait_ge(hn_ready, i1)
                    sp.dma_start(S["hn"][before, :], hn[0:r2, :]).then_inc(hn_stored, 16)

            step(0, True, False)
            for dst, name in ((ssm_w, "ssm_norm_w"), (ffn_w, "norm_ffn_w"), (b_router, "b_router")):
                sp.dma_start(dst[:], A[name][0].partition_broadcast(P)).then_inc(later_loaded, 16)
            sp.dma_start(w_router[:], A["w_router"]).then_inc(later_loaded, 16)
            sp.dma_start(w_out_ssm[:], A["w_out"][:, 0:KT, :]).then_inc(w_out_ssm_loaded, 16)
            step(1, True, True)
            with sp.Fori(2, NT) as I:
                step(I, True, True)
            for j in range(2):
                sp.dma_start(old[j][:], A["state_ssm"][j]).then_inc(old_loaded[j], 16)
            step(NT, True, True)
            sp.wait_ge(state_ready, 2 * NT)
            sp.dma_start(A["ssm_prompt"], state[:]).then_inc(final_stored, 16)
            sp.wait_ge(vn_ready, NT + 1)
            sp.dma_start(A["sg_v_sample"], v[0:TS, :]).then_inc(final_stored, 16)
            for b in range(DEC_B):
                j = b % 2
                sp.wait_ge(new_ready, 2 * (b + 1))
                if b + 2 < DEC_B:
                    sp.dma_start(old[j][:], A["state_ssm"][b + 2]).then_inc(old_loaded[j], 16)
                sp.dma_start(A["ssm_sample"][b], new[j]).then_inc(new_stored[j], 16)
            step(NT + 1, False, True)
            for s in new_stored:
                sp.wait_ge(s, 16 * (DEC_B // 2))
            sp.wait_ge(final_stored, 32)
            sp.wait_ge(h_stored, 16 * (NT + 1))
            sp.wait_ge(hn_stored, 16 * (NT + 1))

        @block.gpsimd
        def _(pool):
            pool.wait_ge(consts_loaded, 16 * 4)
            pool.wait_ge(consts_done, N_DTA)

            def step(i):
                r = rows_of(i)
                le = C["le"] if r == P else le_s
                wait(pool, seg_psum, i * 4)
                for seg, part in ((seg_h, dta_h), (seg_l, dta_l)):
                    ins = nc.gpsimd.tensor_tensor(seg[0:r, :, 0:r], le[0:r, 0:r].unsqueeze(1).to_broadcast([r, HEADS, r]),
                                                  part[0:r, bass.ds(i, 1), :].bitcast(F32).rearrange("p o h -> p (o h)").unsqueeze(2).to_broadcast([r, HEADS, r]),
                                                  ALU.mult)
                ins.then_inc(seg_ready, 1)
                pool.wait_ge(xb_loaded, i * 16 + 16)
                wait(pool, gated, i)
                nc.gpsimd.tensor_tensor(heads(xD, r), heads(xb, r), d_skip[0:r, :].unsqueeze(2).to_broadcast([r, HEADS, HD]),
                                        ALU.mult).then_inc(xD_ready, 1)
                pool.wait_ge(decay_ready, i + 1)
                pool.wait_ge(xdt_ready, i + 1)
                wait(pool, st_psum, i * 2)
                nc.gpsimd.tensor_tensor(heads(xdtE, r), heads(xdt, r), decay[0:r, 2, :].unsqueeze(2).to_broadcast([r, HEADS, HD]),
                                        ALU.mult).then_inc(xdtE_ready, 1)

            step(0)
            with pool.Fori(1, NT) as i:
                step(i)
            pool.wait_ge(consts_done, N_CONSTS)
            step(NT)

        @block.tensor
        def _(pe):
            def sg_projection(i, k0, k1):
                r = rows_of(i)
                for k in range(k0, k1):
                    for n in range(2):
                        last = nc.tensor.matmul(bank[6 + n][0:r, :], ysgT[:, k, 0:r], w_out_sg[:, k, n * 512:(n + 1) * 512],
                                                start=(k == 0), stop=False)
                return last

            def turn_hn(i, half):
                r = rows_of(i)
                pe.wait_ge(hn_ready, i + 1)
                if half == 0:
                    pe.wait_ge(yo_used, min(2 * i + 4, 2 * NT + 2) if isinstance(i, int) else i * 2 + 4)
                    if isinstance(i, int) and i > 0 or not isinstance(i, int):
                        pe.wait_ge(counted, i)
                else:
                    pe.wait_ge(hnT_done, i * 2 + 1)
                for q in range(4):
                    k = 4 * half + q
                    last = nc.tensor.transpose(bank[5][:, q * P:q * P + r], hn[0:r, k * P:(k + 1) * P], C["ident"][0:r, 0:r])
                last.then_inc(hnT_psum, 1)

            def step(I, s1, s2, s3):
                if s2:
                    i2 = I - 1
                    pe.wait_ge(sg_ready, i2 * 2 + 2)
                    wait(pe, h_ready, i2 * 2)
                    if isinstance(i2, int) and i2 == NT:
                        pe.wait_ge(new_ready, 2 * DEC_B)
                    sg_projection(i2, 0, KT // 2)
                if s3:
                    turn_hn(I - 2, 0)
                if s2:
                    sg_projection(i2, KT // 2, KT).then_inc(sgproj_done, 1)
                if s3:
                    turn_hn(I - 2, 1)
                if s1:
                    r = rows_of(I)
                    le, gt = (C["le"], C["gt"]) if r == P else (le_s, gt_s)
                    dta = dtk[0:r, bass.ds(I, 1), HEADS:2 * HEADS].rearrange("p o h -> p (o h)")
                    pe.wait_ge(bct_loaded, I * 16 + 16)
                    wait(pe, yo_used, I * 2)
                    for g in range(GROUPS):
                        nc.tensor.matmul(bank[2][0:r, g * P:g * P + r], bct[:, g, 0:r], bct[:, GROUPS + g, 0:r],
                                         start=True, stop=True)
                    nc.tensor.matmul(bank[2][0:r, 256:272], le[0:r, 0:r], dta, start=True, stop=True)
                    if r == P:
                        nc.tensor.matmul(bank[2][:, 272:288], C["ones"][:], dta, start=True, stop=True)
                    nc.tensor.matmul(bank[2][0:r, 288:304], gt[0:r, 0:r], dta, start=True, stop=True).then_inc(cb_psum, 1)
                    if r == TS:
                        pe.wait_ge(link1, LINK1 * NT + 3)
                        nc.tensor.matmul(bank[2][:, 304:304 + DEC_B * HEADS], C["ones"][0:TS, :],
                                         dta_s[:].rearrange("p b h -> p (b h)"), start=True, stop=True).then_inc(cb_psum, 1)
                    pe.wait_ge(seg_ready, I + 1)
                    wait(pe, state_ready, I * 2)
                    def sums(quarters):
                        for q in quarters:
                            if q >= 2:
                                pe.wait_ge(seg_exp, I * 4 + (q - 1))
                            G = gt_r if r == P else gt_s_r
                            acc = bank[q % 2][:].rearrange("p (h l) -> p h l", h=4)[0:r, :, 0:r]
                            nc.tensor.matmul(acc, G[0:r, 0:r], seg_h[0:r, 4 * q:4 * q + 4, 0:r], start=True, stop=False)
                            nc.tensor.matmul(acc, G[0:r, 0:r], seg_l[0:r, 4 * q:4 * q + 4, 0:r], start=False, stop=True).then_inc(seg_psum, 1)

                    sums((0, 1))
                if s3:
                    i3 = I - 2
                    r3 = rows_of(i3)
                    pe.wait_ge(hnT_done, i3 * 2 + 2)
                    for k in range(KT):
                        last = nc.tensor.matmul(bank[5][0:r3, 0:EG + E], hnT[:, k, 0:r3], w_router[:, k, :],
                                                start=(k == 0), stop=(k == KT - 1))
                    last.then_inc(logits_psum, 1)
                if s1:
                    sums((2, 3))
                if s2:
                    r2 = rows_of(i2)
                    pe.wait_ge(yn_ready, i2 + 1)
                    for half in range(2):
                        for q in range(4):
                            k = 4 * half + q
                            last = nc.tensor.transpose(bank[3 + half][:, q * P:q * P + r2], y[0:r2, k * P:(k + 1) * P],
                                                       C["ident"][0:r2, 0:r2])
                        last.then_inc(yT_psum, 1)
                if s1:
                    W = sgWT if r == P else sgWT_s
                    pe.wait_ge(vn_ready, I + 1)
                    for q in range(2):
                        pe.wait_ge(seg_exp, I * 4 + (3 + q))
                        for hh in range(4):
                            hd = 4 * q + hh
                            last = nc.tensor.matmul(bank[q][:, hh * P:hh * P + r], v[0:r, hd * P:(hd + 1) * P],
                                                    W[0:r, hd, 0:r], start=True, stop=True)
                        last.then_inc(sg_psum, 1)
                if s2:
                    if isinstance(i2, int) and i2 == 0:
                        pe.wait_ge(w_out_ssm_loaded, 16)
                    for half in range(2):
                        pe.wait_ge(yT_done, i2 * 2 + (half + 1))
                        for k in range(4 * half, 4 * half + 4):
                            for n in range(2):
                                last = nc.tensor.matmul(bank[6 + n][0:r2, :], yT[:, k, 0:r2], w_out_ssm[:, k, n * 512:(n + 1) * 512],
                                                        start=False, stop=(k == KT - 1))
                    last.then_inc(mix_psum, 1)
                if s3:
                    pe.wait_ge(assigned, i3 + 1)
                    nc.tensor.matmul(bank[5][0:r3, 64:64 + E], C["lt"][0:r3, 0:r3], chosen[0:r3, :], start=True, stop=True)
                    nc.tensor.matmul(bank[5][:, 96:96 + E], C["ones"][0:r3, :], chosen[0:r3, :], start=True, stop=True).then_inc(count_psum, 1)
                if s1:
                    pe.wait_ge(xdt_ready, I + 1)
                    wait(pe, yT_done, I * 2)
                    for g in range(GROUPS):
                        pe.wait_ge(m_ready, I * 4 + (2 * g + 2))
                        for hh in range(8):
                            hd = 8 * g + hh
                            last = nc.tensor.matmul(bank[3 + g][0:r, hh * HD:(hh + 1) * HD], M[0:r, hd, 0:r],
                                                    xdt[0:r, hd * HD:(hd + 1) * HD], start=True, stop=True)
                        last.then_inc(yd_psum, 1)
                    pe.wait_ge(xdtE_ready, I + 1)
                    if s3:
                        pe.wait_ge(counted, i3 + 1)
                    if r == P:
                        for g in range(GROUPS):
                            pe.wait_ge(sg_sum, I * 2 + (g + 1))
                            nc.tensor.matmul(bank[g][:, :], xb[:, D + g * NSTATE:D + (g + 1) * NSTATE],
                                             xdtE[:, g * 512:(g + 1) * 512], start=True, stop=True).then_inc(st_psum, 1)
                        pe.wait_ge(decay_ready, I + 1)
                        pe.wait_ge(cbm_ready, I + 1)
                        for g in (1, 0):
                            nc.tensor.matmul(bank[2 if g else 5][:, :], bct[:, GROUPS + g, :], state[:, g * 512:(g + 1) * 512],
                                             start=True, stop=True).then_inc(yo_psum, 1)
                    else:
                        pe.wait_ge(sg_sum, I * 2 + 2)
                        pe.wait_ge(decay_ready, I + 1)
                        pe.wait_ge(cbm_ready, I + 1)
                        pe.wait_ge(h_ready, NT * 2)
                        for b in range(DEC_B):
                            j = b % 2
                            pe.wait_ge(old_loaded[j], 16 * (b // 2 + 1))
                            pe.wait_ge(of_ready, b + 1)
                            for g in (1, 0):
                                last = nc.tensor.matmul(bank[2 if g else 5][0:TS, :], c_of[j][:, g, :], old[j][:, g * 512:(g + 1) * 512],
                                                        start=(b == 0), stop=(b == DEC_B - 1))
                                if b == DEC_B - 1:
                                    last.then_inc(yo_psum, 1)
                            for g in range(GROUPS):
                                wait(pe, new_ready, 2 * (b - 2) + g + 1)
                                nc.tensor.matmul(new_bank(b, g)[:, :], b_of[j][:, g * NSTATE:(g + 1) * NSTATE],
                                                 xdtE[0:TS, g * 512:(g + 1) * 512], start=True, stop=True).then_inc(new_psum, 1)

            pe.wait_ge(consts_done, N_DTA + 1)
            nc.tensor.matmul(bank[2][0:TS, 0:SGH * DEC_S], C["repeat"][:], sgWT[0:DEC_S, :, 0:DEC_S],
                             start=True, stop=True).then_inc(rep_psum, 1)
            pe.wait_ge(consts_done, N_CONSTS)
            step(0, True, False, False)
            pe.wait_ge(S["w_out_loaded"], 16)
            pe.wait_ge(later_loaded, 16 * 4)
            step(1, True, True, False)
            with pe.Fori(2, NT) as I:
                step(I, True, True, True)
            step(NT, True, True, True)
            step(NT + 1, False, True, True)
            step(NT + 2, False, False, True)

        @block.scalar
        def _(act):
            def step(I, s1, s2, s3):
                if s1:
                    r = rows_of(I)
                    act.wait_ge(v_loaded, I * 16 + 16)
                    wait(act, vn_ready, I)
                    then_own(act, nc.scalar.activation(junk[0:r, :], v[0:r, :], ACT.Square, accum_out=st_v[0:r, 0:1]), v_sq, I + 1)
                    nc.scalar.activation(st_v[0:r, 1:2], st_v[0:r, 0:1], ACT.Sqrt, bias=C["eps"][0:r, :], scale=1.0 / D).then_inc(v_rms, 1)
                if s3:
                    i3 = I - 2
                    r3 = rows_of(i3)
                    for half in range(2):
                        act.wait_ge(hnT_psum, i3 * 2 + (half + 1))
                        wait(act, logits_psum, i3)
                        nc.scalar.copy(hnT[:, 4 * half:4 * half + 4, 0:r3],
                                       bank[5][:].rearrange("p (k t) -> p k t", k=4)[:, :, 0:r3]).then_inc(hnT_done, 1)
                if s1:
                    r = rows_of(I)
                    if r == P:
                        act.wait_ge(cb_psum, I + 1)
                    else:
                        act.wait_ge(cb_psum, NT + 2)
                        nc.scalar.activation(decay_s[:].rearrange("p b h -> p (b h)"), bank[2][:, 304:304 + DEC_B * HEADS], ACT.Exp)
                    wait(act, xdtE_ready, I)
                    wait(act, state_ready, I * 2)
                    if r == P:
                        nc.scalar.activation(decay[:].rearrange("p a h -> p (a h)"), bank[2][:, 256:304], ACT.Exp).then_inc(decay_ready, 1)
                    else:
                        nc.scalar.activation(decay[0:TS, 0, :], bank[2][0:TS, 256:272], ACT.Exp)
                        nc.scalar.activation(decay[0:TS, 2, :], bank[2][0:TS, 288:304], ACT.Exp).then_inc(decay_ready, 1)
                    wait(act, yd_psum, I * 2)
                    for q in range(4):
                        act.wait_ge(seg_psum, I * 4 + (q + 1))
                        nc.scalar.activation(M[0:r, 4 * q:4 * q + 4, 0:r],
                                             bank[q % 2][:].rearrange("p (h l) -> p h l", h=4)[0:r, :, 0:r],
                                             ACT.Exp).then_inc(seg_exp, 1)
                if s3:
                    act.wait_ge(shifted, i3 * 2 + 1)
                    nc.scalar.activation(r8[0:r3, 1, 0:EG], lg[0:r3, 0:EG], ACT.Exp, bias=r8[0:r3, 0, 1:2],
                                         accum_out=r8[0:r3, 0, 2:3]).then_inc(exped, 1)
                if s2:
                    i2 = I - 1
                    r2 = rows_of(i2)
                    wait(act, mix_psum, i2)
                    for half in range(2):
                        act.wait_ge(yT_psum, i2 * 2 + (half + 1))
                        nc.scalar.copy(yT[:, 4 * half:4 * half + 4, 0:r2],
                                       bank[3 + half][:].rearrange("p (k t) -> p k t", k=4)[:, :, 0:r2]).then_inc(yT_done, 1)
                if s3:
                    act.wait_ge(shifted, i3 * 2 + 2)
                    nc.scalar.activation(r8[0:r3, 4, :], r8[0:r3, 3, :], ACT.Exp, bias=r8[0:r3, 0, 4:5],
                                         accum_out=r8[0:r3, 0, 5:6]).then_inc(exped, 1)
                if s2:
                    act.wait_ge(h_ready, i2 * 2 + 2)
                    wait(act, hn_ready, i2)
                    then_own(act, nc.scalar.activation(junk[0:r2, :], h[0:r2, :], ACT.Square, accum_out=st_h[0:r2, 0:1]), h_sq, i2 + 1)
                    nc.scalar.activation(st_h[0:r2, 1:2], st_h[0:r2, 0:1], ACT.Sqrt, bias=C["eps"][0:r2, :], scale=1.0 / D).then_inc(h_rms, 1)
                if s1:
                    act.wait_ge(gated, I + 1)
                    wait(act, yn_ready, I)
                    for g in range(GROUPS):
                        nc.scalar.activation(junk[0:r, g * 512:(g + 1) * 512], y[0:r, g * 512:(g + 1) * 512], ACT.Square,
                                             accum_out=st_y[0:r, g:g + 1]).then_inc(y_sq, 1)
                    act.wait_ge(y_sq, I * 2 + 2)
                    nc.scalar.activation(st_y[0:r, 2:4], st_y[0:r, 0:2], ACT.Sqrt, bias=C["eps"][0:r, :],
                                         scale=2.0 / D).then_inc(y_rms, 1)

            act.wait_ge(consts_done, N_CONSTS)
            step(0, True, False, False)
            step(1, True, True, False)
            with act.Fori(2, NT) as I:
                step(I, True, True, True)
            step(NT, True, True, True)
            step(NT + 1, False, True, True)
            step(NT + 2, False, False, True)

        @block.vector
        def _(dve):
            l1, l2, l3 = Links(dve, link1, LINK1), Links(dve, link2, LINK2), Links(dve, link3, LINK3)

            def over(t, r, n):
                return t.unsqueeze(2).to_broadcast([r, HEADS, n])

            def halves(t, r, g):
                return t[0:r, g * 512:(g + 1) * 512].rearrange("p (h d) -> p h d", d=HD)

            def route(i, r):
                l3.begin(i)
                dve.wait_ge(logits_psum, i + 1)
                R = r8[0:r]
                l3(nc.vector.tensor_tensor(lg[0:r, :], bank[5][0:r, 0:EG + E], b_router[0:r, :], ALU.add))
                l3(nc.vector.tensor_reduce(R[:, 0, 0:1], lg[0:r, 0:EG], AX.X, ALU.max))
                nc.vector.tensor_scalar(R[:, 0, 1:2], R[:, 0, 0:1], -1.0, None, ALU.mult).then_inc(shifted, 1)
                dve.wait_ge(exped, i * 2 + 1)
                l3(nc.vector.reciprocal(R[:, 0, 0:1], R[:, 0, 2:3]))
                l3(nc.vector.tensor_scalar(R[:, 1, 0:EG], R[:, 1, 0:EG], R[:, 0, 0:1], None, ALU.mult))
                l3.settle()
                l3(nc.vector.max(R[:, 2, :], R[:, 1, :]))
                l3.settle()
                l3(nc.vector.max_index(idx[0:r, 0, :], R[:, 2, :], R[:, 1, :]))
                l3(nc.vector.tensor_copy(R[:, 0, 6:7], idx[0:r, 0, 0:1]))
                l3(nc.vector.tensor_scalar(R[:, 7, 0:EG], C["expert_no"][0:r, 0:EG], R[:, 0, 6:7], None, ALU.is_equal))
                l3(nc.vector.tensor_tensor(pick[0:r], lg[0:r, EG:].rearrange("p (g e) -> p g e", e=EPG),
                                           R[:, 7, 0:EG].unsqueeze(2).to_broadcast([r, EG, EPG]), ALU.mult))
                l3(nc.vector.tensor_reduce(R[:, 3, :], pick[0:r].rearrange("p g e -> p e g"), AX.X, ALU.add))
                l3(nc.vector.tensor_reduce(R[:, 0, 3:4], R[:, 3, :], AX.X, ALU.max))
                nc.vector.tensor_scalar(R[:, 0, 4:5], R[:, 0, 3:4], -1.0, None, ALU.mult).then_inc(shifted, 1)
                dve.wait_ge(exped, i * 2 + 2)
                l3(nc.vector.reciprocal(R[:, 0, 7:8], R[:, 0, 5:6]))
                l3(nc.vector.tensor_scalar(R[:, 4, :], R[:, 4, :], R[:, 0, 7:8], None, ALU.mult))
                l3.settle()
                l3(nc.vector.max(R[:, 5, :], R[:, 4, :]))
                l3.settle()
                l3(nc.vector.max_index(idx[0:r, 1, :], R[:, 5, :], R[:, 4, :]))
                l3(nc.vector.tensor_copy(R[:, 6, 0:2], idx[0:r, 1, 0:2]))
                l3(nc.vector.tensor_scalar(R[:, 0, 3:4], R[:, 0, 6:7], float(EPG), None, ALU.mult))
                l3(nc.vector.tensor_scalar(R[:, 6, 2:4], R[:, 6, 0:2], R[:, 0, 3:4], None, ALU.add))
                l3(nc.vector.tensor_tensor(R[:, 6, 4:5], R[:, 5, 0:1], R[:, 5, 1:2], ALU.add))
                l3(nc.vector.reciprocal(R[:, 6, 5:6], R[:, 6, 4:5]))
                l3(nc.vector.tensor_scalar(S["gate"][0:r, bass.ds(i, 1), :], R[:, 5:6, 0:2], R[:, 2, 0:1], R[:, 6, 5:6],
                                           ALU.mult, ALU.mult))
                hot = S["hot"]
                for k in range(2):
                    l3(nc.vector.tensor_scalar(hot[0:r, bass.ds(i, 1), k, :], C["expert_no"][0:r, :].unsqueeze(1),
                                               R[:, 6, 2 + k:3 + k], None, ALU.is_equal))
                nc.vector.tensor_tensor(chosen[0:r, :].unsqueeze(1), hot[0:r, bass.ds(i, 1), 0, :], hot[0:r, bass.ds(i, 1), 1, :],
                                        ALU.add).then_inc(assigned, 1)

            def step(I, s1, s2, s3):
                if s1:
                    r = rows_of(I)
                    le = C["le"] if r == P else le_s
                    dt_r = dtk[0:r, bass.ds(I, 1), 0:HEADS].rearrange("p o h -> p (o h)")
                    l1.begin(I)
                    dve.wait_ge(v_rms, I + 1)
                    l1(nc.vector.reciprocal(st_v[0:r, 2:3], st_v[0:r, 1:2]))
                    nc.vector.scalar_tensor_tensor(out=v[0:r, :], in0=v[0:r, :], scalar=st_v[0:r, 2:3], in1=sg_w_row[0:r, :],
                                                   op0=ALU.mult, op1=ALU.mult).then_inc(vn_ready, 1)
                    if r == TS:
                        l1(nc.vector.tensor_copy(dta_s[:], dtk[0:TS, NT, HEADS:2 * HEADS].unsqueeze(1).to_broadcast([TS, DEC_B, HEADS])))
                        l1(nc.vector.tensor_tensor(dta_s[:], dta_s[:],
                                                   C["same"][:, 0:TS:DEC_S].unsqueeze(2).to_broadcast([TS, DEC_B, HEADS]), ALU.mult))
                    dve.wait_ge(decay_ready, I + 1)
                    nc.vector.tensor_tensor(cbm[0:r, :, 0:r], bank[2][:, 0:2 * P].rearrange("p (g l) -> p g l", g=2)[0:r, :, 0:r],
                                            le[0:r, 0:r].unsqueeze(1).to_broadcast([r, 2, r]), ALU.mult).then_inc(cbm_ready, 1)
                    dve.wait_ge(xb_loaded, I * 16 + 16)
                    wait(dve, yd_psum, I * 2)
                    wait(dve, xdtE_ready, I)
                    nc.vector.tensor_tensor(heads(xdt, r), heads(xb, r), over(dt_r, r, HD), ALU.mult).then_inc(xdt_ready, 1)
                    dve.wait_ge(cbm_ready, I + 1)
                    for q in range(4):
                        dve.wait_ge(seg_exp, I * 4 + (q + 1))
                        nc.vector.tensor_tensor(M[0:r, 4 * q:4 * q + 4, 0:r], M[0:r, 4 * q:4 * q + 4, 0:r],
                                                cbm[0:r, q // 2, 0:r].unsqueeze(1).to_broadcast([r, 4, r]), ALU.mult).then_inc(m_ready, 1)
                if s3:
                    route(I - 2, rows_of(I - 2))
                if s1:
                    wait(dve, sgproj_done, I)
                    for q in range(2):
                        dve.wait_ge(sg_psum, I * 2 + (q + 1))
                        s = slice(4 * q, 4 * q + 4)
                        got = bank[q][:].rearrange("p (h t) -> p h t", h=4)[:, :, 0:r]
                        if r == P:
                            ins = nc.vector.tensor_tensor(ysgT[:, s, :], got, sgb[:, s, :], ALU.add)
                            ins.then_inc(sg_sum, 1)
                        else:
                            for hh in range(4):
                                seqs = lambda t: t.rearrange("p (b s) -> p b s", s=DEC_S)
                                ins = nc.vector.tensor_tensor(
                                    seqs(ysgT[:, 4 * q + hh, 0:TS]), seqs(got[:, hh, :]),
                                    sgb[:, 4 * q + hh, 0:DEC_S].unsqueeze(1).to_broadcast([P, DEC_B, DEC_S]), ALU.add)
                            ins.then_inc(sg_sum, 1)
                    dve.wait_ge(u_loaded, I * 16 + 16)
                    for q in range(2):
                        s = slice(4 * q, 4 * q + 4)
                        dve.wait_ge(sg_sum, I * 2 + (q + 1))
                        nc.vector.tensor_tensor(ysgT[:, s, 0:r], ysgT[:, s, 0:r], uT[:, s, 0:r], ALU.mult).then_inc(sg_ready, 1)
                if s2:
                    i2 = I - 1
                    r2 = rows_of(i2)
                    l2.begin(i2)
                    dve.wait_ge(mix_psum, i2 + 1)
                    dve.wait_ge(xr_loaded, i2 * 16 + 16)
                    wait(dve, h_stored, i2 * 16)
                    for n in range(2):
                        s = slice(n * 512, (n + 1) * 512)
                        nc.vector.tensor_tensor(h[0:r2, s], bank[6 + n][0:r2, :], x[0:r2, s], ALU.add).then_inc(h_ready, 1)
                if s3:
                    i3, r3 = I - 2, rows_of(I - 2)
                    dve.wait_ge(count_psum, i3 + 1)
                    l3(nc.vector.tensor_tensor(S["before"][0:r3, bass.ds(i3, 1), :], bank[5][0:r3, 64:64 + E].unsqueeze(1),
                                               run[0:r3, :].unsqueeze(1), ALU.add))
                    nc.vector.tensor_tensor(run[:], bank[5][:, 96:96 + E], run[:], ALU.add).then_inc(counted, 1)
                    dve.wait_ge(counted, i3 + 1)
                if s2:
                    dve.wait_ge(h_rms, i2 + 1)
                    l2(nc.vector.reciprocal(st_h[0:r2, 2:3], st_h[0:r2, 1:2]))
                    wait(dve, hn_stored, i2 * 16)
                    wait(dve, hnT_psum, i2 * 2)
                    dve.wait_ge(h_ready, i2 * 2 + 2)
                    nc.vector.scalar_tensor_tensor(out=hn[0:r2, :], in0=h[0:r2, :], scalar=st_h[0:r2, 2:3], in1=ffn_w[0:r2, :],
                                                   op0=ALU.mult, op1=ALU.mult).then_inc(hn_ready, 1)
                if s1:
                    if r == TS:
                        sample_states()
                    wait(dve, yT_psum, I * 2)
                    for n, g in enumerate((1, 0)):
                        dve.wait_ge(yo_psum, I * 2 + (n + 1))
                        nc.vector.tensor_tensor(halves(y, r, g), bank[2 if g else 5][0:r, :].rearrange("p (h d) -> p h d", d=HD),
                                                decay[0:r, 0, 8 * g:8 * g + 8].unsqueeze(2).to_broadcast([r, 8, HD]),
                                                ALU.mult).then_inc(yo_used, 1)
                    for g in range(GROUPS):
                        dve.wait_ge(yd_psum, I * 2 + (g + 1))
                        dve.wait_ge(yo_used, I * 2 + 2)
                        nc.vector.tensor_tensor(halves(y, r, g), halves(y, r, g),
                                                bank[3 + g][0:r, :].rearrange("p (h d) -> p h d", d=HD), ALU.add).then_inc(yd_used, 1)
                    dve.wait_ge(yd_used, I * 2 + 2)
                    dve.wait_ge(xD_ready, I + 1)
                    l1(nc.vector.tensor_tensor(y[0:r, :], y[0:r, :], xD[0:r, :], ALU.add))
                    dve.wait_ge(z_loaded, I * 16 + 16)
                    nc.vector.tensor_tensor(y[0:r, :], y[0:r, :], z[0:r, :], ALU.mult).then_inc(gated, 1)
                    if r == P:
                        l1(nc.vector.tensor_tensor(heads(state, P), heads(state, P), over(decay[:, 1, :], P, HD), ALU.mult))
                        for g in range(GROUPS):
                            dve.wait_ge(st_psum, I * 2 + (g + 1))
                            s = slice(g * 512, (g + 1) * 512)
                            nc.vector.tensor_tensor(state[:, s], state[:, s], bank[g][:, :], ALU.add).then_inc(state_ready, 1)
                    dve.wait_ge(gated, I + 1)
                    if r == P:
                        dve.wait_ge(state_ready, I * 2 + 2)
                    dve.wait_ge(y_rms, I + 1)
                    l1(nc.vector.reciprocal(st_y[0:r, 4:6], st_y[0:r, 2:4]))
                    if isinstance(I, int) and I == 0:
                        dve.wait_ge(later_loaded, 16 * 4)
                    for g in range(GROUPS):
                        s = slice(g * 512, (g + 1) * 512)
                        ins = nc.vector.scalar_tensor_tensor(out=y[0:r, s], in0=y[0:r, s], scalar=st_y[0:r, 4 + g:5 + g],
                                                             in1=ssm_w[0:r, s], op0=ALU.mult, op1=ALU.mult)
                    ins.then_inc(yn_ready, 1)

            def sample_states():
                dve.wait_ge(bct_loaded, 16 * (NT + 1))
                dve.wait_ge(decay_ready, NT + 1)

                def mask(b):
                    j = b % 2
                    wait(dve, new_psum, 2 * (b - 1))
                    for g in range(GROUPS):
                        nc.vector.tensor_tensor(c_of[j][:, g, :], bct[:, GROUPS + g, 0:TS], C["of_seq"][:, b, :], ALU.mult)
                    nc.vector.tensor_scalar(b_of[j][:], xb[0:TS, D:], C["same"][:, DEC_S * b:DEC_S * b + 1], None,
                                            ALU.mult).then_inc(of_ready, 1)

                mask(0)
                mask(1)
                dve.wait_ge(yd_psum, 2 * NT + 2)
                for b in range(DEC_B):
                    j = b % 2
                    dve.wait_ge(new_psum, 2 * b + 2)
                    l1(nc.vector.tensor_tensor(heads(old[j], P), heads(old[j], P), over(decay_s[:, b, :], P, HD), ALU.mult))
                    wait(dve, new_stored[j], 16 * (b // 2))
                    for g in range(GROUPS):
                        s = slice(g * 512, (g + 1) * 512)
                        nc.vector.tensor_tensor(new[j][:, s], old[j][:, s], new_bank(b, g)[:, :], ALU.add).then_inc(new_ready, 1)
                    if b + 2 < DEC_B:
                        mask(b + 2)

            for t in (S["hot"], S["before"]):
                nc.vector.memset(t[:, NT:NT + 1], 0.0)
            nc.vector.memset(run[:], 0.0)
            nc.vector.memset(state[:], 0.0)
            nc.vector.memset(r8[:], -1.0)
            for rows, tiles in ((P, slice(0, NT)), (TS, slice(NT, NT + 1))):
                nc.vector.tensor_copy(dta_h[0:rows, tiles, :], dtk[0:rows, tiles, HEADS:]).then_inc(consts_done, 1)
            nc.vector.tensor_copy(gt_r[:], C["gt"][:]).then_inc(consts_done, 1)
            dve.wait_ge(consts_done, 2)
            for rows, tiles in ((P, slice(0, NT)), (TS, slice(NT, NT + 1))):
                nc.vector.tensor_tensor(dta_l[0:rows, tiles, :], dtk[0:rows, tiles, HEADS:], dta_h[0:rows, tiles, :].bitcast(F32),
                                        ALU.subtract).then_inc(consts_done, 1)
            dve.wait_ge(consts_loaded, 16 * 4)
            nc.vector.tensor_tensor(sgWT[:], sgWT[:], C["le"][:].unsqueeze(1).to_broadcast([P, SGH, P]), ALU.mult).then_inc(consts_done, 1)
            nc.vector.tensor_tensor(le_s[:], C["le"][0:TS, 0:TS], C["same"][:], ALU.mult).then_inc(consts_done, 1)
            nc.vector.tensor_tensor(gt_s[:], C["gt"][0:TS, 0:TS], C["same"][:], ALU.mult).then_inc(consts_done, 1)
            dve.wait_ge(rep_psum, 1)
            for b in range(DEC_B):
                ins = nc.vector.tensor_copy(sgWT_s[:, :, b * DEC_S:(b + 1) * DEC_S],
                                            bank[2][0:TS, 0:SGH * DEC_S].rearrange("p (h t) -> p h t", h=SGH))
            ins.then_inc(consts_done, 1)
            dve.wait_ge(consts_done, N_DTA + 4)
            nc.vector.tensor_copy(gt_s_r[:], gt_s[:]).then_inc(consts_done, 1)
            nc.vector.tensor_tensor(sgWT_s[:], sgWT_s[:], C["same"][:].unsqueeze(1).to_broadcast([TS, SGH, TS]),
                                    ALU.mult).then_inc(consts_done, 1)
            nc.vector.memset(st_v[:], 1.0).then_inc(consts_done, 1)
            nc.vector.memset(st_y[:], 1.0).then_inc(consts_done, 1)
            dve.wait_ge(consts_done, N_CONSTS)
            step(0, True, False, False)
            step(1, True, True, False)
            with dve.Fori(2, NT) as I:
                step(I, True, True, True)
            step(NT, True, True, True)
            step(NT + 1, False, True, True)
            step(NT + 2, False, False, True)


LINK1, LINK2, LINK3 = 4, 1, 28


def experts(nc, A, S, C, bank):
    with ExitStack() as ctx:
        def sb(name, shape, dt=F32):
            return ctx.enter_context(nc.sbuf_tensor(name, shape, dt))

        def sem(name):
            return ctx.enter_context(nc.semaphore(name))

        N_ASG = 2 * (NT + 1)
        over = sb("over", [P, E, NT + 1])
        n_blk, blk_end, row0 = sb("n_blk", [P, E]), sb("blk_end", [P, E]), sb("row0", [P, E])
        place = sb("place", [P, NT + 1, 2, E])
        row_f = sb("row_f", [P, NT + 1, 2])
        ended = sb("ended", [MAXBLK, E])
        blk_col = sb("blk_col", [MAXBLK, 1])
        blk_i = sb("blk_i", [1, MAXBLK + 1], I32)
        at_or_past = sb("at_or_past", [P, N_ASG, MAXBLK + 1])
        of_block, in_block = sb("of_block", [P, N_ASG]), sb("in_block", [P, N_ASG])
        of_row_f = sb("of_row_f", [P, 2, MAXBLK])
        of_row = sb("of_row", [P, 2, MAXBLK], I32)
        src, dst = sb("src", [P, 1], I32), sb("dst", [P, 1], I32)
        xg = sb("xg", [P, D])
        xh, xl = sb("xh_blk", [P, KT, P], F32R), sb("xl_blk", [P, KT, P], F32R)
        wg, wu = sb("wg", [P, KT, FF]), sb("wu", [P, KT, FF])
        wd = sb("wd", [P, FF // P, D])
        wg_h, wg_l = sb("wg_h", [P, KT, FF], F32R), sb("wg_l", [P, KT, FF], F32R)
        wu_h, wu_l = sb("wu_h", [P, KT, FF], F32R), sb("wu_l", [P, KT, FF], F32R)
        wd_h, wd_l = sb("wd_h", [P, FF // P, D], F32R), sb("wd_l", [P, FF // P, D], F32R)
        spare = S["h_final"][:].rearrange("p t d -> p (t d)")
        place_hot = spare[:, 0:N_ASG * P].rearrange("p (a c) -> p a c", a=N_ASG)
        block_value = spare[:, N_ASG * P:N_ASG * (P + 2 * MAXBLK)].rearrange("p (a o n) -> p a o n", a=N_ASG, o=2)
        act_g, hid = sb("act_g", [P, FF]), sb("hid", [P, FF])
        hT_h, hT_l = sb("hT_h", [P, FF // P, P], F32R), sb("hT_l", [P, FF // P, P], F32R)
        yb = sb("yb", [P, D])

        chain, table_ready = sem("chain"), sem("table_ready")
        blk_ready, blk_psum = sem("blk_ready"), sem("blk_psum")
        zeroed, rows_psum, rows_ready = sem("zeroed"), sem("rows_psum"), sem("rows_ready")
        gate_up_loaded = [sem(f"gate_up_loaded{p}") for p in range(4)]
        down_loaded = [sem(f"down_loaded{p}") for p in range(4)]
        src_ready, dst_ready, xg_loaded = sem("src_ready"), sem("dst_ready"), sem("xg_loaded")
        gu_high, gu_split, gu_used = sem("gu_high"), sem("gu_split"), sem("gu_used")
        down_high, down_split, down_used = sem("down_high"), sem("down_split"), sem("down_used")
        x_high, h_high = sem("xb_high"), sem("h_high")
        silu_done, hid_ready = sem("silu_done"), sem("hid_ready")
        xT_psum, xT_done = sem("xTb_psum"), sem("xTb_done")
        hT_psum, hT_done = sem("hT_psum"), sem("hT_done")
        y_done, y_stored = sem("y_done"), sem("y_stored")
        holder = C["holder"]

        block = ctx.enter_context(nc.Block())

        def blocks_but_three(eng):
            eng.wait_ge(table_ready, 2)
            return eng.value_load(blk_i[0:1, MAXBLK:MAXBLK + 1], min_val=MINBLK - 3, max_val=MAXBLK - 3)

        @block.sync
        def _(sp):
            def expert(i):
                e = sp.value_load(blk_i[0:1, bass.ds(i, 1)], min_val=0, max_val=E - 1)
                return bass.ds(e, 1)

            def load_gate_up(i):
                e = expert(i)
                at = [held(sp, i * 4 + (p - 3)) for p in range(4)]
                for p in range(4):
                    wait(sp, gu_split, at[p])
                    rows = slice(2 * p * P, (2 * p + 2) * P)
                    for t, name in ((wg, "w_gate"), (wu, "w_up")):
                        sp.dma_start(t[:, 2 * p:2 * p + 2, :], A[name][e, rows, :].rearrange("e (k p) f -> p (e k) f", p=P)).then_inc(gate_up_loaded[p], 16)

            def load_down(i):
                e = expert(i)
                at = [held(sp, i * 4 + (p - 3)) for p in range(4)]
                for p in range(4):
                    wait(sp, down_split, at[p])
                    sp.dma_start(wd[:, p, :], A["w_down"][e, p * P:(p + 1) * P, :].rearrange("e p d -> p (e d)")).then_inc(down_loaded[p], 16)

            m = blocks_but_three(sp) + 1
            load_gate_up(0)
            load_down(0)
            load_gate_up(1)
            with sp.Fori(0, m) as i:
                load_gate_up(i + 2)
                load_down(i + 1)
            load_down(m + 1)
            sp.dma_start(S["w_final"][:], A["norm_final_w"][0].partition_broadcast(P)).then_inc(S["final_loaded"][0], 16)
            sp.wait_ge(rows_ready, 1)
            for j in range(FIRST):
                sp.dma_start(S["h_final"][:, j, :], S["h"][j * P:(j + 1) * P, :]).then_inc(S["final_loaded"][j], 16)
            sp.wait_ge(y_stored, m * 16 + 32)
            sp.sem_inc(holder, 1)

        @block.gpsimd
        def _(pool):
            nc.gpsimd.memset(xg[:], 0.0).then_inc(zeroed, 1)
            pool.wait_ge(zeroed, 1)
            pool.wait_ge(rows_ready, 1)
            m = blocks_but_three(pool)

            def gather(i):
                wait(pool, xg_loaded, i * 16)
                then_own(pool, nc.gpsimd.tensor_copy(src[:], of_row[:, 0, bass.ds(i, 1)]), src_ready, i + 1)
                wait(pool, xT_psum, i * 2)
                pool.sem_inc(holder, 1)
                pool.indirect_dma_start(out=xg[:], out_offset=None, in_=S["hn"],
                                        in_offset=bass.IndirectOffsetOnAxis(ap=src[:], axis=0),
                                        bounds_check=T - 1, oob_is_err=False).then_inc(xg_loaded, 16)

            def scatter(i):
                wait(pool, y_stored, i * 16)
                then_own(pool, nc.gpsimd.tensor_copy(dst[:], of_row[:, 1, bass.ds(i, 1)]), dst_ready, i + 1)
                pool.wait_ge(y_done, i * 2 + 2)
                pool.sem_inc(holder, 1)
                pool.indirect_dma_start(out=S["picked"], out_offset=bass.IndirectOffsetOnAxis(ap=dst[:], axis=0),
                                        in_=yb[:], in_offset=None, bounds_check=2 * T - 1, oob_is_err=False).then_inc(y_stored, 16)

            gather(0)
            gather(1)
            gather(2)
            with pool.Fori(1, m + 1) as i:
                gather(i + 2)
                scatter(i - 1)
            scatter(m)
            scatter(m + 1)
            scatter(m + 2)

        @block.tensor
        def _(pe):
            def turn_x(i):
                pe.wait_ge(xg_loaded, i * 16 + 16)
                for half in range(2):
                    wait(pe, xT_done, i * 2 + (half - 1))
                    for q in range(4):
                        last = nc.tensor.transpose(bank[4 + half][:, q * P:(q + 1) * P], xg[:, (4 * half + q) * P:(4 * half + q + 1) * P],
                                                   C["ident"][:])
                    last.then_inc(xT_psum, 1)

            def gate_up(i):
                wait(pe, hid_ready, i)
                for k in range(KT):
                    if k % 2 == 0:
                        pe.wait_ge(gu_split, i * 4 + (k // 2 + 1))
                    if k % 4 == 0:
                        pe.wait_ge(xT_done, i * 2 + (k // 4 + 1))
                    for n, (w_h, w_l) in enumerate(((wg_h, wg_l), (wu_h, wu_l))):
                        last = split_product(nc, bank[n][:, :], (xh[:, k, :], xl[:, k, :]), (w_h[:, k, :], w_l[:, k, :]),
                                             start=(k == 0), stop=(k == KT - 1))
                    if k % 2:
                        last.then_inc(gu_used, 1)

            def turn_hid(i):
                pe.wait_ge(hid_ready, i + 1)
                for f in range(FF // P):
                    last = nc.tensor.transpose(bank[6][:, f * P:(f + 1) * P], hid[:, f * P:(f + 1) * P], C["ident"][:])
                last.then_inc(hT_psum, 1)

            def down(i):
                pe.wait_ge(hT_done, i + 1)
                wait(pe, y_done, i * 2)
                for f in range(FF // P):
                    pe.wait_ge(down_split, i * 4 + (f + 1))
                    for n in range(2):
                        s = slice(n * 512, (n + 1) * 512)
                        last = split_product(nc, bank[2 + n][:, :], (hT_h[:, f, :], hT_l[:, f, :]), (wd_h[:, f, s], wd_l[:, f, s]),
                                             start=(f == 0), stop=(f == FF // P - 1))
                    last.then_inc(down_used, 1)

            pe.wait_ge(blk_ready, 1)
            nc.tensor.matmul(bank[1][0:1, 0:MAXBLK], blk_col[:], C["ident"][0:MAXBLK, 0:MAXBLK], start=True, stop=True).then_inc(blk_psum, 1)
            pe.wait_ge(table_ready, 3)
            for a in range(N_ASG):
                r = P if a < 2 * NT else TS
                last = nc.tensor.matmul(bank[0][:, 0:2 * MAXBLK], place_hot[0:r, a, :],
                                        block_value[0:r, a].rearrange("p o n -> p (o n)"), start=(a == 0), stop=(a == N_ASG - 1))
            last.then_inc(rows_psum, 1)
            pe.wait_ge(rows_ready, 1)
            m = blocks_but_three(pe) + 1
            turn_x(0)
            gate_up(0)
            turn_x(1)
            turn_hid(0)
            with pe.Fori(1, m + 1) as i:
                gate_up(i)
                turn_x(i + 1)
                down(i - 1)
                turn_hid(i)
            gate_up(m + 1)
            down(m)
            turn_hid(m + 1)
            down(m + 1)

        @block.scalar
        def _(act):
            def high_gate_up(i, pieces):
                for p in pieces:
                    act.wait_ge(gate_up_loaded[p], i * 32 + 32)
                    wait(act, gu_used, i * 4 + (p - 3))
                    s = slice(2 * p, 2 * p + 2)
                    nc.scalar.copy(wg_h[:, s, :], wg[:, s, :])
                    nc.scalar.copy(wu_h[:, s, :], wu[:, s, :]).then_inc(gu_high, 1)

            def high_down(i):
                for p in range(4):
                    act.wait_ge(down_loaded[p], i * 16 + 16)
                    wait(act, down_used, i * 4 + (p - 3))
                    nc.scalar.copy(wd_h[:, p, :], wd[:, p, :]).then_inc(down_high, 1)

            def high_x(i):
                for half in range(2):
                    act.wait_ge(xT_psum, i * 2 + (half + 1))
                    wait(act, gu_used, i * 4)
                    nc.scalar.copy(xh[:, 4 * half:4 * half + 4, :], bank[4 + half][:].rearrange("p (k t) -> p k t", k=4)).then_inc(x_high, 1)

            def silu(i):
                act.wait_ge(gu_used, i * 4 + 4)
                wait(act, hid_ready, i)
                nc.scalar.activation(act_g[:], bank[0][:, :], ACT.Silu).then_inc(silu_done, 1)

            def high_hid(i):
                act.wait_ge(hT_psum, i + 1)
                wait(act, down_used, i * 4)
                nc.scalar.copy(hT_h[:], bank[6][:].rearrange("p (k t) -> p k t", k=4)).then_inc(h_high, 1)

            m = blocks_but_three(act) + 1
            high_gate_up(0, range(4))
            high_x(0)

            def block_of(i):
                high_gate_up(i + 1, range(3))
                silu(i)
                high_x(i + 1)
                high_gate_up(i + 1, range(3, 4))
                high_down(i)
                high_hid(i)

            block_of(0)
            with act.Fori(1, m + 1) as i:
                block_of(i)
            silu(m + 1)
            high_down(m + 1)
            high_hid(m + 1)

        @block.vector
        def _(dve):
            links = [0]

            def after(ins):
                links[0] += 1
                then_own(dve, ins, chain, links[0])

            after(nc.vector.tensor_tensor(over[:], S["run"][:].unsqueeze(2).to_broadcast([P, E, NT + 1]),
                                          C["row_step"][:].unsqueeze(1).to_broadcast([P, E, NT + 1]), ALU.is_gt))
            after(nc.vector.tensor_reduce(n_blk[:], over[:], AX.X, ALU.add))
            after(nc.vector.tensor_tensor_scan(blk_end[:], C["ones"][:, 0:E], n_blk[:], 0.0, ALU.mult, ALU.add))
            after(nc.vector.tensor_tensor(row0[:], blk_end[:], n_blk[:], ALU.subtract))
            after(nc.vector.tensor_scalar(row0[:], row0[:], float(P), None, ALU.mult))
            after(nc.vector.tensor_scalar(ended[:], blk_end[0:MAXBLK, :], C["row_no"][0:MAXBLK, :], None, ALU.is_le))
            after(nc.vector.tensor_reduce(blk_col[:], ended[:], AX.X, ALU.add))
            nc.vector.tensor_scalar(blk_col[:], blk_col[:], float(E - 1), None, ALU.min).then_inc(blk_ready, 1)
            dve.wait_ge(blk_psum, 1)
            nc.vector.tensor_copy(blk_i[:, 0:MAXBLK], bank[1][0:1, 0:MAXBLK]).then_inc(table_ready, 1)
            nc.vector.tensor_scalar(blk_i[:, MAXBLK:], blk_end[0:1, E - 1:E], -3.0, None, ALU.add).then_inc(table_ready, 1)
            after(nc.vector.tensor_tensor(S["before"][:], S["before"][:], row0[:].unsqueeze(1).to_broadcast([P, NT + 1, E]), ALU.add))
            for k in range(2):
                after(nc.vector.tensor_tensor(place[:, :, k, :], S["before"][:], S["hot"][:, :, k, :], ALU.mult))
            after(nc.vector.tensor_reduce(row_f[:], place[:], AX.X, ALU.add))
            row = row_f[:].rearrange("p t k -> p (t k)")
            after(nc.vector.tensor_tensor(at_or_past[:], row.unsqueeze(2).to_broadcast([P, N_ASG, MAXBLK + 1]),
                                          C["block_row"][:].unsqueeze(1).to_broadcast([P, N_ASG, MAXBLK + 1]), ALU.is_ge))
            after(nc.vector.tensor_reduce(of_block[:], at_or_past[:, :, 1:], AX.X, ALU.add))
            after(nc.vector.scalar_tensor_tensor(out=in_block[:], in0=of_block[:], scalar=-float(P), in1=row,
                                                 op0=ALU.mult, op1=ALU.add))
            after(nc.vector.tensor_tensor(place_hot, C["column_no"][:].unsqueeze(1).to_broadcast([P, N_ASG, P]),
                                          in_block[:].unsqueeze(2).to_broadcast([P, N_ASG, P]), ALU.is_equal))
            after(nc.vector.tensor_tensor(at_or_past[:, :, 0:MAXBLK], at_or_past[:, :, 0:MAXBLK], at_or_past[:, :, 1:],
                                          ALU.subtract))
            for o in range(2):
                ins = nc.vector.tensor_tensor(block_value[:, :, o, :], at_or_past[:, :, 0:MAXBLK],
                                              C["token_slot"][:, :, o:o + 1].to_broadcast([P, N_ASG, MAXBLK]), ALU.mult)
            ins.then_inc(table_ready, 1)
            dve.wait_ge(rows_psum, 1)
            got = bank[0][:, 0:2 * MAXBLK].rearrange("p (o n) -> p o n", o=2)
            for o in range(2):
                after(nc.vector.tensor_scalar(of_row_f[:, o, :], got[:, o, :], float((1 + o) * T), None, ALU.add))
            nc.vector.tensor_copy(of_row[:], of_row_f[:]).then_inc(rows_ready, 1)

            def gated(i):
                dve.wait_ge(silu_done, i + 1)
                wait(dve, hT_psum, i)
                nc.vector.tensor_tensor(hid[:], act_g[:], bank[1][:, :], ALU.mult).then_inc(hid_ready, 1)

            def unload_y(i):
                wait(dve, y_stored, i * 16)
                dve.wait_ge(down_used, i * 4 + 4)
                for n in range(2):
                    nc.vector.tensor_copy(yb[:, n * 512:(n + 1) * 512], bank[2 + n][:, :]).then_inc(y_done, 1)

            def low_gate_up(i, pieces):
                for p in pieces:
                    dve.wait_ge(gu_high, i * 4 + (p + 1))
                    s = slice(2 * p, 2 * p + 2)
                    nc.vector.tensor_tensor(wg_l[:, s, :], wg[:, s, :], wg_h[:, s, :].bitcast(F32), ALU.subtract)
                    nc.vector.tensor_tensor(wu_l[:, s, :], wu[:, s, :], wu_h[:, s, :].bitcast(F32), ALU.subtract).then_inc(gu_split, 1)

            def low_x(i):
                for half in range(2):
                    dve.wait_ge(x_high, i * 2 + (half + 1))
                    s = slice(4 * half, 4 * half + 4)
                    nc.vector.tensor_tensor(xl[:, s, :], bank[4 + half][:].rearrange("p (k t) -> p k t", k=4),
                                            xh[:, s, :].bitcast(F32), ALU.subtract).then_inc(xT_done, 1)

            def low_down(i):
                for p in range(4):
                    dve.wait_ge(down_high, i * 4 + (p + 1))
                    nc.vector.tensor_tensor(wd_l[:, p, :], wd[:, p, :], wd_h[:, p, :].bitcast(F32), ALU.subtract).then_inc(down_split, 1)

            def low_hid(i):
                dve.wait_ge(h_high, i + 1)
                nc.vector.tensor_tensor(hT_l[:], bank[6][:].rearrange("p (k t) -> p k t", k=4), hT_h[:].bitcast(F32),
                                        ALU.subtract).then_inc(hT_done, 1)

            m = blocks_but_three(dve) + 1
            low_gate_up(0, range(4))
            low_x(0)

            def block_of(i, first=False):
                low_gate_up(i + 1, range(3))
                gated(i)
                low_x(i + 1)
                low_gate_up(i + 1, range(3, 4))
                low_down(i)
                if not first:
                    unload_y(i - 1)
                low_hid(i)

            block_of(0, first=True)
            with dve.Fori(1, m + 1) as i:
                block_of(i)
            gated(m + 1)
            low_down(m + 1)
            unload_y(m)
            low_hid(m + 1)
            unload_y(m + 1)


FIRST = 4


def combine(nc, A, S, C):
    with ExitStack() as ctx:
        def sb(name, shape, dt=F32):
            return ctx.enter_context(nc.sbuf_tensor(name, shape, dt))

        def sem(name):
            return ctx.enter_context(nc.semaphore(name))

        yy = [sb(f"yy{t}", [P, 2, D]) for t in range(NT + 1)]
        late_h = sb("late_h", [P, NT + 1 - FIRST, D])
        h = [S["h_final"][:, t, :] if t < FIRST else late_h[:, t - FIRST, :] for t in range(NT + 1)]
        w = S["w_final"]
        junk = sb("junkf", [P, D])
        st = sb("st_f", [P, NT + 1, 3])
        late = [sem(f"f_loaded{t}") for t in (4, 5, 7)]
        loaded = S["final_loaded"] + [late[0], late[1], late[1], late[2], late[2]]
        loaded_at = [48, 32, 32, 32, 32, 64, 64, 64, 64]
        out_stored = sem("out_stored")
        part, summed, squared, rms, rinv, out_ready = (sem(n) for n in ("part", "summed", "squared", "rms", "rinv", "out_ready"))

        block = ctx.enter_context(nc.Block())

        @block.sync
        def _(sp):
            for t in range(NT + 1):
                r = rows_of(t)
                if t >= FIRST:
                    sp.dma_start(h[t][0:r, :], S["h"][t * P:t * P + r, :]).then_inc(loaded[t], 16)
                sp.dma_start(yy[t][0:r], S["picked"].rearrange("(t k) d -> t k d", k=2)[t * P:t * P + r]).then_inc(loaded[t], 16)

        @block.gpsimd
        def _(pool):
            for t in range(NT + 1):
                r = rows_of(t)
                pool.wait_ge(out_ready, t + 1)
                dst = A["y_sample"] if r == TS else A["y_prompt"][t * P:t * P + r, :]
                pool.dma_start(dst, h[t][0:r, :]).then_inc(out_stored, 16)
            pool.wait_ge(out_stored, 16 * (NT + 1))

        @block.scalar
        def _(act):
            for t in range(NT + 1):
                r = rows_of(t)
                act.wait_ge(summed, t + 1)
                then_own(act, nc.scalar.activation(junk[0:r, :], h[t][0:r, :], ACT.Square, accum_out=st[0:r, t, 0:1]), squared, t + 1)
                nc.scalar.activation(st[0:r, t, 1:2], st[0:r, t, 0:1], ACT.Sqrt, bias=C["eps"][0:r, :], scale=1.0 / D).then_inc(rms, 1)

        @block.vector
        def _(dve):
            def add(t):
                r = rows_of(t)
                dve.wait_ge(loaded[t], loaded_at[t])
                for k, done in ((0, part), (1, summed)):
                    ins = nc.vector.scalar_tensor_tensor(out=h[t][0:r, :], in0=yy[t][0:r, k, :], scalar=S["gate"][0:r, t, k:k + 1],
                                                         in1=h[t][0:r, :], op0=ALU.mult, op1=ALU.add)
                    ins.then_inc(done, 1)
                    if k == 0:
                        dve.wait_ge(part, t + 1)

            def norm(t):
                r = rows_of(t)
                dve.wait_ge(rms, t + 1)
                then_own(dve, nc.vector.reciprocal(st[0:r, t, 2:3], st[0:r, t, 1:2]), rinv, t + 1)
                nc.vector.scalar_tensor_tensor(out=h[t][0:r, :], in0=h[t][0:r, :], scalar=st[0:r, t, 2:3], in1=w[0:r, :],
                                               op0=ALU.mult, op1=ALU.mult).then_inc(out_ready, 1)

            add(0)
            for t in range(1, NT + 1):
                add(t)
                norm(t - 1)
            norm(NT)




OUTPUTS = {
    "y_prompt": (SEQ, D), "y_sample": (TS, D), "conv_tail": (P, CT_N, DEC_B + 1, CONV_K - 1),
    "ssm_prompt": (NSTATE, D), "ssm_sample": (DEC_B, NSTATE, D), "sg_v_sample": (TS, D),
}
SCRATCH = {
    "z": (T, D), "xb": (T, D + GROUPS * NSTATE), "bct": (2 * GROUPS * NSTATE, T), "uT": (D, T), "v": (T, D),
    "h": (T, D), "hn": (T, D), "picked": (2 * T, D),
}


def program(nc, A, S):
    with ExitStack() as ctx:
        def sb(name, shape, dt=F32):
            return ctx.enter_context(nc.sbuf_tensor(name, shape, dt))

        C = {
            "ident": sb("ident", [P, P]), "eps": sb("eps", [P, 1]), "ones": sb("ones", [P, P]), "le": sb("le", [P, P]),
            "lt": sb("lt", [P, P]), "gt": sb("gt", [P, P]), "same": sb("same", [TS, TS]),
            "of_seq": sb("of_seq", [P, DEC_B, TS]), "repeat": sb("repeat", [DEC_S, TS]),
            "expert_no": sb("expert_no", [P, E]), "row_step": sb("row_step", [P, NT + 1]),
            "row_no": sb("row_no", [P, 1]), "token_slot": sb("token_slot", [P, 2 * (NT + 1), 2]),
            "block_row": sb("block_row", [P, MAXBLK + 1]), "column_no": sb("column_no", [P, P]),
            "const_made": ctx.enter_context(nc.semaphore("const_made")), "holder": ctx.enter_context(nc.semaphore("holder")),
        }
        S["dtk"] = sb("dtk", [P, NT + 1, 2 * HEADS])
        bank = [ctx.enter_context(nc.psum_tensor(f"bank{b}", [P, 512], F32)) for b in range(8)]
        S["gate"] = sb("gate", [P, NT + 1, 2])
        S["hot"] = sb("hot", [P, NT + 1, 2, E])
        S["before"] = sb("before", [P, NT + 1, E])
        S["run"] = sb("run", [P, E])
        S["consts_loaded"], S["w_out_loaded"] = (ctx.enter_context(nc.semaphore(n)) for n in ("consts_loaded", "w_out_loaded"))
        with ExitStack() as early:
            for name, shape in (("sg_w_row", [P, D]), ("sgWT", [P, SGH, P]), ("sgb", [P, SGH, P]), ("d_skip", [P, HEADS]),
                                ("w_out_sg", [P, KT, D])):
                S[name] = early.enter_context(nc.sbuf_tensor(name, shape, F32))
            projections(nc, A, S, C, bank)
            mixer(nc, A, S, C, bank)
        S["w_final"] = sb("w_final", [P, D])
        S["h_final"] = sb("h_final", [P, FIRST, D])
        S["final_loaded"] = [ctx.enter_context(nc.semaphore(f"final_loaded{j}")) for j in range(FIRST)]
        experts(nc, A, S, C, bank)
        combine(nc, A, S, C)


def laid_out(np, x_prompt, x_sample, state_conv, state_ssm, norm_mix_w, w_in, conv_w, conv_b, dt_bias, a_log, d_skip,
             ssm_norm_w, sg_norm_w, sg_w, sg_b, w_out, norm_ffn_w, w_router_group, b_router_group, w_router_expert,
             b_router_expert, w_gate, w_up, w_down, norm_final_w):
    w = w_in[0]
    columns = np.concatenate([w[:, :COL_DT], w[:, COL_U:]], axis=1)
    return {
        "x_prompt": x_prompt, "x_sample": x_sample,
        "state_conv": state_conv[0].reshape(DEC_B, CONV_K - 1, CT_N, P).transpose(3, 2, 0, 1),
        "state_ssm": state_ssm[0].reshape(DEC_B, D, NSTATE).transpose(0, 2, 1),
        "norm_mix_w": norm_mix_w[0].reshape(KT, P).T,
        "w_in_tiles": columns.reshape(KT, P, M_END, P).transpose(2, 1, 0, 3),
        "w_dt": w[:, COL_DT:COL_U].reshape(KT, P, HEADS).transpose(1, 0, 2),
        "conv_w": conv_w[0].reshape(CONV_K, CT_N, P).transpose(2, 0, 1),
        "conv_b": conv_b[0].reshape(CT_N, P).T,
        "dt_bias": dt_bias.T, "a_log": a_log.T, "d_skip": d_skip, "ssm_norm_w": ssm_norm_w, "sg_norm_w": sg_norm_w,
        "sg_w": sg_w[0].transpose(2, 0, 1), "sg_b": sg_b,
        "w_out": w_out[0].reshape(2 * KT, P, D).transpose(1, 0, 2), "norm_ffn_w": norm_ffn_w,
        "w_router": np.concatenate([w_router_group[0], w_router_expert[0]], axis=1).reshape(KT, P, EG + E).transpose(1, 0, 2),
        "b_router": np.concatenate([b_router_group, b_router_expert], axis=1),
        "w_gate": w_gate[0], "w_up": w_up[0], "w_down": w_down[0], "norm_final_w": norm_final_w[None],
    }


def kernel(**inputs):
    import numpy as _np
    import concourse.bacc as _bacc
    from concourse import mybir as _mybir
    from concourse.bass_utils import run_bass_kernel_spmd as _run

    nc = _bacc.Bacc("TRN2", target_bir_lowering=False, num_devices=1)
    arrays, A = {}, {}
    for name, a in laid_out(_np, **inputs).items():
        arrays[f"in_{name}"] = _np.ascontiguousarray(a)
        A[name] = nc.dram_tensor(f"in_{name}", a.shape, _mybir.dt.from_np(a.dtype), kind="ExternalInput").ap()
    for name, shape in OUTPUTS.items():
        A[name] = nc.dram_tensor(f"out_{name}", shape, F32, kind="ExternalOutput").ap()
    S = {name: nc.dram_tensor(f"scratch_{name}", shape, F32, kind='Internal').ap() for name, shape in SCRATCH.items()}
    program(nc, A, S)
    r = _run(nc, [arrays], core_ids=[0])
    got = {name: r.results[0][f"out_{name}"] for name in OUTPUTS}
    tail = got["conv_tail"].transpose(2, 3, 1, 0).reshape(1, DEC_B + 1, CONV_K - 1, C_CONV)
    state = (GROUPS, HEADS // GROUPS, HD, NSTATE)
    return (got["y_prompt"].reshape(1, SEQ, D), got["y_sample"].reshape(DEC_B, DEC_S, D), tail[:, 0:1],
            got["ssm_prompt"].T.reshape(1, 1, *state), tail[:, 1:],
            got["ssm_sample"].transpose(0, 2, 1).reshape(1, DEC_B, *state),
            got["sg_v_sample"].reshape(1, DEC_B, DEC_S, D))
```
